# Optimizing a Trainium2 kernel written in Bass

```python
import jax
import jax.numpy as jnp
from jax import lax
import numpy as np

D_MODEL = 1024
BATCH = 1
SEQ = 256
DEPTH = 2

CHUNK = 64
CONV_K = 4
EPS = 1e-6
H_A = 4
DK_A = 128
DV_A = 128
H_B = 4
DK_B = 64
DV_B = 128
H_C = 4
DK_C = 64
DV_C = 128
GLA_RANK = 16
GLA_TAU = 16.0
QK_A = H_A * DK_A
V_A = H_A * DV_A
QK_B = H_B * DK_B
V_B = H_B * DV_B
QK_C = H_C * DK_C
V_C = H_C * DV_C
N_BRANCH = 3
BRANCH_WIDTH = V_A
IN_SPLITS = (QK_A, QK_A, V_A, V_A, H_A, H_A,
             QK_B, QK_B, V_B, V_B, H_B, H_B,
             QK_C, QK_C, V_C, V_C, GLA_RANK)
IN_WIDTH = sum(IN_SPLITS)
D_FF = 2816
N_EXPERTS = 8
TOP_K = 2
D_FF_EXPERT = 3584
N_DENSE = (DEPTH + 1) // 2
N_MOE = DEPTH // 2

kernel_name = "hybrid_deltanet_mlstm_gla_moe_adaln"

def _rms(x, g):
    xf = x.astype(jnp.float32)
    y = xf * lax.rsqrt(jnp.mean(jnp.square(xf), axis=-1, keepdims=True) + EPS)
    return (y * g.astype(jnp.float32)).astype(x.dtype)

def _l2norm(x):
    return x * lax.rsqrt(jnp.sum(jnp.square(x), axis=-1, keepdims=True) + 1e-6)

def _causal_conv(x, w):
    return lax.conv_general_dilated(
        x, w[:, None, :].astype(x.dtype), window_strides=(1,), padding=[(CONV_K - 1, 0)],
        dimension_numbers=("NWC", "WIO", "NWC"), feature_group_count=x.shape[-1])

def _to_chunks(x, n_heads):
    b, s, _ = x.shape
    return x.reshape(b, s // CHUNK, CHUNK, n_heads, -1).transpose(0, 3, 1, 2, 4).astype(jnp.float32)

def _scalar_chunks(x):
    b, s, h = x.shape
    return x.reshape(b, s // CHUNK, CHUNK, h).transpose(0, 3, 1, 2).astype(jnp.float32)

def _from_chunks(o):
    b, h, n, l, d = o.shape
    return o.transpose(0, 2, 3, 1, 4).reshape(b, n * l, h, d)

def _causal_masks():
    pos = jnp.arange(CHUNK)
    return pos[:, None] >= pos[None, :], pos[:, None] > pos[None, :]

def _chunk_first(a):
    return jnp.moveaxis(a, 2, 0)

def _gated_delta_rule(q, k, v, g, beta):
    dk, dv = q.shape[-1], v.shape[-1]
    tri, strict = _causal_masks()
    q = _l2norm(q) * (dk ** -0.5)
    k = _l2norm(k)
    gc = jnp.cumsum(g, axis=-1)
    seg = gc[..., :, None] - gc[..., None, :]
    decay = jnp.where(tri, jnp.exp(jnp.where(tri, seg, 0.0)), 0.0)
    kb = k * beta[..., None]
    a_mat = jnp.where(strict, jnp.einsum("bhnid,bhnjd->bhnij", kb, k) * decay, 0.0)
    t_mat = a_mat + jnp.eye(CHUNK, dtype=a_mat.dtype)
    rhs = jnp.concatenate([v * beta[..., None], kb * jnp.exp(gc)[..., None]], axis=-1)
    sol = lax.linalg.triangular_solve(t_mat, rhs, left_side=True, lower=True, unit_diagonal=True)
    u, w = sol[..., :dv], sol[..., dv:]
    k_end = k * jnp.exp(gc[..., -1:] - gc)[..., None]
    g_end = jnp.exp(gc[..., -1])

    def step(s, inp):
        w_n, u_n, ke_n, ge_n = inp
        delta = u_n - jnp.einsum("bhlk,bhkv->bhlv", w_n, s)
        s_new = ge_n[..., None, None] * s + jnp.einsum("bhlk,bhlv->bhkv", ke_n, delta)
        return s_new, s

    s0 = jnp.zeros(q.shape[:2] + (dk, dv), jnp.float32)
    _, s_prev = lax.scan(step, s0, (_chunk_first(w), _chunk_first(u), _chunk_first(k_end), _chunk_first(g_end)))
    s_prev = jnp.moveaxis(s_prev, 0, 2)
    delta = u - jnp.einsum("bhnlk,bhnkv->bhnlv", w, s_prev)
    attn = jnp.einsum("bhnik,bhnjk->bhnij", q, k) * decay
    return (jnp.einsum("bhnlk,bhnkv->bhnlv", q * jnp.exp(gc)[..., None], s_prev)
            + jnp.einsum("bhnij,bhnjv->bhniv", attn, delta))

def _mlstm(q, k, v, i_pre, f_pre):
    dk = q.shape[-1]
    tri, _ = _causal_masks()
    k = k * (dk ** -0.5)
    bcum = jnp.cumsum(jax.nn.log_sigmoid(f_pre), axis=-1)
    dlog = jnp.where(tri, bcum[..., :, None] - bcum[..., None, :] + i_pre[..., None, :], -jnp.inf)
    m_intra = jnp.max(dlog, axis=-1)
    wts = jnp.exp(dlog - m_intra[..., None]) * jnp.einsum("bhnik,bhnjk->bhnij", q, k)
    num_intra = jnp.einsum("bhnij,bhnjv->bhniv", wts, v)
    den_intra = jnp.sum(wts, axis=-1)
    a_end = bcum[..., -1:] - bcum + i_pre
    m_chunk = jnp.max(a_end, axis=-1)
    k_w = k * jnp.exp(a_end - m_chunk[..., None])[..., None]
    kv_chunk = jnp.einsum("bhnlk,bhnlv->bhnkv", k_w, v)
    n_chunk = jnp.sum(k_w, axis=-2)
    b_end = bcum[..., -1]

    def step(carry, inp):
        c_s, n_s, m_s = carry
        kv_n, nc_n, mc_n, be_n = inp
        m_new = jnp.maximum(be_n + m_s, mc_n)
        sp = jnp.exp(be_n + m_s - m_new)
        sc = jnp.exp(mc_n - m_new)
        c_new = sp[..., None, None] * c_s + sc[..., None, None] * kv_n
        n_new = sp[..., None] * n_s + sc[..., None] * nc_n
        return (c_new, n_new, m_new), (c_s, n_s, m_s)

    bh = q.shape[:2]
    init = (jnp.zeros(bh + (dk, v.shape[-1]), jnp.float32), jnp.zeros(bh + (dk,), jnp.float32),
            jnp.zeros(bh, jnp.float32))
    _, (c_prev, n_prev, m_prev) = lax.scan(
        step, init, (_chunk_first(kv_chunk), _chunk_first(n_chunk), _chunk_first(m_chunk), _chunk_first(b_end)))
    c_prev = jnp.moveaxis(c_prev, 0, 2)
    n_prev = jnp.moveaxis(n_prev, 0, 2)
    m_prev = jnp.moveaxis(m_prev, 0, 2)[..., None]
    m_tot = jnp.maximum(bcum + m_prev, m_intra)
    s_inter = jnp.exp(bcum + m_prev - m_tot)
    s_intra = jnp.exp(m_intra - m_tot)
    num = (s_inter[..., None] * jnp.einsum("bhnlk,bhnkv->bhnlv", q, c_prev)
           + s_intra[..., None] * num_intra)
    den = s_inter * jnp.einsum("bhnlk,bhnk->bhnl", q, n_prev) + s_intra * den_intra
    return num / jnp.maximum(jnp.abs(den), jnp.exp(-m_tot))[..., None]

def _gla(q, k, v, log_a):
    dk = q.shape[-1]
    tri, _ = _causal_masks()
    q = q * (dk ** -0.5)
    bc = jnp.cumsum(log_a, axis=-2)
    ref = bc[..., CHUNK // 2:CHUNK // 2 + 1, :]
    attn = jnp.where(tri, jnp.einsum("bhnik,bhnjk->bhnij", q * jnp.exp(bc - ref), k * jnp.exp(ref - bc)), 0.0)
    o_intra = jnp.einsum("bhnij,bhnjv->bhniv", attn, v)
    k_end = k * jnp.exp(bc[..., -1:, :] - bc)
    kv_chunk = jnp.einsum("bhnlk,bhnlv->bhnkv", k_end, v)
    a_end = jnp.exp(bc[..., -1, :])

    def step(s, inp):
        kv_n, ae_n = inp
        return ae_n[..., None] * s + kv_n, s

    s0 = jnp.zeros(q.shape[:2] + (dk, v.shape[-1]), jnp.float32)
    _, s_prev = lax.scan(step, s0, (_chunk_first(kv_chunk), _chunk_first(a_end)))
    s_prev = jnp.moveaxis(s_prev, 0, 2)
    return jnp.einsum("bhnlk,bhnkv->bhnlv", q * jnp.exp(bc), s_prev) + o_intra

def _token_mixers(h, w_in, conv_a, a_log, dt_bias, norm_a, conv_b, b_i, b_f, norm_b,
                  w_gla2, b_gla, norm_c, w_br, w_mg, b_mg, w_o):
    bsz, seq, _ = h.shape
    f32 = jnp.float32
    proj = h @ w_in
    points = [int(p) for p in np.cumsum(IN_SPLITS)[:-1]]
    (q_a, k_a, v_a, z_a, a_a, b_a, q_b, k_b, v_b, o_b, i_b, f_b,
     q_c, k_c, v_c, z_c, g_c) = jnp.split(proj, points, axis=-1)

    qkv_a = jax.nn.silu(_causal_conv(jnp.concatenate([q_a, k_a, v_a], axis=-1), conv_a))
    q_a, k_a, v_a = jnp.split(qkv_a, [QK_A, 2 * QK_A], axis=-1)
    g_a = -jnp.exp(a_log.astype(f32)) * jax.nn.softplus(a_a.astype(f32) + dt_bias.astype(f32))
    beta_a = jax.nn.sigmoid(b_a.astype(f32))
    o_a = _gated_delta_rule(_to_chunks(q_a, H_A), _to_chunks(k_a, H_A), _to_chunks(v_a, H_A),
                            _scalar_chunks(g_a), _scalar_chunks(beta_a))
    y_a = (_rms(_from_chunks(o_a).astype(h.dtype), norm_a)
           * jax.nn.silu(z_a.reshape(bsz, seq, H_A, DV_A))).reshape(bsz, seq, V_A)

    qk_b = jax.nn.silu(_causal_conv(jnp.concatenate([q_b, k_b], axis=-1), conv_b))
    q_b, k_b = jnp.split(qk_b, [QK_B], axis=-1)
    h_b = _mlstm(_to_chunks(q_b, H_B), _to_chunks(k_b, H_B), _to_chunks(v_b, H_B),
                 _scalar_chunks(i_b.astype(f32) + b_i.astype(f32)),
                 _scalar_chunks(f_b.astype(f32) + b_f.astype(f32)))
    y_b = (jax.nn.sigmoid(o_b.reshape(bsz, seq, H_B, DV_B))
           * _rms(_from_chunks(h_b).astype(h.dtype), norm_b)).reshape(bsz, seq, V_B)

    log_a_c = jax.nn.log_sigmoid(g_c.astype(f32) @ w_gla2.astype(f32) + b_gla.astype(f32)) / GLA_TAU
    o_c = _gla(_to_chunks(q_c, H_C), _to_chunks(k_c, H_C), _to_chunks(v_c, H_C), _to_chunks(log_a_c, H_C))
    y_c = (_rms(_from_chunks(o_c).astype(h.dtype), norm_c)
           * jax.nn.silu(z_c.reshape(bsz, seq, H_C, DV_C))).reshape(bsz, seq, V_C)

    branches = (y_a, y_b, y_c)
    merged = jax.nn.sigmoid(h @ w_mg[0] + b_mg[0]) * (branches[0] @ w_br[0])
    for g in range(1, N_BRANCH):
        merged = merged + jax.nn.sigmoid(h @ w_mg[g] + b_mg[g]) * (branches[g] @ w_br[g])
    return merged @ w_o

def _swiglu(h, w1, w3, w2):
    return (jax.nn.silu(h @ w1) * (h @ w3)) @ w2

def _moe(h, w_router, b_router, w1, w3, w2):
    bsz, seq, d = h.shape
    t = h.reshape(-1, d)
    logits = (t @ w_router).astype(jnp.float32) + b_router.astype(jnp.float32)
    top_logit, top_idx = lax.top_k(logits, TOP_K)
    top_w = jax.nn.softmax(top_logit, axis=-1)
    combine = jnp.einsum("tk,tke->te", top_w,
                         jax.nn.one_hot(top_idx, N_EXPERTS, dtype=jnp.float32)).astype(t.dtype)
    out = jnp.zeros_like(t)
    for e in range(N_EXPERTS):
        out = out + combine[:, e:e + 1] * _swiglu(t, w1[e], w3[e], w2[e])
    return out.reshape(bsz, seq, d)

def setup_inputs(seed: int = 0) -> dict:
    key = jax.random.key(seed)
    ks = jax.random.split(key, 32)
    f32 = jnp.float32
    D = D_MODEL

    def nrm(k, shape, scale):
        return jax.random.normal(k, shape, f32) * scale

    gate_offset = jnp.concatenate([jnp.zeros((2 * D,), f32), jnp.ones((D,), f32),
                                   jnp.zeros((2 * D,), f32), jnp.ones((D,), f32)])
    dt = jnp.exp(jax.random.uniform(ks[9], (DEPTH, H_A), f32, np.log(1e-3), np.log(1e-1)))
    return {
        "x": nrm(ks[0], (BATCH, SEQ, D), 1.0),
        "c": nrm(ks[1], (BATCH, D), 1.0),
        "w_ada": nrm(ks[2], (DEPTH, D, 6 * D), 0.1 * D ** -0.5),
        "b_ada": nrm(ks[3], (DEPTH, 6 * D), 0.02) + gate_offset,
        "g_mix": 1.0 + nrm(ks[4], (DEPTH, D), 0.02),
        "g_ffn": 1.0 + nrm(ks[5], (DEPTH, D), 0.02),
        "g_final": 1.0 + nrm(ks[6], (D,), 0.02),
        "w_in": nrm(ks[7], (DEPTH, D, IN_WIDTH), D ** -0.5),
        "conv_a": nrm(ks[8], (DEPTH, CONV_K, 2 * QK_A + V_A), CONV_K ** -0.5),
        "a_log": jnp.log(jax.random.uniform(ks[10], (DEPTH, H_A), f32, 1.0, 16.0)),
        "dt_bias": dt + jnp.log(-jnp.expm1(-dt)),
        "norm_a": 1.0 + nrm(ks[11], (DEPTH, DV_A), 0.02),
        "conv_b": nrm(ks[12], (DEPTH, CONV_K, 2 * QK_B), CONV_K ** -0.5),
        "b_i": nrm(ks[13], (DEPTH, H_B), 0.1),
        "b_f": jax.random.uniform(ks[14], (DEPTH, H_B), f32, 3.0, 6.0),
        "norm_b": 1.0 + nrm(ks[15], (DEPTH, DV_B), 0.02),
        "w_gla2": nrm(ks[16], (DEPTH, GLA_RANK, QK_C), GLA_RANK ** -0.5),
        "b_gla": nrm(ks[17], (DEPTH, QK_C), 0.1),
        "norm_c": 1.0 + nrm(ks[18], (DEPTH, DV_C), 0.02),
        "w_br": nrm(ks[19], (DEPTH, N_BRANCH, BRANCH_WIDTH, D), BRANCH_WIDTH ** -0.5),
        "w_mg": nrm(ks[20], (DEPTH, N_BRANCH, D, D), D ** -0.5),
        "b_mg": nrm(ks[21], (DEPTH, N_BRANCH, D), 0.02),
        "w_o": nrm(ks[22], (DEPTH, D, D), D ** -0.5),
        "w1_d": nrm(ks[23], (N_DENSE, D, D_FF), D ** -0.5),
        "w3_d": nrm(ks[24], (N_DENSE, D, D_FF), D ** -0.5),
        "w2_d": nrm(ks[25], (N_DENSE, D_FF, D), D_FF ** -0.5),
        "w_router": nrm(ks[26], (N_MOE, D, N_EXPERTS), D ** -0.5),
        "b_router": nrm(ks[27], (N_MOE, N_EXPERTS), 0.01),
        "w1_e": nrm(ks[28], (N_MOE, N_EXPERTS, D, D_FF_EXPERT), D ** -0.5),
        "w3_e": nrm(ks[29], (N_MOE, N_EXPERTS, D, D_FF_EXPERT), D ** -0.5),
        "w2_e": nrm(ks[30], (N_MOE, N_EXPERTS, D_FF_EXPERT, D), D_FF_EXPERT ** -0.5),
    }

def reference(x, c, w_ada, b_ada, g_mix, g_ffn, g_final, w_in, conv_a, a_log, dt_bias, norm_a,
              conv_b, b_i, b_f, norm_b, w_gla2, b_gla, norm_c, w_br, w_mg, b_mg, w_o,
              w1_d, w3_d, w2_d, w_router, b_router, w1_e, w3_e, w2_e):
    c_act = jax.nn.silu(c)
    for layer in range(DEPTH):
        mod = c_act @ w_ada[layer] + b_ada[layer]
        sh1, sc1, gt1, sh2, sc2, gt2 = [m[:, None, :] for m in jnp.split(mod, 6, axis=-1)]
        h = _rms(x, g_mix[layer]) * (1 + sc1) + sh1
        x = x + gt1 * _token_mixers(h, w_in[layer], conv_a[layer], a_log[layer], dt_bias[layer], norm_a[layer],
                                    conv_b[layer], b_i[layer], b_f[layer], norm_b[layer], w_gla2[layer],
                                    b_gla[layer], norm_c[layer], w_br[layer], w_mg[layer], b_mg[layer],
                                    w_o[layer])
        h = _rms(x, g_ffn[layer]) * (1 + sc2) + sh2
        j = layer // 2
        if layer % 2 == 0:
            f = _swiglu(h, w1_d[j], w3_d[j], w2_d[j])
        else:
            f = _moe(h, w_router[j], b_router[j], w1_e[j], w3_e[j], w2_e[j])
        x = x + gt2 * f
    return _rms(x, g_final)


_drawn_inputs = setup_inputs


def setup_inputs(seed=0):
    import zlib

    import numpy as np

    out = dict(_drawn_inputs(seed))
    spreads = {}
    factors = {'g_final': 2.732, 'b_i': 8.0, 'norm_b': 2.768, 'b_mg': 3.26}
    for name, (base, spread) in spreads.items():
        noise = np.random.default_rng([zlib.crc32(name.encode()), seed]).standard_normal(out[name].shape)
        drawn = base * np.exp(spread * noise) if base else spread * noise
        out[name] = jnp.asarray(drawn.astype(out[name].dtype))
    for name, factor in factors.items():
        out[name] = (out[name] * factor).astype(out[name].dtype)
    return out
```

```python
from contextlib import ExitStack

import numpy as np

import concourse.bass as bass
from concourse import mybir

F32 = mybir.dt.float32
U32 = mybir.dt.uint32
ACT = mybir.ActivationFunctionType
ALU = mybir.AluOpType
X = mybir.AxisListType.X

P = 128
D = 1024
KD = D // P
SEQ = 256
NT = SEQ // P
L = 64
NCH = SEQ // L
H = 4
DEPTH = 2
W512 = 512
NEG = -1.0e30
EPS = 1e-6
D_FF = 2816
N_EXP = 8
D_FFE = 3584
RING = 7
NBANK = 4

QA, ZA = 0, 1536
AB = 2048
QB, VB, OB = 2056, 2568, 3080
IF = 3592
QC, VC, ZC = 3600, 4112, 4624
GC = 5136
LN_DKA = float(-0.5 * np.log(128.0))
LN_DKB = float(-0.5 * np.log(64.0))


def slab_plan(l):
    plan = []
    for piece in (0, 1):
        plan += [("ada", l, k, piece * D + hf * W512) for hf in range(2) for k in range(2)]
    for col in (QA, QA + 512, QA + 1024, QB, QC, ZA, VB, OB, VC, ZC):
        plan += [("in", l, k, col) for k in range(2)]
    for piece in (2, 3, 4, 5):
        plan += [("ada", l, k, piece * D + hf * W512) for hf in range(2) for k in range(2)]
    for g in range(3):
        for hf in range(2):
            plan += [("mg", l, g, k, hf) for k in range(2)] + [("br", l, g, hf)]
    for hf in range(2):
        plan += [("wo", l, k, hf) for k in range(2)]
    return plan


def ffn_widths(dff):
    return [W512] * (dff // W512) + ([dff % W512] if dff % W512 else [])


def job_plan(l):
    j = [("cols", l)]
    j += [("mod", l, piece, hf) for piece in (0, 1) for hf in range(2)]
    j += [("hT", l, 0, t, q) for t in range(NT) for q in range(2)]
    j += [("small", l), ("gT", l), ("cum", l), ("la", l)]
    j += [("qkvA", l, i) for i in range(6)] + [("qkB", l, i) for i in range(2)] + [("qkC", l, i) for i in range(2)]
    j += [(n, l, t) for n in ("zA", "vB", "oB", "vC", "zC") for t in range(NT)]
    j += [(n, l, t) for t in range(NT) for n in ("TQ", "TK", "TV")]
    for t in range(NT):
        j += [("R1", l, t), ("KK", l, t), ("R2", l, t), ("KQ", l, t)]
    j += [("X", l, 0, t) for t in range(NT)]
    for lev in range(1, 6):
        for t in range(NT):
            j += [("X", l, lev, t)]
        for t in range(NT):
            j += ([("Y", l, lev, t)] if lev < 5 else []) + [("YT", l, lev, t)]
    for t in range(NT):
        j += [("U", l, t), ("WT", l, t)]
    j += [("RA", l, t) for t in range(NT)]
    for t in range(NT):
        j += [("TKB", l, t), ("RB", l, t), ("KQB", l, t), ("KQC", l, t), ("TKC", l, t)]
    for n in range(NCH):
        j += [("P1", l, n), ("P2", l, n), ("QB0", l, n), ("QB1", l, n), ("KVB", l, n), ("QC", l, n), ("KVC", l, n),
              ("P3", l, n)]
    for t in range(NT):
        j += [("OA", l, t), ("OB0", l, t), ("OB1", l, t), ("OC", l, t)]
    j += [("mod", l, piece, hf) for piece in (2, 3, 4, 5) for hf in range(2)]
    j += [("yT", l, g, t) for g in range(3) for t in range(NT)]
    for g in range(3):
        for hf in range(2):
            j += [(n, l, g, hf, t) for t in range(NT) for n in ("mg", "br")]
    j += [("mT", l, t, q) for t in range(NT) for q in range(2)]
    j += [("wo", l, hf, t) for hf in range(2) for t in range(NT)]
    j += [("hT", l, 1, t, q) for t in range(NT) for q in range(2)]
    if l % 2 == 1:
        j += [("router", l)]
    return j


def ffn_jobs(widths):
    j, last = [], None
    for f in range(len(widths)):
        for t in range(NT):
            j += [("w1", f, t), ("w3", f, t)]
            if last is not None:
                j += [("gT", *last)]
            last = (f, t)
    return j + [("gT", *last)]


def hybrid_kernel(nc, x, c, w_ada, b_ada, g_mix, g_ffn, g_final, w_in, conv_a, a_log, dt_bias, norm_a,
                  conv_b, b_i, b_f, norm_b, w_gla2, b_gla, norm_c, w_br, w_mg, b_mg, w_o,
                  w1_d, w3_d, w2_d, w_router, b_router, w1_e, w3_e, w2_e, out):
    with ExitStack() as ctx:
        sems = {}

        def S(name):
            if name not in sems:
                sems[name] = ctx.enter_context(nc.semaphore(name))
            return sems[name]

        def sb(name, shape, dt=F32):
            return ctx.enter_context(nc.sbuf_tensor(name, shape, dt))

        ring = sb("ring", [P, RING, 4, W512])
        xs = sb("xs", [P, NT, D])
        mod = sb("mod", [P, 4, D])
        hT = sb("hT", [P, KD, SEQ])
        ident = sb("ident", [P, P])
        tri = sb("tri", [P, P])
        same = sb("same", [P, P])
        half = sb("half", [P, 2, P])
        negI = sb("negI", [P, P])
        negS = sb("negS", [P, P])
        negL = sb("negL", [P, P])
        lev_m = sb("lev_m", [P, 6, P])
        ones = sb("ones", [P, P])
        rst = sb("rst", [P, SEQ])
        cst = sb("cst", [P, 8])
        crow = sb("crow", [8, P])
        cact = sb("cact", [P, KD])
        bglar = sb("bglar", [2, P])
        cols = sb("cols", [P, 66])
        wsm = sb("wsm", [P, KD, 32])
        wgla = sb("wgla", [16, 256])
        bias16 = sb("bias16", [P, 16])
        sgn16 = sb("sgn16", [P, 16])
        cf16 = sb("cf16", [P, 16])
        normr = sb("normr", [P, 3, P])
        wrt = sb("wrt", [P, KD, 8])
        brt = sb("brt", [P, 8])
        st = sb("st", [P, 64])
        comb = sb("comb", [P, NT, 8])
        scal = sb("scal", [P, 12, NT, 16])
        WORK = 25650
        work = sb("work", [P, WORK])
        used = [0]

        def wk(n, *shape):
            a = used[0]
            used[0] += n
            assert used[0] <= WORK, used
            v = work[:, a:a + n]
            if len(shape) == 2:
                return v.rearrange("p (a b) -> p a b", b=shape[1])
            if len(shape) == 3:
                return v.rearrange("p (a b c) -> p a b c", b=shape[1], c=shape[2])
            return v

        fA = wk(12 * SEQ, 12, SEQ)
        fB = wk(4 * SEQ, 4, SEQ)
        fC = wk(4 * SEQ, 4, SEQ)
        zA = wk(NT * 512, NT, 512)
        oBg = wk(NT * 512, NT, 512)
        zC = wk(NT * 512, NT, 512)
        vB = wk(NT * 516, NT, 4, 129)
        vC = wk(NT * 512, NT, 512)
        lt_at = used[0]
        LT = wk(NT * 512, NT, 512)
        AT = wk(NT * 512, NT, 512)
        WB = wk(NT * 512, NT, 512)
        AC = wk(NT * 512, NT, 512)
        Dm = wk(NT * 512, NT, 512)
        DT = wk(NT * 512, NT, 512)
        LB = wk(NT * 512, NT, 512)
        XB = wk(NT * 512, NT, 512)
        ktok = wk(NT * 512, NT, 512)
        vb = wk(NT * 512, NT, 512)
        uu_at = used[0]
        UU = wk(NT * 512, NT, 512)
        wT = wk(NT * 512, NT, 512)
        SA = wk(512)
        SB = wk(2 * 129, 2, 129)
        SC = wk(2 * 128, 2, 128)
        kw = wk(NT * 256, NT, 256)
        keC = wk(NT * 256, NT, 256)
        qg = wk(2 * SEQ, 2, SEQ)
        keT = wk(2 * SEQ, 2, SEQ)
        convr = work[0:4, lt_at:lt_at + 2048]
        kbg, kend = XB, LB
        oA, nB, oC = Dm, DT, LT
        half_t = lambda b, t: b[:, t, :].rearrange("p (f i) -> p f i", f=2)
        bc, uc, tc1, tc2 = half_t(Dm, 0), half_t(Dm, 1), half_t(DT, 0), half_t(DT, 1)
        gTs = LB[:, 0, 0:SEQ]
        grow = zA.rearrange("p t n -> p (t n)")
        bmg = oBg.rearrange("p t n -> p (t n)")
        sq = [XB[:, 0, :], XB[:, 1, :]]
        h = work[:, 0:NT * D].rearrange("p (t d) -> p t d", t=NT)
        yTv = [b.rearrange("p t n -> p (t n)").rearrange("p (f i) -> p f i", i=SEQ) for b in (AT, WB, AC)]
        mg_s = [XB[:, 0, :], XB[:, 1, :]]
        merged = work[:, 12 * SEQ:12 * SEQ + NT * D].rearrange("p (t d) -> p t d", t=NT)
        mT = work[:, uu_at:uu_at + NT * D].rearrange("p (k i) -> p k i", i=SEQ)
        fs = [ktok[:, i, :] for i in range(2)]
        fg = [vb[:, i, :] for i in range(2)]
        fgT = [LB[:, i, :].rearrange("p (f i) -> p f i", f=4) for i in range(2)]
        facc = work[:, lt_at:lt_at + NT * D].rearrange("p (t d) -> p t d", t=NT)

        RAW, AB_, EX, LG, SP, CUM, TOT = 0, 1, 2, 3, 4, 5, 6
        Z1, Z2, BJ, ZE, AJ = (7, 0), (7, 4), (7, 8), (7, 12), (8, 0)

        def sc(kind, a=0, n=16):
            return scal[:, kind, :, a:a + n]

        def at(where, t=None, n=4):
            k, a = where
            return scal[:, k, :, a:a + n] if t is None else scal[:, k, t, a:a + n]

        CM, MX, MP, MN = (8, 4), (8, 8), (9, 0), (9, 4)
        EZ1, EZ2, EZE, BETA = (10, 0), (10, 4), (10, 8), (9, 8)
        SI, THR, KWS, NZ = (11, 0), (11, 4), (11, 8), (11, 12)
        BJB, T0, T1 = (10, 12), (9, 12), (8, 12)
        tot2 = sb("tot2", [P, NCH, 16])
        geA = sb("geA", [P, NCH, 4])
        cmaxB = sb("cmaxB", [P, NCH, 4])
        mB = sb("mB", [P, NCH + 1, 4])
        spB = sb("spB", [P, NCH, 4])
        spc = sb("spc", [P, NCH, 2])
        aeC = sb("aeC", [P, 2, NCH])
        dB = sb("dB", [P, NT, 4])
        ssA = sb("ssA", [P, NT, 8])

        banks = [ctx.enter_context(nc.psum_tensor(f"bank{i}", [P, 512], F32)) for i in range(8)]
        facc_ps = banks[4:8]

        order = []
        for l in range(DEPTH):
            order += job_plan(l)
            if l == 0:
                order += [("ffn", l) + k for k in ffn_jobs(ffn_widths(D_FF))]
        JOB = {k: i for i, k in enumerate(order)}
        moe_jobs = ffn_jobs(ffn_widths(D_FFE))
        while len(moe_jobs) % NBANK:
            moe_jobs.append(("pad",))
        MJOB = {k: i for i, k in enumerate(moe_jobs)}
        MOE_BASE = len(order)
        while MOE_BASE % NBANK:
            MOE_BASE += 1
        PAD0 = MOE_BASE - len(order)

        def rows(n, o=1):
            return n

        def bc3(ap, n):
            return ap.rearrange("p (a o) -> p a o", o=1).broadcast_to([ap.shape[0], ap.shape[1], n])

        def rep(ap, n):
            return ap.rearrange("p (o w) -> p o w", o=1).broadcast_to([ap.shape[0], n, ap.shape[1]])

        def h4(ap, w=128):
            return ap.rearrange("p (h d) -> p h d", d=w)

        ld = {}

        block = ctx.enter_context(nc.Block())

        @block.sync
        def _(sp):
            sp.dma_start(xs[:], x[0].rearrange("(t p) d -> p t d", p=P)).then_inc(S("x_landed"), 16)
            n = 0

            def slab(src, width=W512, kt=4):
                nonlocal n
                if n >= RING:
                    sp.wait_ge(S("slab_used"), n - RING + 1)
                sp.dma_start(ring[:, n % RING, 0:kt, 0:width],
                             src.rearrange("(k p) n -> p k n", p=P)).then_inc(S(f"slab{n % RING}"), 16)
                n += 1

            def rows4(w, k, col, width=W512):
                return w[k * 512:(k + 1) * 512, col:col + width]

            for l in range(DEPTH):
                for key in slab_plan(l):
                    if key[0] == "ada":
                        slab(rows4(w_ada[l], key[2], key[3]))
                    elif key[0] == "in":
                        slab(rows4(w_in[l], key[2], key[3]))
                    elif key[0] == "mg":
                        slab(rows4(w_mg[l, key[2]], key[3], key[4] * W512))
                    elif key[0] == "br":
                        slab(rows4(w_br[l, key[2]], 0, key[3] * W512))
                    elif key[0] == "wo":
                        slab(rows4(w_o[l], key[2], key[3] * W512))
                if l == 0:
                    for f, wd in enumerate(ffn_widths(D_FF)):
                        for w in (w1_d, w3_d):
                            for k in range(2):
                                slab(rows4(w[0], k, f * W512, wd), wd)
                        for hf in range(2):
                            slab(w2_d[0, f * W512:f * W512 + wd, hf * W512:(hf + 1) * W512], kt=wd // P)
            base = n
            per = 6 * (D_FFE // W512)
            assert per % RING == 0
            with sp.Fori(0, N_EXP) as e:
                m = 0
                for f in range(D_FFE // W512):
                    srcs = [w[0, bass.ds(e, 1), k * 512:(k + 1) * 512, f * W512:(f + 1) * W512]
                            for w in (w1_e, w3_e) for k in range(2)]
                    srcs += [w2_e[0, bass.ds(e, 1), f * W512:(f + 1) * W512, hf * W512:(hf + 1) * W512]
                             for hf in range(2)]
                    for src in srcs:
                        slot = (base + m) % RING
                        sp.wait_ge(S("slab_used"), e * per + (base + m - RING + 1))
                        sp.dma_start(ring[:, slot, :, :],
                                     src.rearrange("o (k p) n -> p (o k) n", p=P)).then_inc(S(f"slab{slot}"), 16)
                        m += 1
            sp.wait_ge(S("y_ready"), 2)
            sp.dma_start(out[0].rearrange("(t p) d -> p t d", p=P), xs[:]).then_inc(S("out_stored"), 16)
            sp.wait_ge(S("out_stored"), 16)

        @block.gpsimd
        def _(pool):
            def bcast(dst, src_row):
                return pool.dma_start(dst, src_row)

            pool.dma_start(crow[:], c[0].rearrange("(k p) -> k p", p=P)).then_inc(S("c_landed"), 16)
            k = [0]

            def chain(ins):
                k[0] += 1
                ins.then_inc(S("pool_chain"), 1)
                pool.wait_ge(S("pool_chain"), k[0])

            chain(pool.memset(ident[:], 0.0))
            chain(pool.affine_select(out=ident[:], in_=ident[:], compare_op=ALU.not_equal, fill=1.0, base=0,
                                     pattern=[[-1, P]], channel_multiplier=1))
            chain(pool.memset(ones[:], 1.0))
            chain(pool.memset(same[:], 1.0))
            sv = same[:].rearrange("p (q w) -> p q w", w=L)
            chain(pool.affine_select(out=sv, in_=sv, compare_op=ALU.is_ge, fill=0.0, base=0,
                                     pattern=[[-L, 2], [0, L]], channel_multiplier=1))
            chain(pool.affine_select(out=sv, in_=sv, compare_op=ALU.is_ge, fill=0.0, base=L - 1,
                                     pattern=[[L, 2], [0, L]], channel_multiplier=-1))
            chain(pool.affine_select(out=tri[:], in_=same[:], compare_op=ALU.is_ge, fill=0.0, base=0,
                                     pattern=[[1, P]], channel_multiplier=-1))
            chain(pool.affine_select(out=negL[:], in_=same[:], compare_op=ALU.is_ge, fill=0.0, base=0,
                                     pattern=[[-1, P]], channel_multiplier=1))
            chain(pool.affine_select(out=negS[:], in_=same[:], compare_op=ALU.is_ge, fill=0.0, base=-1,
                                     pattern=[[1, P]], channel_multiplier=-1))
            chain(pool.tensor_scalar(negI[:], tri[:], -1.0, -NEG, ALU.add, ALU.mult))
            chain(pool.tensor_scalar(negS[:], negS[:], -1.0, -NEG, ALU.add, ALU.mult))
            chain(pool.tensor_scalar(negL[:], negL[:], -1.0, -NEG, ALU.add, ALU.mult))
            chain(pool.memset(half[:], 1.0))
            chain(pool.affine_select(out=half[:], in_=half[:], compare_op=ALU.is_ge, fill=0.0, base=0,
                                     pattern=[[-L, 2], [0, P]], channel_multiplier=1))
            chain(pool.affine_select(out=half[:], in_=half[:], compare_op=ALU.is_ge, fill=0.0, base=L - 1,
                                     pattern=[[L, 2], [0, P]], channel_multiplier=-1))
            chain(pool.memset(lev_m[:], 0.0))
            for lev in range(6):
                b = 1 << lev
                q = P // (2 * b)
                v = lev_m[:, lev, :].rearrange("p (q w) -> p q w", w=2 * b)[:, :, b:2 * b]
                chain(pool.memset(v, 1.0))
                chain(pool.affine_select(out=v, in_=v, compare_op=ALU.is_ge, fill=0.0, base=0,
                                         pattern=[[-2 * b, q], [0, b]], channel_multiplier=1))
                chain(pool.affine_select(out=v, in_=v, compare_op=ALU.is_ge, fill=0.0, base=b - 1,
                                         pattern=[[2 * b, q], [0, b]], channel_multiplier=-1))
            chain(pool.memset(rst[:], 1.0))
            chain(pool.memset(rst[:].rearrange("p (q w) -> p q w", w=L)[:, :, 0:1], 0.0))
            for i, v in enumerate((EPS, 1.0, LN_DKB, 0.0)):
                chain(pool.memset(cst[:, i:i + 1], v))
            chain(pool.memset(sgn16[:], 1.0))
            chain(pool.memset(sgn16[:, 4:8], -1.0))
            chain(pool.memset(sgn16[:, 12:16], -1.0))
            chain(pool.memset(cf16[:], -1.0))
            chain(pool.memset(bias16[:], 0.0))
            chain(pool.memset(mB[:], 0.0))
            chain(pool.memset(st[:], 0.0))
            pool.memset(cst[:, 4:8], 0.0).then_inc(S("consts_ready"), 1)

            for l in range(DEPTH):
                if l:
                    pool.wait_ge(S("x_ready"), 2 * NT)
                def small(dst, src):
                    pool.dma_start(dst, src).then_inc(S("small_landed"), 16)
                small(grow, g_mix[l:l + 1, :].broadcast_to([P, D]))
                for s in range(2):
                    small(mod[:, s, :], b_ada[l:l + 1, s * D:(s + 1) * D].broadcast_to([P, D]))
                small(mod[:, 2, :], b_ada[l:l + 1, 2 * D:3 * D].broadcast_to([P, D]))
                small(mod[:, 3, :], b_ada[l:l + 1, 5 * D:6 * D].broadcast_to([P, D]))
                small(convr[:, 0:1536], conv_a[l])
                small(convr[:, 1536:2048], conv_b[l])
                small(bglar[:], b_gla[l].rearrange("(k p) -> k p", p=P))
                win = w_in[l].rearrange("(k p) n -> p k n", p=P)
                small(wsm[:, :, 0:8], win[:, :, AB:AB + 8])
                small(wsm[:, :, 8:16], win[:, :, IF:IF + 8])
                small(wsm[:, :, 16:32], win[:, :, GC:GC + 16])
                small(wgla[:], w_gla2[l])
                small(bias16[:, 0:4], dt_bias[l:l + 1, :].broadcast_to([P, 4]))
                small(bias16[:, 8:12], b_i[l:l + 1, :].broadcast_to([P, 4]))
                small(bias16[:, 12:16], b_f[l:l + 1, :].broadcast_to([P, 4]))
                small(cf16[:, 0:4], a_log[l:l + 1, :].broadcast_to([P, 4]))
                small(normr[:, 0, :], norm_a[l:l + 1, :].broadcast_to([P, P]))
                small(normr[:, 1, :], norm_b[l:l + 1, :].broadcast_to([P, P]))
                small(normr[:, 2, :], norm_c[l:l + 1, :].broadcast_to([P, P]))
                small(wrt[:], w_router[0].rearrange("(k p) n -> p k n", p=P))
                small(brt[:], b_router[0:1, :].broadcast_to([P, 8]))
                pool.wait_ge(S("h_ready"), (2 * l + 1) * NT)
                for s in range(2):
                    pool.dma_start(mod[:, s, :], b_ada[l:l + 1, (3 + s) * D:(4 + s) * D].broadcast_to([P, D])) \
                        .then_inc(S("ffn_rows_landed"), 16)
                pool.wait_ge(S("y_branch"), l * 6 + 2)
                pool.dma_start(grow, g_ffn[l:l + 1, :].broadcast_to([P, D])).then_inc(S("gffn_landed"), 16)
                pool.wait_ge(S("y_branch"), l * 6 + 4)
                for g in range(3):
                    pool.dma_start(bmg[32 * g:32 * g + 1, :], b_mg[l, g:g + 1, :]).then_inc(S("bmg_landed"), 16)
            pool.wait_ge(S("h_ready"), 2 * DEPTH * NT)
            pool.dma_start(grow, g_final.rearrange("(o d) -> o d", o=1).broadcast_to([P, D])) \
                .then_inc(S("gfinal_landed"), 16)
        SMALLS = 21 * 16

        @block.tensor
        def _(pe):
            nj = [0]
            ns = [0]
            lows = [0]

            def begin(key):
                i = nj[0]
                assert order[i] == key, (order[i], key)
                if i >= NBANK:
                    pe.wait_ge(S(f"bank_free{i % NBANK}"), i // NBANK)
                return banks[i % NBANK]

            def end(ins):
                nj[0] += 1
                ins.then_inc(S("mm_done"), 1)

            def slab_at(i):
                pe.wait_ge(S(f"slab{i % RING}"), 16 * (i // RING + 1))
                return ring[:, i % RING]

            def take():
                ns[0] += 1
                return slab_at(ns[0] - 1)

            def mm(o, a, b, start, stop, **kw):
                return pe.matmul(o, a, b, start=start, stop=stop, skip_group_check=True, **kw)

            def T(o, a):
                n = a.shape[0]
                return pe.transpose(o, a, ident[0:n, 0:n])

            def project_cols(key, slabs, fts, release):
                o = begin(key)
                for i, ft in enumerate(fts):
                    for k in range(KD):
                        ins = mm(o[:, i * SEQ:(i + 1) * SEQ], slabs[k // 4][:, k % 4, ft * P:(ft + 1) * P], hT[:, k, :],
                                 k == 0, k == KD - 1)
                end(ins)

            def over_d(o, act_t, slabs, wd=W512):
                for k in range(KD):
                    ins = mm(o[:, 0:wd], act_t[:, k, :], slabs[k // 4][:, k % 4, 0:wd], k == 0, k == KD - 1)
                return ins

            def mods(l, pieces):
                for piece in pieces:
                    for hf in range(2):
                        s = [take(), take()]
                        o = begin(("mod", l, piece, hf))
                        for k in range(KD):
                            ins = mm(o[:], cact[:, k:k + 1].broadcast_to([P, P]), s[k // 4][:, k % 4, :],
                                     k == 0, k == KD - 1)
                        end(ins)
                        release(2)

            pending = []

            def release(n):
                pending.append((nj[0], n))
                if len(pending) > 1:
                    flush()

            def flush():
                upto, n = pending.pop(0)
                pe.wait_ge(S("mm_done"), upto)
                pe.sem_inc(S("slab_used"), n)

            def transposes(key, src_of, n=4):
                o = begin(key)
                for i in range(n):
                    ins = T(o[:, i * P:(i + 1) * P], src_of(i))
                end(ins)

            pe.wait_ge(S("consts_ready"), 1)
            pe.wait_ge(S("c_landed"), 16)
            pe.transpose(banks[7][:, 0:8], crow[:], ident[0:8, 0:8]).then_inc(S("c_turned"), 1)
            pe.wait_ge(S("cact_ready"), 1)
            for l in range(DEPTH):
                pe.wait_ge(S("small_landed"), SMALLS * (l + 1))
                o = begin(("cols", l))
                for i in range(16):
                    T(o[:, 4 * i:4 * i + 4], convr[:, i * P:(i + 1) * P])
                end(T(o[:, 64:66], bglar[:]))
                mods(l, (0, 1))

                def make_hT(which):
                    pe.wait_ge(S("h_ready"), (2 * l + which + 1) * NT)
                    for t in range(NT):
                        for q in range(2):
                            transposes(("hT", l, which, t, q), lambda i: h[:, t, (4 * q + i) * P:(4 * q + i + 1) * P])
                    pe.wait_ge(S("hT_ready"), (2 * l + which + 1) * 4)

                make_hT(0)
                o = begin(("small", l))
                for t in range(NT):
                    for k in range(KD):
                        ins = mm(o[:, t * 16:(t + 1) * 16], hT[:, k, t * P:(t + 1) * P], wsm[:, k, 0:16],
                                 k == 0, k == KD - 1)
                end(ins)
                o = begin(("gT", l))
                for k in range(KD):
                    ins = mm(o[0:16, 0:SEQ], wsm[:, k, 16:32], hT[:, k, :], k == 0, k == KD - 1)
                end(ins)
                pe.wait_ge(S("decay_ready"), l + 1)
                o = begin(("cum", l))
                for t in range(NT):
                    for i, m in enumerate((tri[:], same[:], half[:, 0, :], half[:, 1, :])):
                        ins = mm(o[:, (4 * t + i) * 16:(4 * t + i + 1) * 16], m, scal[:, SP, t, :], True, True)
                end(ins)
                pe.wait_ge(S("gTs_ready"), l + 1)
                o = begin(("la", l))
                for f in range(2):
                    ins = mm(o[:, f * SEQ:(f + 1) * SEQ], wgla[:, f * P:(f + 1) * P], gTs[0:16, :], True, True)
                end(ins)
                for name, n in (("qkvA", 3), ("qkB", 1), ("qkC", 1)):
                    for i in range(n):
                        s = [take(), take()]
                        project_cols((name, l, 2 * i), s, (0, 1), 0)
                        project_cols((name, l, 2 * i + 1), s, (2, 3), 0)
                        release(2)
                for name in ("zA", "vB", "oB", "vC", "zC"):
                    s = [take(), take()]
                    for t in range(NT):
                        o = begin((name, l, t))
                        end(over_d(o, hT[:, :, t * P:(t + 1) * P], s))
                    release(2)
                pe.wait_ge(S("fA_ready"), (l + 1) * 12)
                for t in range(NT):
                    for i, name in enumerate(("TQ", "TK", "TV")):
                        transposes((name, l, t), lambda j: fA[:, 4 * i + j, t * P:(t + 1) * P])

                def row_matrix(key, where, mask, t):
                    o = begin(key)
                    if mask is not None:
                        for hh in range(H):
                            mm(o[:, hh * P:(hh + 1) * P], ident[:], mask[:], hh == 0, False)
                    for hh in range(H):
                        ins = mm(o[:, hh * P:(hh + 1) * P],
                                 scal[:, where[0], t, where[1] + hh:where[1] + hh + 1].broadcast_to([P, P]),
                                 ident[:], mask is None and hh == 0, hh == H - 1)
                    end(ins)

                def scores(key, kk, qq):
                    o = begin(key)
                    for hh in range(H):
                        ins = mm(o[:, hh * P:(hh + 1) * P], kk(hh), qq(hh), hh == 0, hh == H - 1)
                    end(ins)

                def by_halves(key, lhs, rhs, rw=slice(0, P)):
                    o = begin(key)
                    for i in range(2):
                        for hh in (i, i + 2):
                            ins = mm(o[rw, hh * P:(hh + 1) * P], lhs(hh), rhs(hh), True, True)
                        if i == 0:
                            ins.then_inc(S("low_half"), 1)
                            lows[0] += 1
                            pe.wait_ge(S("low_half"), lows[0])
                    end(ins)

                pe.wait_ge(S("zA_ready"), l + 1)
                for t in range(NT):
                    ts = slice(t * P, (t + 1) * P)
                    row_matrix(("R1", l, t), Z1, negS, t)
                    scores(("KK", l, t), lambda hh: fA[:, 4 + hh, ts], lambda hh: fA[:, 4 + hh, ts])
                    row_matrix(("R2", l, t), Z2, negI, t)
                    scores(("KQ", l, t), lambda hh: fA[:, 4 + hh, ts], lambda hh: fA[:, hh, ts])
                hd = lambda b, t, hh: b[:, t, hh * P:(hh + 1) * P]
                for t in range(NT):
                    pe.wait_ge(S("LB_ready"), l * 6 * NT + t + 1)
                    scores(("X", l, 0, t), lambda hh: hd(LB, t, hh), lambda hh: ident[:])
                for lev in range(1, 6):
                    for t in range(NT):
                        pe.wait_ge(S("LB_ready"), (l * 6 + lev) * NT + t + 1)
                        pe.wait_ge(S("D_ready"), (l * 5 + lev - 1) * NT + t + 1)
                        pe.wait_ge(S("DT_ready"), (l * 6 + lev - 1) * NT + t + 1)
                        scores(("X", l, lev, t), lambda hh: hd(LB, t, hh), lambda hh: hd(Dm, t, hh))
                    for t in range(NT):
                        pe.wait_ge(S("X_ready"), (l * 5 + lev - 1) * NT + t + 1)
                        if lev < 5:
                            scores(("Y", l, lev, t), lambda hh: hd(DT, t, hh), lambda hh: hd(XB, t, hh))
                        scores(("YT", l, lev, t), lambda hh: hd(XB, t, hh), lambda hh: hd(DT, t, hh))
                for t in range(NT):
                    pe.wait_ge(S("DT_ready"), (l * 6 + 5) * NT + t + 1)
                    pe.wait_ge(S("kbg_ready"), l * NT + t + 1)
                    scores(("U", l, t), lambda hh: hd(DT, t, hh), lambda hh: hd(vb, t, hh))
                    scores(("WT", l, t), lambda hh: hd(kbg, t, hh), lambda hh: hd(DT, t, hh))
                pe.wait_ge(S("aj_ready"), l + 1)
                for t in range(NT):
                    row_matrix(("RA", l, t), AJ, None, t)
                hp = lambda hh: slice(64 * (hh % 2), 64 * (hh % 2) + 64)
                pe.wait_ge(S("fB_ready"), (l + 1) * 4)
                pe.wait_ge(S("gla_ready"), l + 1)
                pe.wait_ge(S("stabB_ready"), l + 1)
                for t in range(NT):
                    ts = slice(t * P, (t + 1) * P)
                    transposes(("TKB", l, t), lambda i: fB[:, 2 + i, ts], n=2)
                    row_matrix(("RB", l, t), NZ, negI, t)
                    by_halves(("KQB", l, t), lambda hh: fB[hp(hh), 2 + hh // 2, ts], lambda hh: fB[hp(hh), hh // 2, ts])
                    by_halves(("KQC", l, t), lambda hh: fC[hp(hh), 2 + hh // 2, ts], lambda hh: fC[hp(hh), hh // 2, ts])
                    transposes(("TKC", l, t), lambda i: keT[:, i, ts], n=2)
                pe.wait_ge(S("scan_ready"), l + 1)
                for n in range(NCH):
                    t, r = n // 2, n % 2
                    rw = slice(64 * r, 64 * r + 64)
                    tk = slice(n * L, (n + 1) * L)
                    pe.wait_ge(S("SA_ready"), l * NCH + n + 1)
                    o = begin(("P1", l, n))
                    for hh in range(H):
                        ins = mm(o[rw, hh * P:(hh + 1) * P], wT[:, t, hh * P + 64 * r:hh * P + 64 * r + 64],
                                 SA[:, hh * P:(hh + 1) * P], True, True)
                    end(ins)
                    o = begin(("P2", l, n))
                    for hh in range(H):
                        ins = mm(o[rw, hh * P:(hh + 1) * P], fA[:, hh, tk], SA[:, hh * P:(hh + 1) * P], True, True)
                    end(ins)
                    pe.wait_ge(S("SB_ready"), l * NCH + n + 1)
                    for p in range(2):
                        o = begin((f"QB{p}", l, n))
                        for i in range(2):
                            ins = mm(o[rw, i * 129:(i + 1) * 129], fB[64 * p:64 * p + 64, i, tk],
                                     SB[64 * p:64 * p + 64, i, :], True, True)
                        end(ins)
                    o = begin(("KVB", l, n))
                    for hh in range(H):
                        ins = mm(o[hp(hh), (hh // 2) * 129:(hh // 2 + 1) * 129], kw[rw, t, hh * 64:(hh + 1) * 64],
                                 vB[rw, t, hh, :], True, True)
                    end(ins)
                    pe.wait_ge(S("SC_ready"), l * NCH + n + 1)
                    by_halves(("QC", l, n), lambda hh: qg[hp(hh), hh // 2, tk], lambda hh: SC[hp(hh), hh // 2, :], rw)
                    o = begin(("KVC", l, n))
                    for hh in range(H):
                        ins = mm(o[hp(hh), (hh // 2) * P:(hh // 2 + 1) * P], keC[rw, t, hh * 64:(hh + 1) * 64],
                                 vC[rw, t, hh * P:(hh + 1) * P], True, True)
                    end(ins)
                    pe.wait_ge(S("delta_ready"), l * NCH + n + 1)
                    o = begin(("P3", l, n))
                    for hh in range(H):
                        ins = mm(o[:, hh * P:(hh + 1) * P], kend[rw, t, hh * P:(hh + 1) * P],
                                 UU[rw, t, hh * P:(hh + 1) * P], True, True)
                    end(ins)
                for t in range(NT):
                    scores(("OA", l, t), lambda hh: hd(AT, t, hh), lambda hh: hd(UU, t, hh))
                    for p in range(2):
                        o = begin((f"OB{p}", l, t))
                        for i in range(2):
                            ins = mm(o[:, i * 129:(i + 1) * 129], hd(WB, t, p + 2 * i), vB[:, t, p + 2 * i, :], True, True)
                        end(ins)
                    scores(("OC", l, t), lambda hh: hd(AC, t, hh), lambda hh: hd(vC, t, hh))
                mods(l, (2, 3, 4, 5))
                ysrc = (oA, nB, oC)
                for g in range(3):
                    for t in range(NT):
                        pe.wait_ge(S("y_branch"), l * 6 + 2 * g + t + 1)
                        transposes(("yT", l, g, t), lambda i: ysrc[g][:, t, i * P:(i + 1) * P])
                pe.wait_ge(S("yT_ready"), (l + 1) * 6)
                pe.wait_ge(S("bmg_landed"), 48 * (l + 1))
                for g in range(3):
                    for hf in range(2):
                        s = [take(), take()]
                        sb_ = take()
                        for t in range(NT):
                            o = begin(("mg", l, g, hf, t))
                            over_d(o, hT[:, :, t * P:(t + 1) * P], s)
                            end(mm(o[:], ones[32 * g:32 * g + 1, :], bmg[32 * g:32 * g + 1, hf * W512:(hf + 1) * W512],
                                   False, True))
                            o = begin(("br", l, g, hf, t))
                            for k in range(4):
                                ins = mm(o[:], yTv[g][:, k, t * P:(t + 1) * P], sb_[:, k, :], k == 0, k == 3)
                            end(ins)
                        release(3)
                pe.wait_ge(S("merged_ready"), (l + 1) * 12)
                for t in range(NT):
                    for q in range(2):
                        transposes(("mT", l, t, q), lambda i: merged[:, t, (4 * q + i) * P:(4 * q + i + 1) * P])
                pe.wait_ge(S("mT_ready"), (l + 1) * 4)
                for hf in range(2):
                    s = [take(), take()]
                    for t in range(NT):
                        o = begin(("wo", l, hf, t))
                        end(over_d(o, mT[:, :, t * P:(t + 1) * P], s))
                    release(2)
                flush()
                make_hT(1)
                if l == 0:
                    widths = ffn_widths(D_FF)
                    last = None

                    def turn(f, t):
                        pe.wait_ge(S("g_ready"), f * NT + t + 1)
                        o = begin(("ffn", l, "gT", f, t))
                        for i in range(widths[f] // P):
                            ins = T(o[:, i * P:(i + 1) * P], fg[t][:, i * P:(i + 1) * P])
                        end(ins)

                    def down(f, t):
                        if t == 0:
                            slabs[f] = [slab_at(slabs[f]), slab_at(slabs[f] + 1)]
                        s = slabs[f]
                        pe.wait_ge(S("gT_ready"), f * NT + t + 1)
                        kt = widths[f] // P
                        for hf in range(2):
                            for k in range(kt):
                                ins = mm(facc_ps[2 * t + hf][:], fgT[t][:, k, :], s[hf][:, k, :], f == 0 and k == 0,
                                         f == len(widths) - 1 and k == kt - 1)
                        ins.then_inc(S("down_done"), 1)

                    slabs = {}
                    steps = [(f, t) for f in range(len(widths)) for t in range(NT)]
                    for i, (f, t) in enumerate(steps):
                        if t == 0:
                            u = [take() for _ in range(4)]
                            slabs[f] = ns[0]
                            ns[0] += 2
                        for j, name in enumerate(("w1", "w3")):
                            o = begin(("ffn", l, name, f, t))
                            end(over_d(o, hT[:, :, t * P:(t + 1) * P], u[2 * j:2 * j + 2], widths[f]))
                        upto = nj[0]
                        if t == 1 and f >= 1:
                            pe.wait_ge(S("down_done"), 2 * f)
                            pe.sem_inc(S("slab_used"), 2)
                        if i > 0:
                            turn(*steps[i - 1])
                            down(*steps[i - 1])
                        if t == 1:
                            pe.wait_ge(S("mm_done"), upto)
                            pe.sem_inc(S("slab_used"), 4)
                    turn(*steps[-1])
                    down(*steps[-1])
                    pe.wait_ge(S("down_done"), 2 * len(widths))
                    pe.sem_inc(S("slab_used"), 2)
                else:
                    o = begin(("router", l))
                    for t in range(NT):
                        for k in range(KD):
                            ins = mm(o[:, 8 * t:8 * t + 8], hT[:, k, t * P:(t + 1) * P], wrt[:, k, :], k == 0, k == KD - 1)
                    end(ins)
            for i in range(PAD0):
                pe.wait_ge(S(f"bank_free{nj[0] % NBANK}"), nj[0] // NBANK)
                pe.wait_ge(S("mm_done"), nj[0])
                pe.sem_inc(S("mm_done"), 1)
                nj[0] += 1
            assert nj[0] == MOE_BASE
            NF = D_FFE // W512
            per, base, jper = 6 * NF, ns[0], len(moe_jobs)
            pe.sem_inc(S("edown_done"), NT)
            with pe.Fori(0, N_EXP) as e:
                cnt = [0]

                def mbegin(key):
                    i = MJOB[key]
                    assert i == cnt[0]
                    pe.wait_ge(S(f"bank_free{i % NBANK}"), e * (jper // NBANK) + (MOE_BASE + i) // NBANK)
                    return banks[i % NBANK]

                def mend(ins):
                    cnt[0] += 1
                    ins.then_inc(S("mm_done"), 1)

                got = [0]

                def mtake():
                    got[0] += 1
                    return mslab(got[0] - 1)

                def mslab(i):
                    i += base
                    pe.wait_ge(S(f"slab{i % RING}"), e * (16 * per // RING) + 16 * (i // RING + 1))
                    return ring[:, i % RING]

                def mturn(f, t):
                    pe.wait_ge(S("eg_ready"), e * (NT * NF) + (NT + f * NT + t + 1))
                    o = mbegin(("gT", f, t))
                    for i in range(4):
                        ins = T(o[:, i * P:(i + 1) * P], fg[t][:, i * P:(i + 1) * P])
                    mend(ins)

                def mdown(f, t):
                    if t == 0:
                        slabs[f] = [mslab(slabs[f]), mslab(slabs[f] + 1)]
                    s = slabs[f]
                    pe.wait_ge(S("egT_ready"), e * (NT * NF) + (NT + f * NT + t + 1))
                    if f == 0:
                        pe.wait_ge(S("facc_free"), e * NT + t + 1)
                    for hf in range(2):
                        for k in range(4):
                            ins = mm(facc_ps[2 * t + hf][:], fgT[t][:, k, :], s[hf][:, k, :], f == 0 and k == 0,
                                     f == NF - 1 and k == 3)
                    ins.then_inc(S("edown_done"), 1)

                steps = [(f, t) for f in range(NF) for t in range(NT)]
                slabs = {}
                for i, (f, t) in enumerate(steps):
                    if t == 0:
                        u = [mtake() for _ in range(4)]
                        slabs[f] = got[0]
                        got[0] += 2
                    for j, name in enumerate(("w1", "w3")):
                        o = mbegin((name, f, t))
                        mend(over_d(o, hT[:, :, t * P:(t + 1) * P], u[2 * j:2 * j + 2]))
                    upto = cnt[0]
                    if t == 1 and f >= 1:
                        pe.wait_ge(S("edown_done"), e * (NT * NF) + (NT + 2 * f))
                        pe.sem_inc(S("slab_used"), 2)
                    if i > 0:
                        pf, pt = steps[i - 1]
                        mturn(pf, pt)
                        mdown(pf, pt)
                    if t == 1:
                        pe.wait_ge(S("mm_done"), e * jper + (MOE_BASE + upto))
                        pe.sem_inc(S("slab_used"), 4)
                pf, pt = steps[-1]
                mturn(pf, pt)
                mdown(pf, pt)
                pe.wait_ge(S("edown_done"), e * (NT * NF) + (NT + 2 * (pf + 1)))
                pe.sem_inc(S("slab_used"), 2)
                while cnt[0] < jper:
                    pe.wait_ge(S(f"bank_free{cnt[0] % NBANK}"), e * (jper // NBANK) + (MOE_BASE + cnt[0]) // NBANK)
                    pe.wait_ge(S("mm_done"), e * jper + (MOE_BASE + cnt[0]))
                    pe.sem_inc(S("mm_done"), 1)
                    cnt[0] += 1

        @block.scalar
        def _(act):
            k = [0]

            def chain(ins):
                k[0] += 1
                ins.then_inc(S("act_chain"), 1)
                act.wait_ge(S("act_chain"), k[0])

            def job(key):
                act.wait_ge(S("mm_done"), JOB[key] + 1)
                return banks[JOB[key] % NBANK]

            def free(key, ins):
                ins.then_inc(S(f"bank_free{JOB[key] % NBANK}"), 1)

            def done(name, ins, n=1):
                ins.then_inc(S(name), n)

            def rstd(dst, src, div):
                chain(act.activation(dst, src, ACT.Ln, bias=cst[:, 0:1], scale=1.0 / div))
                return act.activation(dst, dst, ACT.Exp, scale=-0.5)

            def rms(l, which):
                for t in range(NT):
                    for q in range(2):
                        chain(act.activation(facc_ps[q][:], xs[:, t, q * 512:(q + 1) * 512], ACT.Square,
                                             accum_out=st[:, 4 * t + q:4 * t + q + 1]))
                    chain(act.activation(st[:, 4 * t + 2:4 * t + 3], st[:, 4 * t:4 * t + 1], ACT.Identity,
                                         bias=st[:, 4 * t + 1:4 * t + 2]))
                    done("rstd_ready", rstd(st[:, 4 * t + 3:4 * t + 4], st[:, 4 * t + 2:4 * t + 3], D))

            act.wait_ge(S("consts_ready"), 1)
            act.wait_ge(S("c_turned"), 1)
            done("cact_ready", act.activation(cact[:], banks[7][:, 0:8], ACT.Silu))
            for l in range(DEPTH):
                if l == 0:
                    act.wait_ge(S("x_landed"), 16)
                    act.wait_ge(S("cact_ready"), 1)
                else:
                    act.wait_ge(S("x_ready"), 2 * NT * l)
                rms(l, 0)
                act.wait_ge(S("small_landed"), SMALLS * (l + 1))
                chain(act.activation(cf16[:, 0:4], cf16[:, 0:4], ACT.Exp))
                done("cf_exp", act.activation(cf16[:, 0:4], cf16[:, 0:4], ACT.Copy, scale=-1.0))

                def copy_hT(which):
                    for t in range(NT):
                        for q in range(2):
                            b = job(("hT", l, which, t, q))
                            chain(act.activation(hT[:, 4 * q:4 * q + 4, t * P:(t + 1) * P], h4(b[:]), ACT.Copy))
                            act.sem_inc(S(f"bank_free{JOB[('hT', l, which, t, q)] % NBANK}"), 1)
                            act.sem_inc(S("hT_ready"), 1)
                copy_hT(0)
                b = job(("gT", l))
                chain(act.activation(gTs[0:16, :], b[0:16, 0:SEQ], ACT.Copy))
                act.sem_inc(S(f"bank_free{JOB[('gT', l)] % NBANK}"), 1)
                act.sem_inc(S("gTs_ready"), 1)
                act.wait_ge(S("abs_ready"), 2 * l + 1)
                chain(act.activation(sc(EX), sc(AB_), ACT.Exp, scale=-1.0))
                done("softplus_ln", act.activation(sc(LG), sc(EX), ACT.Ln, bias=cst[:, 1:2]))
                act.wait_ge(S("decay_ready"), l + 1)
                done("beta_ready", act.activation(at(BETA), sc(SP, 4, 4), ACT.Exp))
                act.wait_ge(S("abs_ready"), 2 * l + 2)
                chain(act.activation(tc1, tc1, ACT.Exp, scale=-1.0))
                done("softplus_ln", act.activation(tc1, tc1, ACT.Ln, bias=cst[:, 1:2]))
                for i in range(6):
                    act.wait_ge(S("conv_ready"), l * 16 + 2 * i + 2)
                    done("fA_ready", act.activation(fA[:, 2 * i:2 * i + 2, :], fA[:, 2 * i:2 * i + 2, :], ACT.Silu), 2)
                for i in range(2):
                    act.wait_ge(S("conv_ready"), l * 16 + 12 + 2 * i + 2)
                    done("fB_ready", act.activation(fB[:, 2 * i:2 * i + 2, :], fB[:, 2 * i:2 * i + 2, :], ACT.Silu), 2)
                for i in range(2):
                    b = job(("qkC", l, i))
                    chain(act.activation(fC[:, 2 * i:2 * i + 2, :].rearrange("p a b -> p (a b)"), b[:], ACT.Copy,
                                         scale=0.125 if i == 0 else 1.0))
                    act.sem_inc(S(f"bank_free{JOB[('qkC', l, i)] % NBANK}"), 1)
                act.sem_inc(S("fC_ready"), 1)
                act.wait_ge(S("glaexp_in"), l + 1)
                chain(act.activation(tc2, uc, ACT.Exp, scale=-1.0))
                chain(act.activation(uc, uc, ACT.Exp))
                chain(act.activation(tc1, tc1, ACT.Exp))
                chain(act.activation(bc, bc, ACT.Exp))
                act.sem_inc(S("glaexp_ready"), 1)
                for name, dst, fn in (("zA", zA, ACT.Silu), ("vB", None, ACT.Copy), ("oB", oBg, ACT.Sigmoid),
                                      ("vC", vC, ACT.Copy), ("zC", zC, ACT.Silu)):
                    for t in range(NT):
                        b = job((name, l, t))
                        d = dst[:, t, :] if dst is not None else vB[:, t, :, 0:128]
                        chain(act.activation(d, b[:] if dst is not None else h4(b[:]), fn))
                        act.sem_inc(S(f"bank_free{JOB[(name, l, t)] % NBANK}"), 1)
                        act.sem_inc(S("tok_ready"), 1)
                for t in range(NT):
                    b = job(("TQ", l, t))
                    if t:
                        act.wait_ge(S("sq_used"), l * 4 + 2 * t - 1)
                    chain(act.activation(sq[0], b[:], ACT.Square))
                    act.sem_inc(S(f"bank_free{JOB[('TQ', l, t)] % NBANK}"), 1)
                    act.sem_inc(S("sq_ready"), 1)
                    b = job(("TK", l, t))
                    if t:
                        act.wait_ge(S("sq_used"), l * 4 + 2 * t)
                    chain(act.activation(ktok[:, t, :], b[:], ACT.Copy))
                    chain(act.activation(sq[1], b[:], ACT.Square))
                    act.sem_inc(S(f"bank_free{JOB[('TK', l, t)] % NBANK}"), 1)
                    act.sem_inc(S("sq_ready"), 1)
                act.wait_ge(S("ss_ready"), l + 1)
                done("lnss_ready", act.activation(ssA[:], ssA[:], ACT.Ln, bias=cst[:, 0:1]))
                act.wait_ge(S("zA_ready"), l + 1)
                chain(act.activation(sc(10, 0, 12)[:, :, 0:8], sc(7, 0, 8), ACT.Exp))
                chain(act.activation(at(EZE), at(ZE), ACT.Exp))
                chain(act.activation(geA[:], tot2[:, :, 0:4], ACT.Exp))
                act.sem_inc(S("expA_ready"), 1)
                for t in range(NT):
                    for name, dst in (("R1", LT), ("R2", AT)):
                        b = job((name, l, t))
                        for hh in range(H):
                            ins = act.activation(dst[:, t, hh * P:(hh + 1) * P], b[:, hh * P:(hh + 1) * P], ACT.Exp,
                                                 bias=scal[:, BJ[0], t, BJ[1] + hh:BJ[1] + hh + 1])
                            if hh < H - 1:
                                ins.then_inc(S("act_chain"), 1)
                                k[0] += 1
                            else:
                                chain(ins)
                        act.sem_inc(S(f"bank_free{JOB[(name, l, t)] % NBANK}"), 1)
                        act.sem_inc(S("decayA_ready"), 1)
                for t in range(NT):
                    b = job(("WT", l, t))
                    chain(act.activation(wT[:, t, :], b[:], ACT.Copy))
                    act.sem_inc(S(f"bank_free{JOB[('WT', l, t)] % NBANK}"), 1)
                    act.sem_inc(S("wT_ready"), 1)
                act.wait_ge(S("stabB_ready"), l + 1)
                chain(act.activation(at(SI), at(T0), ACT.Exp))
                chain(act.activation(at(THR), at(T1), ACT.Exp))
                chain(act.activation(at(KWS), at(MN), ACT.Exp, bias=cst[:, 2:3]))
                chain(act.activation(spB[:], spB[:], ACT.Exp))
                act.sem_inc(S("expB_ready"), 1)
                for t in range(NT):
                    b = job(("RB", l, t))
                    for hh in range(H):
                        chain(act.activation(WB[:, t, hh * P:(hh + 1) * P], b[:, hh * P:(hh + 1) * P], ACT.Exp,
                                             bias=scal[:, BJB[0], t, BJB[1] + hh:BJB[1] + hh + 1]))
                    act.sem_inc(S(f"bank_free{JOB[('RB', l, t)] % NBANK}"), 1)
                    act.sem_inc(S("decayB_ready"), 1)
                for g in range(3):
                    for t in range(NT):
                        act.wait_ge(S("o_ready"), l * 6 + 2 * g + t + 1)
                        src = (oA, nB, oC)[g][:, t, :]
                        src = h4(src)
                        done("osq_ready", act.activation(h4(UU[:, t, :]), src, ACT.Square))
                        act.wait_ge(S("oss_ready"), l * 6 + 2 * g + t + 1)
                        r = st[:, 16 + 8 * t:20 + 8 * t]
                        done("orstd_ready", rstd(r, r, P))
                for g in range(3):
                    for t in range(NT):
                        key = ("yT", l, g, t)
                        b = job(key)
                        chain(act.activation(yTv[g][:, :, t * P:(t + 1) * P], h4(b[:]), ACT.Copy))
                        act.sem_inc(S(f"bank_free{JOB[key] % NBANK}"), 1)
                        act.sem_inc(S("yT_ready"), 1)
                m = 0
                for g in range(3):
                    for hf in range(2):
                        for t in range(NT):
                            key = ("mg", l, g, hf, t)
                            b = job(key)
                            if m >= 2:
                                act.wait_ge(S("merged_ready"), l * 12 + m - 1)
                            chain(act.activation(mg_s[m % 2], b[:], ACT.Sigmoid))
                            act.sem_inc(S(f"bank_free{JOB[key] % NBANK}"), 1)
                            act.sem_inc(S("mgate_ready"), 1)
                            m += 1
                for t in range(NT):
                    for q in range(2):
                        key = ("mT", l, t, q)
                        b = job(key)
                        chain(act.activation(mT[:, 4 * q:4 * q + 4, t * P:(t + 1) * P], h4(b[:]), ACT.Copy))
                        act.sem_inc(S(f"bank_free{JOB[key] % NBANK}"), 1)
                        act.sem_inc(S("mT_ready"), 1)
                act.wait_ge(S("x_ready"), (2 * l + 1) * NT)
                rms(l, 1)
                copy_hT(1)
                if l == 0:
                    widths = ffn_widths(D_FF)
                    steps = [(f, t) for f in range(len(widths)) for t in range(NT)]

                    def gT_copy(f, t):
                        key = ("ffn", l, "gT", f, t)
                        b = job(key)
                        if f > 0:
                            act.wait_ge(S("down_done"), f * NT + t - 1)
                        kt = widths[f] // P
                        chain(act.activation(fgT[t][:, 0:kt, :], b[:, 0:widths[f]].rearrange("p (a b) -> p a b", b=P),
                                             ACT.Copy))
                        act.sem_inc(S(f"bank_free{JOB[key] % NBANK}"), 1)
                        act.sem_inc(S("gT_ready"), 1)

                    for i, (f, t) in enumerate(steps):
                        b = job(("ffn", l, "w1", f, t))
                        if f > 0:
                            act.wait_ge(S("g_ready"), (f - 1) * NT + t + 1)
                        done("silu_ready", act.activation(fs[t][:, 0:widths[f]], b[:, 0:widths[f]], ACT.Silu))
                        act.wait_ge(S("silu_ready"), f * NT + t + 1)
                        act.sem_inc(S(f"bank_free{JOB[('ffn', l, 'w1', f, t)] % NBANK}"), 1)
                        if i > 0:
                            gT_copy(*steps[i - 1])
                    gT_copy(*steps[-1])
            act.wait_ge(S("route_in"), 1)
            done("route_exp", act.activation(comb[:], comb[:], ACT.Exp))
            NF = D_FFE // W512
            jper = len(moe_jobs)
            act.sem_inc(S("egT_ready"), NT)
            with act.Fori(0, N_EXP) as e:
                def mjob(key):
                    act.wait_ge(S("mm_done"), e * jper + (MOE_BASE + MJOB[key] + 1))
                    return banks[MJOB[key] % NBANK]

                def mcopy(f, t):
                    b = mjob(("gT", f, t))
                    act.wait_ge(S("edown_done"), e * (NT * NF) + (f * NT + t + 1))
                    act.activation(fgT[t], h4(b[:]), ACT.Copy).then_inc(S("egT_ready"), 1)
                    act.wait_ge(S("egT_ready"), e * (NT * NF) + (NT + f * NT + t + 1))
                    act.sem_inc(S(f"bank_free{MJOB[('gT', f, t)] % NBANK}"), 1)

                steps = [(f, t) for f in range(NF) for t in range(NT)]
                for i, (f, t) in enumerate(steps):
                    b = mjob(("w1", f, t))
                    act.wait_ge(S("eg_ready"), e * (NT * NF) + (f * NT + t + 1))
                    act.activation(fs[t], b[:], ACT.Silu).then_inc(S("esilu_ready"), 1)
                    act.wait_ge(S("esilu_ready"), e * (NT * NF) + (f * NT + t + 1))
                    act.sem_inc(S(f"bank_free{MJOB[('w1', f, t)] % NBANK}"), 1)
                    if i > 0:
                        mcopy(*steps[i - 1])
                mcopy(*steps[-1])
            act.wait_ge(S("x_ready"), 2 * NT * DEPTH)
            rms(DEPTH, 0)

        @block.vector
        def _(v):
            k = [0]

            def chain(ins):
                k[0] += 1
                ins.then_inc(S("dve_chain"), 1)
                v.wait_ge(S("dve_chain"), k[0])

            def job(key):
                v.wait_ge(S("mm_done"), JOB[key] + 1)
                return banks[JOB[key] % NBANK]

            def fr(key):
                v.sem_inc(S(f"bank_free{JOB[key] % NBANK}"), 1)

            def tt(o, a, b, op=ALU.mult):
                return v.tensor_tensor(o, a, b, op)

            def normalise(l, which):
                chain(v.scalar_tensor_tensor(mod[:, 1, :], mod[:, 1, :], 1.0, grow, ALU.add, ALU.mult))
                for t in range(NT):
                    v.wait_ge(S("rstd_ready"), (2 * l + which) * NT + t + 1)
                    chain(v.scalar_tensor_tensor(h[:, t, :], xs[:, t, :], st[:, 4 * t + 3:4 * t + 4], mod[:, 1, :],
                                                 ALU.mult, ALU.mult))
                    chain(tt(h[:, t, :], h[:, t, :], mod[:, 0, :], ALU.add))
                    v.sem_inc(S("h_ready"), 1)

            def add_mod(l, piece, slot):
                for hf in range(2):
                    b = job(("mod", l, piece, hf))
                    s = mod[:, slot, hf * 512:(hf + 1) * 512]
                    chain(tt(s, b[:], s, ALU.add))
                    fr(("mod", l, piece, hf))

            v.wait_ge(S("consts_ready"), 1)
            v.wait_ge(S("x_landed"), 16)
            for l in range(DEPTH):
                v.wait_ge(S("small_landed"), SMALLS * (l + 1))
                b = job(("cols", l))
                chain(v.tensor_copy(cols[:], b[:, 0:66]))
                fr(("cols", l))
                add_mod(l, 0, 0)
                add_mod(l, 1, 1)
                normalise(l, 0)
                b = job(("small", l))
                pv = b[:, 0:32].rearrange("p (t n) -> p t n", n=16)
                chain(tt(sc(RAW), pv, rep(bias16[:], NT), ALU.add))
                fr(("small", l))
                chain(tt(sc(RAW), sc(RAW), rep(sgn16[:], NT)))
                chain(v.scalar_tensor_tensor(sc(AB_), sc(RAW), -1.0, sc(RAW), ALU.mult, ALU.max))
                v.sem_inc(S("abs_ready"), 1)
                v.wait_ge(S("softplus_ln"), 2 * l + 1)
                chain(v.scalar_tensor_tensor(sc(SP), sc(RAW), 0.0, sc(LG), ALU.max, ALU.add))
                v.wait_ge(S("cf_exp"), l + 1)
                chain(tt(sc(SP), sc(SP), rep(cf16[:], NT)))
                v.sem_inc(S("decay_ready"), 1)
                b = job(("cum", l))
                pv = b[:, 0:128].rearrange("p (t i n) -> p t i n", t=NT, i=4)
                chain(v.tensor_copy(sc(CUM), pv[:, :, 0, :]))
                chain(v.tensor_copy(sc(TOT), pv[:, :, 1, :]))
                chain(v.tensor_copy(tot2[:].rearrange("p (t r) n -> p t r n", r=2), pv[:, :, 2:4, :]))
                fr(("cum", l))
                b = job(("la", l))
                for f in range(2):
                    chain(v.tensor_scalar(uc[:, f, :], b[:, f * SEQ:(f + 1) * SEQ], cols[:, 64 + f:65 + f], -1.0,
                                          ALU.add, ALU.mult))
                fr(("la", l))
                chain(v.scalar_tensor_tensor(tc1, uc, -1.0, uc, ALU.mult, ALU.max))
                v.sem_inc(S("abs_ready"), 1)
                v.wait_ge(S("softplus_ln"), 2 * l + 2)
                chain(v.scalar_tensor_tensor(tc2, uc, 0.0, tc1, ALU.max, ALU.add))
                chain(v.tensor_scalar(tc2, tc2, -1.0 / 16.0, None, ALU.mult))
                for f in range(2):
                    chain(v.tensor_tensor_scan(bc[:, f, :], rst[:], tc2[:, f, :], 0.0, ALU.mult, ALU.add))
                for i in range(8):
                    key = ("qkvA", l, i) if i < 6 else ("qkB", l, i - 6)
                    b = job(key)
                    for j in range(2):
                        f = 2 * i + j
                        dst = fA[:, f, :] if i < 6 else fB[:, f - 12, :]
                        src = b[:, j * SEQ:(j + 1) * SEQ]
                        tap = lambda q: cols[:, 4 * f + q:4 * f + q + 1]
                        chain(v.tensor_scalar(dst, src, tap(3), None, ALU.mult))
                        for s in range(1, 4):
                            chain(v.scalar_tensor_tensor(dst[:, s:SEQ], src[:, 0:SEQ - s], tap(3 - s),
                                                         dst[:, s:SEQ], ALU.mult, ALU.add))
                        v.sem_inc(S("conv_ready"), 1)
                    fr(key)
                v.wait_ge(S("fC_ready"), l + 1)
                bcv = bc.rearrange("p f (n i) -> p (f n) i", i=L)
                fc = lambda ap: ap.rearrange("p f (n i) -> p (f n) i", i=L)
                chain(tt(fc(uc), bcv, bcv[:, :, L // 2:L // 2 + 1].broadcast_to([P, 8, L]), ALU.subtract))
                chain(tt(fc(tc1), bcv[:, :, L - 1:L].broadcast_to([P, 8, L]), bcv, ALU.subtract))
                v.sem_inc(S("glaexp_in"), 1)
                v.wait_ge(S("glaexp_ready"), l + 1)
                chain(tt(keT, fC[:, 2:4, :], tc1))
                chain(tt(qg, fC[:, 0:2, :], bc))
                chain(v.tensor_copy(aeC[:], bc.rearrange("p f (n i) -> p f n i", i=L)[:, :, :, L - 1]))
                chain(tt(fC[:, 0:2, :], fC[:, 0:2, :], uc))
                chain(tt(fC[:, 2:4, :], fC[:, 2:4, :], tc2))
                v.sem_inc(S("gla_ready"), 1)
                for t in range(NT):
                    for i in range(2):
                        v.wait_ge(S("sq_ready"), l * 4 + 2 * t + i + 1)
                        chain(v.tensor_reduce(ssA[:, t, 4 * i:4 * i + 4], h4(sq[i]), X, ALU.add))
                        v.sem_inc(S("sq_used"), 1)
                    if t == 0:
                        v.wait_ge(S("beta_ready"), l + 1)
                    b = job(("TV", l, t))
                    chain(tt(h4(vb[:, t, :]), h4(b[:]), bc3(at(BETA, t), P)))
                    fr(("TV", l, t))
                v.sem_inc(S("ss_ready"), 1)
                v.wait_ge(S("lnss_ready"), l + 1)
                gc, lb = sc(CUM, 0, 4), sc(SP, 4, 4)
                lq, lk = ssA[:, :, 0:4], ssA[:, :, 4:8]
                stt = v.scalar_tensor_tensor
                chain(stt(at(BJ), lk, -0.5, gc, ALU.mult, ALU.subtract))
                chain(stt(at(Z1), lk, -0.5, gc, ALU.mult, ALU.add))
                chain(tt(at(Z1), at(Z1), lb, ALU.add))
                chain(stt(at(Z2), lq, -0.5, gc, ALU.mult, ALU.add))
                chain(v.tensor_scalar(at(Z2), at(Z2), LN_DKA, None, ALU.add))
                chain(tt(at(ZE), at(BJ), sc(TOT, 0, 4), ALU.add))
                chain(tt(at(AJ), sc(RAW, 8, 4), sc(CUM, 12, 4), ALU.subtract))
                v.sem_inc(S("zA_ready"), 1)
                v.sem_inc(S("aj_ready"), 1)
                for t in range(NT):
                    b = job(("KK", l, t))
                    v.wait_ge(S("decayA_ready"), l * 4 + 2 * t + 1)
                    chain(tt(LT[:, t, :], b[:], LT[:, t, :]))
                    fr(("KK", l, t))
                    b = job(("KQ", l, t))
                    v.wait_ge(S("decayA_ready"), l * 4 + 2 * t + 2)
                    chain(tt(AT[:, t, :], b[:], AT[:, t, :]))
                    fr(("KQ", l, t))
                for t in range(NT):
                    chain(tt(h4(LB[:, t, :]), h4(LT[:, t, :]), rep(lev_m[:, 0, :], H)))
                    v.sem_inc(S("LB_ready"), 1)
                    chain(tt(h4(DT[:, t, :]), rep(ident[:], H), h4(LB[:, t, :]), ALU.subtract))
                    v.sem_inc(S("DT_ready"), 1)
                for t in range(NT):
                    b = job(("X", l, 0, t))
                    chain(tt(h4(Dm[:, t, :]), rep(ident[:], H), h4(b[:]), ALU.subtract))
                    fr(("X", l, 0, t))
                    v.sem_inc(S("D_ready"), 1)
                    chain(tt(h4(LB[:, t, :]), h4(LT[:, t, :]), rep(lev_m[:, 1, :], H)))
                    v.sem_inc(S("LB_ready"), 1)
                for lev in range(1, 6):
                    for t in range(NT):
                        b = job(("X", l, lev, t))
                        chain(v.tensor_copy(XB[:, t, :], b[:]))
                        fr(("X", l, lev, t))
                        v.sem_inc(S("X_ready"), 1)
                        if lev < 5:
                            chain(tt(h4(LB[:, t, :]), h4(LT[:, t, :]), rep(lev_m[:, lev + 1, :], H)))
                            v.sem_inc(S("LB_ready"), 1)
                    for t in range(NT):
                        if lev < 5:
                            b = job(("Y", l, lev, t))
                            chain(tt(Dm[:, t, :], Dm[:, t, :], b[:], ALU.subtract))
                            fr(("Y", l, lev, t))
                            v.sem_inc(S("D_ready"), 1)
                        b = job(("YT", l, lev, t))
                        chain(tt(DT[:, t, :], DT[:, t, :], b[:], ALU.subtract))
                        fr(("YT", l, lev, t))
                        v.sem_inc(S("DT_ready"), 1)
                v.wait_ge(S("expA_ready"), l + 1)
                for t in range(NT):
                    chain(tt(h4(kbg[:, t, :]), h4(ktok[:, t, :]), bc3(at(EZ1, t), P)))
                    v.sem_inc(S("kbg_ready"), 1)
                    chain(tt(h4(kend[:, t, :]), h4(ktok[:, t, :]), bc3(at(EZE, t), P)))
                for t in range(NT):
                    b = job(("U", l, t))
                    chain(v.tensor_copy(UU[:, t, :], b[:]))
                    fr(("U", l, t))
                for t in range(NT):
                    b = job(("RA", l, t))
                    chain(v.tensor_reduce(cmaxB[:, 2 * t:2 * t + 2, :].rearrange("p r h -> p h r"),
                                          b[:].rearrange("p (h r i) -> p h r i", h=H, r=2), X, ALU.max))
                    chain(tt(h4(WB[:, t, :]), h4(b[:]), rep(negL[:], H), ALU.add))
                    fr(("RA", l, t))
                    chain(v.tensor_reduce(at(CM, t), h4(WB[:, t, :]), X, ALU.max))
                be = tot2[:, :, 12:16]
                chain(tt(cmaxB[:], cmaxB[:], be, ALU.add))
                for n in range(NCH):
                    chain(tt(spB[:, n, :], mB[:, n, :], be[:, n, :], ALU.add))
                    chain(tt(mB[:, n + 1, :], spB[:, n, :], cmaxB[:, n, :], ALU.max))
                chain(tt(spB[:], spB[:], mB[:, 1:NCH + 1, :], ALU.subtract))
                for r in range(2):
                    rw = slice(64 * r, 64 * r + 64)
                    mv = mB[rw, 0:NCH, :].rearrange("p (t r) h -> p t r h", r=2)
                    mw = mB[rw, 1:NCH + 1, :].rearrange("p (t r) h -> p t r h", r=2)
                    chain(v.tensor_copy(scal[rw, MP[0], :, MP[1]:MP[1] + 4], mv[:, :, r, :]))
                    chain(v.tensor_copy(scal[rw, MN[0], :, MN[1]:MN[1] + 4], mw[:, :, r, :]))
                chain(tt(at(MX), at(MP), at(CM), ALU.max))
                chain(v.tensor_scalar(at(NZ), at(MX), -1.0, None, ALU.mult))
                chain(tt(at(T0), at(MP), at(MX), ALU.subtract))
                chain(stt(at(T1), at(MX), -1.0, sc(CUM, 12, 4), ALU.mult, ALU.subtract))
                chain(tt(at(MN), sc(TOT, 12, 4), at(MN), ALU.subtract))
                chain(tt(at(MN), at(MN), at(AJ), ALU.add))
                chain(v.tensor_scalar(at(BJB), at(AJ), LN_DKB, None, ALU.add))
                v.sem_inc(S("stabB_ready"), 1)
                v.wait_ge(S("expB_ready"), l + 1)
                for i in range(2):
                    rw = slice(64 * i, 64 * i + 64)
                    chain(v.tensor_copy(spc[rw], spB[rw].rearrange("p n (a b) -> p n a b", b=2)[:, :, :, i]))
                chain(v.memset(vB[:, :, :, 128:129], 1.0))
                chain(v.memset(AC[:], 0.0))
                for t in range(NT):
                    b = job(("TKB", l, t))
                    chain(tt(h4(kw[:, t, :], 64), h4(b[:, 0:256], 64), bc3(at(KWS, t), 64)))
                    fr(("TKB", l, t))
                    b = job(("KQB", l, t))
                    v.wait_ge(S("decayB_ready"), l * NT + t + 1)
                    chain(tt(WB[:, t, :], b[:], WB[:, t, :]))
                    fr(("KQB", l, t))
                    b = job(("KQC", l, t))
                    chain(v.copy_predicated(h4(AC[:, t, :]), rep(tri[:].bitcast(U32), H), h4(b[:])))
                    fr(("KQC", l, t))
                    b = job(("TKC", l, t))
                    chain(v.tensor_copy(keC[:, t, :], b[:, 0:256]))
                    fr(("TKC", l, t))
                chain(v.memset(SA[:], 0.0))
                chain(v.memset(SB[:], 0.0))
                chain(v.memset(SC[:], 0.0))
                v.wait_ge(S("wT_ready"), (l + 1) * NT)
                v.wait_ge(S("tok_ready"), (l + 1) * 5 * NT)
                v.sem_inc(S("scan_ready"), 1)
                for name in ("SA_ready", "SB_ready", "SC_ready"):
                    v.sem_inc(S(name), 1)
                for n in range(NCH):
                    t, r = n // 2, n % 2
                    rw = slice(64 * r, 64 * r + 64)
                    b = job(("P1", l, n))
                    chain(tt(UU[rw, t, :], UU[rw, t, :], b[rw, :], ALU.subtract))
                    fr(("P1", l, n))
                    v.sem_inc(S("delta_ready"), 1)
                    b = job(("P2", l, n))
                    chain(tt(h4(oA[rw, t, :]), h4(b[rw, :]), bc3(scal[rw, EZ2[0], t, EZ2[1]:EZ2[1] + 4], P)))
                    fr(("P2", l, n))
                    for p in range(2):
                        b = job((f"QB{p}", l, n))
                        bv = b[rw, 0:258].rearrange("p (a d) -> p a d", d=129)
                        sv = scal[rw, SI[0], t, SI[1] + p:SI[1] + 4:2]
                        chain(tt(h4(nB[rw, t, :])[:, p:4:2, :], bv[:, :, 0:128], bc3(sv, P)))
                        chain(tt(dB[rw, t, p:4:2], bv[:, :, 128], sv))
                        fr((f"QB{p}", l, n))
                    b = job(("KVB", l, n))
                    for p in range(2):
                        chain(stt(SB[:, p, :], SB[:, p, :], spc[:, n, p:p + 1], b[:, p * 129:(p + 1) * 129],
                                  ALU.mult, ALU.add))
                    fr(("KVB", l, n))
                    b = job(("QC", l, n))
                    chain(v.tensor_copy(oC[rw, t, :], b[rw, :]))
                    fr(("QC", l, n))
                    b = job(("KVC", l, n))
                    for p in range(2):
                        chain(stt(SC[:, p, :], SC[:, p, :], aeC[:, p, n:n + 1], b[:, p * P:(p + 1) * P],
                                  ALU.mult, ALU.add))
                    fr(("KVC", l, n))
                    b = job(("P3", l, n))
                    for hh in range(H):
                        hs = slice(hh * P, (hh + 1) * P)
                        chain(stt(SA[:, hs], SA[:, hs], geA[:, n, hh:hh + 1], b[:, hs], ALU.mult, ALU.add))
                    fr(("P3", l, n))
                    if n < NCH - 1:
                        for name in ("SA_ready", "SB_ready", "SC_ready"):
                            v.sem_inc(S(name), 1)
                for t in range(NT):
                    b = job(("OA", l, t))
                    chain(tt(oA[:, t, :], oA[:, t, :], b[:], ALU.add))
                    fr(("OA", l, t))
                    for p in range(2):
                        b = job((f"OB{p}", l, t))
                        bv = b[:, 0:258].rearrange("p (a d) -> p a d", d=129)
                        nv = h4(nB[:, t, :])[:, p:4:2, :]
                        chain(tt(nv, nv, bv[:, :, 0:128], ALU.add))
                        dv = dB[:, t, p:4:2]
                        chain(tt(dv, dv, bv[:, :, 128], ALU.add))
                        fr((f"OB{p}", l, t))
                    b = job(("OC", l, t))
                    chain(tt(oC[:, t, :], oC[:, t, :], b[:], ALU.add))
                    fr(("OC", l, t))
                chain(stt(at(T0), dB[:], -1.0, dB[:], ALU.mult, ALU.max))
                chain(tt(at(T0), at(T0), at(THR), ALU.max))
                chain(v.reciprocal(at(T0), at(T0)))
                for t in range(NT):
                    chain(tt(h4(nB[:, t, :]), h4(nB[:, t, :]), bc3(at(T0, t), P)))
                add_mod(l, 2, 2)
                v.wait_ge(S("ffn_rows_landed"), 32 * (l + 1))
                add_mod(l, 3, 0)
                add_mod(l, 4, 1)
                add_mod(l, 5, 3)
                for g, (o, z) in enumerate(((oA, zA), (nB, oBg), (oC, zC))):
                    for t in range(NT):
                        chain(tt(h4(z[:, t, :]), h4(z[:, t, :]), rep(normr[:, g, :], H)))
                        v.sem_inc(S("o_ready"), 1)
                        v.wait_ge(S("osq_ready"), l * 6 + 2 * g + t + 1)
                        r = st[:, 16 + 8 * t:20 + 8 * t]
                        chain(v.tensor_reduce(r, h4(UU[:, t, :]), X, ALU.add))
                        v.sem_inc(S("oss_ready"), 1)
                        v.wait_ge(S("orstd_ready"), l * 6 + 2 * g + t + 1)
                        chain(tt(h4(o[:, t, :]), h4(o[:, t, :]), bc3(r, P)))
                        chain(tt(o[:, t, :], o[:, t, :], z[:, t, :]))
                        v.sem_inc(S("y_branch"), 1)
                m = 0
                for g in range(3):
                    for hf in range(2):
                        for t in range(NT):
                            v.wait_ge(S("mgate_ready"), l * 12 + m + 1)
                            b = job(("br", l, g, hf, t))
                            dst = merged[:, t, hf * 512:(hf + 1) * 512]
                            if g == 0:
                                chain(tt(dst, b[:], mg_s[m % 2]))
                            else:
                                chain(tt(mg_s[m % 2], b[:], mg_s[m % 2]))
                                chain(tt(dst, dst, mg_s[m % 2], ALU.add))
                            fr(("br", l, g, hf, t))
                            v.sem_inc(S("merged_ready"), 1)
                            m += 1

                def residual(bank_ap, gate, t, hf, tmp):
                    cs = slice(hf * 512, (hf + 1) * 512)
                    chain(tt(tmp, bank_ap, mod[:, gate, cs]))
                    chain(tt(xs[:, t, cs], xs[:, t, cs], tmp, ALU.add))

                for hf in range(2):
                    for t in range(NT):
                        b = job(("wo", l, hf, t))
                        residual(b[:], 2, t, hf, ktok[:, 0, :])
                        fr(("wo", l, hf, t))
                        if hf == 1:
                            v.sem_inc(S("x_ready"), 1)
                v.wait_ge(S("gffn_landed"), 16 * (l + 1))
                normalise(l, 1)
                if l == 0:
                    widths = ffn_widths(D_FF)
                    for f, wd in enumerate(widths):
                        for t in range(NT):
                            key = ("ffn", l, "w3", f, t)
                            b = job(key)
                            v.wait_ge(S("silu_ready"), f * NT + t + 1)
                            if f > 0:
                                v.wait_ge(S("gT_ready"), (f - 1) * NT + t + 1)
                            chain(tt(fg[t][:, 0:wd], fs[t][:, 0:wd], b[:, 0:wd]))
                            fr(key)
                            v.sem_inc(S("g_ready"), 1)
                    v.wait_ge(S("down_done"), NT * len(widths))
                    for t in range(NT):
                        for hf in range(2):
                            residual(facc_ps[2 * t + hf][:], 3, t, hf, Dm[:, 0, :])
                        v.sem_inc(S("x_ready"), 1)
                else:
                    b = job(("router", l))
                    lg = LT[:, 0, 0:16].rearrange("p (t n) -> p t n", n=8)
                    chain(tt(lg, b[:, 0:16].rearrange("p (t n) -> p t n", n=8), rep(brt[:], NT), ALU.add))
                    fr(("router", l))
                    cmp = LT[:, 0, 64:128].rearrange("p (a b) -> p a b", b=8)
                    eq = LT[:, 0, 128:192].rearrange("p (a b) -> p a b", b=8)
                    lower = LT[:, 0, 192:256].rearrange("p (a b) -> p a b", b=8)
                    chain(v.memset(lower, 0.0))
                    for i in range(1, 8):
                        chain(v.memset(lower[:, i, 0:i], 1.0))
                    sel = LT[:, 0, 256:272].rearrange("p (t n) -> p t n", n=8)
                    top = st[:, 32:34]
                    for t in range(NT):
                        mine = bc3(lg[:, t, :], 8)
                        other = rep(lg[:, t, :], 8)
                        chain(tt(cmp, other, mine, ALU.is_gt))
                        chain(tt(eq, other, mine, ALU.is_equal))
                        chain(tt(eq, eq, lower))
                        chain(tt(cmp, cmp, eq, ALU.add))
                        chain(v.tensor_reduce(sel[:, t, :], cmp, X, ALU.add))
                        chain(v.tensor_scalar(sel[:, t, :], sel[:, t, :], 2.0, None, ALU.is_lt))
                        chain(v.tensor_reduce(top[:, t:t + 1], lg[:, t, :], X, ALU.max))
                        chain(v.tensor_scalar(comb[:, t, :], lg[:, t, :], top[:, t:t + 1], None, ALU.subtract))
                    v.sem_inc(S("route_in"), 1)
                    v.wait_ge(S("route_exp"), 1)
                    for t in range(NT):
                        chain(tt(comb[:, t, :], comb[:, t, :], sel[:, t, :]))
                        chain(v.tensor_reduce(top[:, t:t + 1], comb[:, t, :], X, ALU.add))
                        chain(v.reciprocal(top[:, t:t + 1], top[:, t:t + 1]))
                        chain(v.tensor_scalar(comb[:, t, :], comb[:, t, :], top[:, t:t + 1], None, ALU.mult))
                    chain(v.memset(facc, 0.0))
            NF = D_FFE // W512
            jper = len(moe_jobs)
            v.sem_inc(S("facc_free"), NT)
            for i in range(len(order), MOE_BASE):
                v.wait_ge(S("mm_done"), i + 1)
                v.sem_inc(S(f"bank_free{i % NBANK}"), 1)
            v.sem_inc(S("eg_ready"), NT)
            with v.Fori(0, N_EXP) as e:
                for f in range(NF):
                    for t in range(NT):
                        i = MJOB[("w3", f, t)]
                        v.wait_ge(S("mm_done"), e * jper + (MOE_BASE + i + 1))
                        v.wait_ge(S("esilu_ready"), e * (NT * NF) + (f * NT + t + 1))
                        v.wait_ge(S("egT_ready"), e * (NT * NF) + (f * NT + t + 1))
                        v.tensor_tensor(fg[t], fs[t], banks[i % NBANK][:], ALU.mult).then_inc(S("eg_ready"), 1)
                        v.wait_ge(S("eg_ready"), e * (NT * NF) + (NT + f * NT + t + 1))
                        v.sem_inc(S(f"bank_free{i % NBANK}"), 1)
                for i, key in enumerate(moe_jobs):
                    if key == ("pad",):
                        v.wait_ge(S("mm_done"), e * jper + (MOE_BASE + i + 1))
                        v.sem_inc(S(f"bank_free{i % NBANK}"), 1)
                v.wait_ge(S("edown_done"), e * (NT * NF) + (NT + NT * NF))
                for t in range(NT):
                    for hf in range(2):
                        dst = facc[:, t, hf * 512:(hf + 1) * 512]
                        v.scalar_tensor_tensor(dst, facc_ps[2 * t + hf][:], comb[:, t, bass.ds(e, 1)], dst,
                                               ALU.mult, ALU.add).then_inc(S("facc_done"), 1)
                    v.wait_ge(S("facc_done"), e * (2 * NT) + (2 * t + 2))
                    v.sem_inc(S("facc_free"), 1)
            for t in range(NT):
                chain(tt(facc[:, t, :], facc[:, t, :], mod[:, 3, :]))
                chain(tt(xs[:, t, :], xs[:, t, :], facc[:, t, :], ALU.add))
                v.sem_inc(S("x_ready"), 1)
            v.wait_ge(S("gfinal_landed"), 16)
            for t in range(NT):
                v.wait_ge(S("rstd_ready"), 2 * DEPTH * NT + t + 1)
                chain(stt(xs[:, t, :], xs[:, t, :], st[:, 4 * t + 3:4 * t + 4], grow, ALU.mult, ALU.mult))
                v.sem_inc(S("y_ready"), 1)


_INS = ["x", "c", "w_ada", "b_ada", "g_mix", "g_ffn", "g_final", "w_in", "conv_a", "a_log", "dt_bias", "norm_a",
        "conv_b", "b_i", "b_f", "norm_b", "w_gla2", "b_gla", "norm_c", "w_br", "w_mg", "b_mg", "w_o",
        "w1_d", "w3_d", "w2_d", "w_router", "b_router", "w1_e", "w3_e", "w2_e"]


def kernel(**inputs):
    import numpy as _np
    import concourse.bacc as _bacc
    from concourse import mybir as _mybir
    from concourse.bass_utils import run_bass_kernel_spmd as _run

    nc = _bacc.Bacc("TRN2", target_bir_lowering=False, num_devices=1)
    arrays, args = {}, []
    for name in _INS:
        a = _np.ascontiguousarray(inputs[name])
        arrays[f"in_{name}_dram"] = a
        args.append(nc.dram_tensor(f"in_{name}_dram", a.shape, _mybir.dt.from_np(a.dtype), kind="ExternalInput").ap())
    args.append(nc.dram_tensor("out_0_dram", (1, SEQ, D), F32, kind="ExternalOutput").ap())
    hybrid_kernel(nc, *args)
    r = _run(nc, [arrays], core_ids=[0])
    return r.results[0]["out_0_dram"]
```

```python
from contextlib import ExitStack

import numpy as np

import concourse.bass as bass
from concourse import mybir

F32 = mybir.dt.float32
U32 = mybir.dt.uint32
ACT = mybir.ActivationFunctionType
ALU = mybir.AluOpType
X = mybir.AxisListType.X

P = 128
D = 1024
KD = D // P
SEQ = 256
NT = SEQ // P
L = 64
NCH = SEQ // L
H = 4
DEPTH = 2
W512 = 512
NEG = -1.0e30
EPS = 1e-6
D_FF = 2816
N_EXP = 8
D_FFE = 3584
RING = 7
NBANK = 4

QA, ZA = 0, 1536
AB = 2048
QB, VB, OB = 2056, 2568, 3080
IF = 3592
QC, VC, ZC = 3600, 4112, 4624
GC = 5136
LN_DKA = float(-0.5 * np.log(128.0))
LN_DKB = float(-0.5 * np.log(64.0))


def slab_plan(l):
    plan = []
    for piece in (0, 1):
        plan += [("ada", l, k, piece * D + hf * W512) for hf in range(2) for k in range(2)]
    for col in (QA, QA + 512, QA + 1024, QB, QC, ZA, VB, OB, VC, ZC):
        plan += [("in", l, k, col) for k in range(2)]
    for piece in (2, 3, 4, 5):
        plan += [("ada", l, k, piece * D + hf * W512) for hf in range(2) for k in range(2)]
    for g in range(3):
        for hf in range(2):
            plan += [("mg", l, g, k, hf) for k in range(2)] + [("br", l, g, hf)]
    for hf in range(2):
        plan += [("wo", l, k, hf) for k in range(2)]
    return plan


def ffn_widths(dff):
    return [W512] * (dff // W512) + ([dff % W512] if dff % W512 else [])


def job_plan(l):
    j = [("cols", l)]
    j += [("mod", l, piece, hf) for piece in (0, 1) for hf in range(2)]
    j += [("hT", l, 0, t, q) for t in range(NT) for q in range(2)]
    j += [("small", l), ("gT", l), ("cum", l), ("la", l)]
    j += [("qkvA", l, i) for i in range(6)] + [("qkB", l, i) for i in range(2)] + [("qkC", l, i) for i in range(2)]
    j += [(n, l, t) for n in ("zA", "vB", "oB", "vC", "zC") for t in range(NT)]
    j += [(n, l, t) for t in range(NT) for n in ("TQ", "TK", "TV")]
    for t in range(NT):
        j += [("R1", l, t), ("KK", l, t), ("R2", l, t), ("KQ", l, t)]
    j += [("X", l, 0, t) for t in range(NT)]
    for lev in range(1, 6):
        for t in range(NT):
            j += [("X", l, lev, t)]
        for t in range(NT):
            j += ([("Y", l, lev, t)] if lev < 5 else []) + [("YT", l, lev, t)]
    for t in range(NT):
        j += [("U", l, t), ("WT", l, t)]
    j += [("RA", l, t) for t in range(NT)]
    for t in range(NT):
        j += [("TKB", l, t), ("RB", l, t), ("KQB", l, t), ("KQC", l, t), ("TKC", l, t)]
    for n in range(NCH):
        j += [("P1", l, n), ("P2", l, n), ("QB0", l, n), ("QB1", l, n), ("KVB", l, n), ("QC", l, n), ("KVC", l, n),
              ("P3", l, n)]
    for t in range(NT):
        j += [("OA", l, t), ("OB0", l, t), ("OB1", l, t), ("OC", l, t)]
    j += [("mod", l, piece, hf) for piece in (2, 3, 4, 5) for hf in range(2)]
    j += [("yT", l, g, t) for g in range(3) for t in range(NT)]
    for g in range(3):
        for hf in range(2):
            j += [(n, l, g, hf, t) for t in range(NT) for n in ("mg", "br")]
    j += [("mT", l, t, q) for t in range(NT) for q in range(2)]
    j += [("wo", l, hf, t) for hf in range(2) for t in range(NT)]
    j += [("hT", l, 1, t, q) for t in range(NT) for q in range(2)]
    if l % 2 == 1:
        j += [("router", l), ("rank", l)]
    return j


def ffn_jobs(widths):
    j = []
    for f in range(len(widths) + 1):
        if f < len(widths):
            j += [("w1", f, t) for t in range(NT)]
        if f > 0:
            j += [("gT", f - 1, t) for t in range(NT)]
        if f < len(widths):
            j += [("w3", f, t) for t in range(NT)]
    return j


NF = D_FFE // W512
CAP = P
BLOCKS = SEQ // CAP
EXPERT_JOBS = [("xg", 0), ("xg", 1)] + [("sc", t, hf) for t in range(NT) for hf in range(2)] + [("pwt",)]
for _f in range(NF + 1):
    if _f < NF:
        EXPERT_JOBS.append(("w1", _f))
    if _f > 0:
        EXPERT_JOBS.append(("gT", _f - 1))
    if _f < NF:
        EXPERT_JOBS.append(("w3", _f))
MJOB = {k: i for i, k in enumerate(EXPERT_JOBS)}
JPER = len(EXPERT_JOBS)
JBLOCK = N_EXP * JPER + 2 * NT
SPER = 6 * NF
MRING = 14


def hybrid_kernel(nc, x, c, w_ada, b_ada, g_mix, g_ffn, g_final, w_in, conv_a, a_log, dt_bias, norm_a,
                  conv_b, b_i, b_f, norm_b, w_gla2, b_gla, norm_c, w_br, w_mg, b_mg, w_o,
                  w1_d, w3_d, w2_d, w_router, b_router, w1_e, w3_e, w2_e, out):
    with ExitStack() as ctx:
        sems = {}

        def S(name):
            if name not in sems:
                sems[name] = ctx.enter_context(nc.semaphore(name))
            return sems[name]

        def sb(name, shape, dt=F32):
            return ctx.enter_context(nc.sbuf_tensor(name, shape, dt))

        ring = sb("ring", [P, RING, 4, W512])
        xs = sb("xs", [P, NT, D])
        mod = sb("mod", [P, 4, D])
        hT = sb("hT", [P, KD, SEQ])
        ident = sb("ident", [P, P])
        tri = sb("tri", [P, P])
        same = sb("same", [P, P])
        half = sb("half", [P, 2, P])
        negI = sb("negI", [P, P])
        negS = sb("negS", [P, P])
        negL = sb("negL", [P, P])
        lev_m = sb("lev_m", [P, 6, P])
        ones = sb("ones", [P, P])
        rst = sb("rst", [P, SEQ])
        cst = sb("cst", [P, 8])
        crow = sb("crow", [8, P])
        cact = sb("cact", [P, KD])
        bglar = sb("bglar", [2, P])
        cols = sb("cols", [P, 66])
        wsm = sb("wsm", [P, KD, 32])
        wgla = sb("wgla", [16, 256])
        bias16 = sb("bias16", [P, 16])
        sgn16 = sb("sgn16", [P, 16])
        cf16 = sb("cf16", [P, 16])
        normr = sb("normr", [P, 3, P])
        wrt = sb("wrt", [P, KD, 8])
        brt = sb("brt", [P, 8])
        st = sb("st", [P, 64])
        comb = sb("comb", [P, NT, 8])
        scal = sb("scal", [P, 12, NT, 16])
        WORK = 25650
        work = sb("work", [P, WORK])
        used = [0]

        def wk(n, *shape):
            a = used[0]
            used[0] += n
            assert used[0] <= WORK, used
            v = work[:, a:a + n]
            if len(shape) == 2:
                return v.rearrange("p (a b) -> p a b", b=shape[1])
            if len(shape) == 3:
                return v.rearrange("p (a b c) -> p a b c", b=shape[1], c=shape[2])
            return v

        fA = wk(12 * SEQ, 12, SEQ)
        fB = wk(4 * SEQ, 4, SEQ)
        fC = wk(4 * SEQ, 4, SEQ)
        zA = wk(NT * 512, NT, 512)
        oBg = wk(NT * 512, NT, 512)
        zC = wk(NT * 512, NT, 512)
        vB = wk(NT * 516, NT, 4, 129)
        vC = wk(NT * 512, NT, 512)
        lt_at = used[0]
        LT = wk(NT * 512, NT, 512)
        AT = wk(NT * 512, NT, 512)
        WB = wk(NT * 512, NT, 512)
        AC = wk(NT * 512, NT, 512)
        Dm = wk(NT * 512, NT, 512)
        DT = wk(NT * 512, NT, 512)
        lb_at = used[0]
        LB = wk(NT * 512, NT, 512)
        XB = wk(NT * 512, NT, 512)
        ktok = wk(NT * 512, NT, 512)
        vb = wk(NT * 512, NT, 512)
        uu_at = used[0]
        UU = wk(NT * 512, NT, 512)
        wT = wk(NT * 512, NT, 512)
        SA = wk(512)
        SB = wk(2 * 129, 2, 129)
        SC = wk(2 * 128, 2, 128)
        kw = wk(NT * 256, NT, 256)
        keC = wk(NT * 256, NT, 256)
        qg = wk(2 * SEQ, 2, SEQ)
        keT = wk(2 * SEQ, 2, SEQ)
        convr = work[0:4, lt_at:lt_at + 2048]
        kbg, kend = XB, LB
        oA, nB, oC = Dm, DT, LT
        half_t = lambda b, t: b[:, t, :].rearrange("p (f i) -> p f i", f=2)
        bc, uc, tc1, tc2 = half_t(Dm, 0), half_t(Dm, 1), half_t(DT, 0), half_t(DT, 1)
        gTs = LB[:, 0, 0:SEQ]
        grow = zA.rearrange("p t n -> p (t n)")
        bmg = oBg.rearrange("p t n -> p (t n)")
        sq = [XB[:, 0, :], XB[:, 1, :]]
        h = work[:, 0:NT * D].rearrange("p (t d) -> p t d", t=NT)
        yTv = [b.rearrange("p t n -> p (t n)").rearrange("p (f i) -> p f i", i=SEQ) for b in (AT, WB, AC)]
        mg_s = [XB[:, 0, :], XB[:, 1, :]]
        merged = work[:, 12 * SEQ:12 * SEQ + NT * D].rearrange("p (t d) -> p t d", t=NT)
        mT = work[:, uu_at:uu_at + NT * D].rearrange("p (k i) -> p k i", i=SEQ)
        fs = [ktok[:, i, :] for i in range(2)]
        fg = [vb[:, i, :] for i in range(2)]
        fgT = [LB[:, i, :].rearrange("p (f i) -> p f i", f=4) for i in range(2)]
        h_words = NT * D
        extra = work[:, h_words:h_words + (MRING - RING) * 2048].rearrange("p (s k n) -> p s k n", s=MRING - RING, k=4)
        assert h_words + (MRING - RING) * 2048 <= lb_at
        facc = work[:, uu_at:uu_at + NT * D].rearrange("p (t d) -> p t d", t=NT)
        y = XB.rearrange("p t n -> p (t n)")
        xgT = hT.rearrange("p k i -> p (k i)")[:, 0:D].rearrange("p (k i) -> p k i", i=P)
        pick = kw[:, 0, :].rearrange("p (t c) -> p t c", t=NT)
        pickw = kw[:, 1, :].rearrange("p (t c) -> p t c", t=NT)
        pwT = keC[:, 0, :]
        slot_no = [keT[:, 0, 0:P], keT[:, 0, P:2 * P]]
        route = XB.rearrange("p t n -> p (t n)")

        RAW, AB_, EX, LG, SP, CUM, TOT = 0, 1, 2, 3, 4, 5, 6
        Z1, Z2, BJ, ZE, AJ = (7, 0), (7, 4), (7, 8), (7, 12), (8, 0)

        def sc(kind, a=0, n=16):
            return scal[:, kind, :, a:a + n]

        def at(where, t=None, n=4):
            k, a = where
            return scal[:, k, :, a:a + n] if t is None else scal[:, k, t, a:a + n]

        CM, MX, MP, MN = (8, 4), (8, 8), (9, 0), (9, 4)
        EZ1, EZ2, EZE, BETA = (10, 0), (10, 4), (10, 8), (9, 8)
        SI, THR, KWS, NZ = (11, 0), (11, 4), (11, 8), (11, 12)
        BJB, T0, T1 = (10, 12), (9, 12), (8, 12)
        tot2 = sb("tot2", [P, NCH, 16])
        geA = sb("geA", [P, NCH, 4])
        cmaxB = sb("cmaxB", [P, NCH, 4])
        mB = sb("mB", [P, NCH + 1, 4])
        spB = sb("spB", [P, NCH, 4])
        spc = sb("spc", [P, NCH, 2])
        aeC = sb("aeC", [P, 2, NCH])
        dB = sb("dB", [P, NT, 4])
        sel = sb("sel", [P, NT, 8])
        rank = sb("rank", [P, NT, 8])
        before = sb("before", [P, P])
        over = sb("over", [P, 1], mybir.dt.int32)
        ssA = sb("ssA", [P, NT, 8])

        banks = [ctx.enter_context(nc.psum_tensor(f"bank{i}", [P, 512], F32)) for i in range(8)]
        facc_ps = banks[4:8]

        order = []
        for l in range(DEPTH):
            order += job_plan(l)
            if l == 0:
                order += [("ffn", l) + k for k in ffn_jobs(ffn_widths(D_FF))]
        JOB = {k: i for i, k in enumerate(order)}
        MOE_BASE = len(order)
        while MOE_BASE % NBANK:
            MOE_BASE += 1
        PAD0 = MOE_BASE - len(order)
        assert JPER % NBANK == 0 and JBLOCK % NBANK == 0 and SPER % MRING == 0

        def bc3(ap, n):
            return ap.rearrange("p (a o) -> p a o", o=1).broadcast_to([ap.shape[0], ap.shape[1], n])

        def rep(ap, n):
            return ap.rearrange("p (o w) -> p o w", o=1).broadcast_to([ap.shape[0], n, ap.shape[1]])

        def h4(ap, w=128):
            return ap.rearrange("p (h d) -> p h d", d=w)

        def mslot(i):
            return ring[:, i] if i < RING else extra[:, i - RING]

        block = ctx.enter_context(nc.Block())

        @block.sync
        def _(sp):
            sp.dma_start(xs[:], x[0].rearrange("(t p) d -> p t d", p=P)).then_inc(S("x_landed"), 16)
            n = 0

            def slab(src, width=W512, kt=4):
                nonlocal n
                if n >= RING:
                    sp.wait_ge(S("slab_used"), n - RING + 1)
                sp.dma_start(ring[:, n % RING, 0:kt, 0:width],
                             src.rearrange("(k p) n -> p k n", p=P)).then_inc(S(f"slab{n % RING}"), 16)
                n += 1

            def rows4(w, k, col, width=W512):
                return w[k * 512:(k + 1) * 512, col:col + width]

            def down_slabs(f):
                wd = ffn_widths(D_FF)[f]
                for hf in range(2):
                    slab(w2_d[0, f * W512:f * W512 + wd, hf * W512:(hf + 1) * W512], kt=wd // P)

            for l in range(DEPTH):
                for key in slab_plan(l):
                    if key[0] == "ada":
                        slab(rows4(w_ada[l], key[2], key[3]))
                    elif key[0] == "in":
                        slab(rows4(w_in[l], key[2], key[3]))
                    elif key[0] == "mg":
                        slab(rows4(w_mg[l, key[2]], key[3], key[4] * W512))
                    elif key[0] == "br":
                        slab(rows4(w_br[l, key[2]], 0, key[3] * W512))
                    elif key[0] == "wo":
                        slab(rows4(w_o[l], key[2], key[3] * W512))
                if l == 0:
                    for f, wd in enumerate(ffn_widths(D_FF)):
                        for w in (w1_d, w3_d):
                            for k in range(2):
                                slab(rows4(w[0], k, f * W512, wd), wd)
                        if f:
                            down_slabs(f - 1)
                    down_slabs(f)
            total = n
            def experts(blk):
                with sp.Fori(0, N_EXP) as e:
                    m = [0]

                    def mslab(w, r0, c0):
                        i = m[0]
                        m[0] += 1
                        sp.wait_ge(S("mslab_used"), e * SPER + (blk * N_EXP * SPER + i + 1))
                        src = w[0, bass.ds(e, 1), r0:r0 + 512, c0:c0 + W512].rearrange("o (k p) n -> p (o k) n", p=P)
                        sp.dma_start(mslot(i % MRING), src).then_inc(S(f"mslab{i % MRING}"), 16)

                    for f in range(NF + 1):
                        if f < NF:
                            for w in (w1_e, w3_e):
                                for k in range(2):
                                    mslab(w, k * 512, f * W512)
                        if f > 0:
                            for hf in range(2):
                                mslab(w2_e, (f - 1) * W512, hf * W512)

            sp.wait_ge(S("slab_used"), total)
            sp.wait_ge(S("h_ready"), 2 * DEPTH * NT)
            experts(0)
            sp.wait_ge(S("route_ready"), 1)
            with sp.If(sp.value_load(over[0:1, 0:1], min_val=0, max_val=1) > 0):
                experts(1)
            sp.wait_ge(S("y_ready"), 2)
            sp.dma_start(out[0].rearrange("(t p) d -> p t d", p=P), xs[:]).then_inc(S("out_stored"), 16)
            sp.wait_ge(S("out_stored"), 16)

        @block.gpsimd
        def _(pool):
            def bcast(dst, src_row):
                return pool.dma_start(dst, src_row)

            pool.dma_start(crow[:], c[0].rearrange("(k p) -> k p", p=P)).then_inc(S("c_landed"), 16)
            k = [0]

            def chain(ins):
                k[0] += 1
                ins.then_inc(S("pool_chain"), 1)
                pool.wait_ge(S("pool_chain"), k[0])

            chain(pool.memset(ident[:], 0.0))
            chain(pool.affine_select(out=ident[:], in_=ident[:], compare_op=ALU.not_equal, fill=1.0, base=0,
                                     pattern=[[-1, P]], channel_multiplier=1))
            chain(pool.memset(ones[:], 1.0))
            chain(pool.memset(same[:], 1.0))
            sv = same[:].rearrange("p (q w) -> p q w", w=L)
            chain(pool.affine_select(out=sv, in_=sv, compare_op=ALU.is_ge, fill=0.0, base=0,
                                     pattern=[[-L, 2], [0, L]], channel_multiplier=1))
            chain(pool.affine_select(out=sv, in_=sv, compare_op=ALU.is_ge, fill=0.0, base=L - 1,
                                     pattern=[[L, 2], [0, L]], channel_multiplier=-1))
            chain(pool.affine_select(out=tri[:], in_=same[:], compare_op=ALU.is_ge, fill=0.0, base=0,
                                     pattern=[[1, P]], channel_multiplier=-1))
            chain(pool.affine_select(out=negL[:], in_=same[:], compare_op=ALU.is_ge, fill=0.0, base=0,
                                     pattern=[[-1, P]], channel_multiplier=1))
            chain(pool.affine_select(out=negS[:], in_=same[:], compare_op=ALU.is_ge, fill=0.0, base=-1,
                                     pattern=[[1, P]], channel_multiplier=-1))
            chain(pool.tensor_scalar(negI[:], tri[:], -1.0, -NEG, ALU.add, ALU.mult))
            chain(pool.tensor_scalar(negS[:], negS[:], -1.0, -NEG, ALU.add, ALU.mult))
            chain(pool.tensor_scalar(negL[:], negL[:], -1.0, -NEG, ALU.add, ALU.mult))
            chain(pool.memset(half[:], 1.0))
            chain(pool.affine_select(out=half[:], in_=half[:], compare_op=ALU.is_ge, fill=0.0, base=0,
                                     pattern=[[-L, 2], [0, P]], channel_multiplier=1))
            chain(pool.affine_select(out=half[:], in_=half[:], compare_op=ALU.is_ge, fill=0.0, base=L - 1,
                                     pattern=[[L, 2], [0, P]], channel_multiplier=-1))
            chain(pool.memset(lev_m[:], 0.0))
            for lev in range(6):
                b = 1 << lev
                q = P // (2 * b)
                v = lev_m[:, lev, :].rearrange("p (q w) -> p q w", w=2 * b)[:, :, b:2 * b]
                chain(pool.memset(v, 1.0))
                chain(pool.affine_select(out=v, in_=v, compare_op=ALU.is_ge, fill=0.0, base=0,
                                         pattern=[[-2 * b, q], [0, b]], channel_multiplier=1))
                chain(pool.affine_select(out=v, in_=v, compare_op=ALU.is_ge, fill=0.0, base=b - 1,
                                         pattern=[[2 * b, q], [0, b]], channel_multiplier=-1))
            chain(pool.memset(rst[:], 1.0))
            chain(pool.memset(rst[:].rearrange("p (q w) -> p q w", w=L)[:, :, 0:1], 0.0))
            for i, v in enumerate((EPS, 1.0, LN_DKB, 0.0)):
                chain(pool.memset(cst[:, i:i + 1], v))
            chain(pool.memset(sgn16[:], 1.0))
            chain(pool.memset(sgn16[:, 4:8], -1.0))
            chain(pool.memset(sgn16[:, 12:16], -1.0))
            chain(pool.memset(cf16[:], -1.0))
            chain(pool.memset(bias16[:], 0.0))
            chain(pool.memset(mB[:], 0.0))
            chain(pool.memset(st[:], 0.0))
            chain(pool.memset(before[:], 1.0))
            chain(pool.affine_select(out=before[:], in_=before[:], compare_op=ALU.is_ge, fill=0.0, base=-1,
                                     pattern=[[1, P]], channel_multiplier=-1))
            pool.memset(cst[:, 4:8], 0.0).then_inc(S("consts_ready"), 1)

            for l in range(DEPTH):
                if l:
                    pool.wait_ge(S("x_ready"), 2 * NT)
                def small(dst, src):
                    pool.dma_start(dst, src).then_inc(S("small_landed"), 16)
                small(grow, g_mix[l:l + 1, :].broadcast_to([P, D]))
                for s in range(2):
                    small(mod[:, s, :], b_ada[l:l + 1, s * D:(s + 1) * D].broadcast_to([P, D]))
                small(mod[:, 2, :], b_ada[l:l + 1, 2 * D:3 * D].broadcast_to([P, D]))
                small(mod[:, 3, :], b_ada[l:l + 1, 5 * D:6 * D].broadcast_to([P, D]))
                small(convr[:, 0:1536], conv_a[l])
                small(convr[:, 1536:2048], conv_b[l])
                small(bglar[:], b_gla[l].rearrange("(k p) -> k p", p=P))
                win = w_in[l].rearrange("(k p) n -> p k n", p=P)
                small(wsm[:, :, 0:8], win[:, :, AB:AB + 8])
                small(wsm[:, :, 8:16], win[:, :, IF:IF + 8])
                small(wsm[:, :, 16:32], win[:, :, GC:GC + 16])
                small(wgla[:], w_gla2[l])
                small(bias16[:, 0:4], dt_bias[l:l + 1, :].broadcast_to([P, 4]))
                small(bias16[:, 8:12], b_i[l:l + 1, :].broadcast_to([P, 4]))
                small(bias16[:, 12:16], b_f[l:l + 1, :].broadcast_to([P, 4]))
                small(cf16[:, 0:4], a_log[l:l + 1, :].broadcast_to([P, 4]))
                small(normr[:, 0, :], norm_a[l:l + 1, :].broadcast_to([P, P]))
                small(normr[:, 1, :], norm_b[l:l + 1, :].broadcast_to([P, P]))
                small(normr[:, 2, :], norm_c[l:l + 1, :].broadcast_to([P, P]))
                small(wrt[:], w_router[0].rearrange("(k p) n -> p k n", p=P))
                small(brt[:], b_router[0:1, :].broadcast_to([P, 8]))
                pool.wait_ge(S("h_ready"), (2 * l + 1) * NT)
                for s in range(2):
                    pool.dma_start(mod[:, s, :], b_ada[l:l + 1, (3 + s) * D:(4 + s) * D].broadcast_to([P, D])) \
                        .then_inc(S("ffn_rows_landed"), 16)
                pool.wait_ge(S("y_branch"), l * 6 + 2)
                pool.dma_start(grow, g_ffn[l:l + 1, :].broadcast_to([P, D])).then_inc(S("gffn_landed"), 16)
                pool.wait_ge(S("y_branch"), l * 6 + 4)
                for g in range(3):
                    pool.dma_start(bmg[32 * g:32 * g + 1, :], b_mg[l, g:g + 1, :]).then_inc(S("bmg_landed"), 16)
            pool.wait_ge(S("h_ready"), 2 * DEPTH * NT)
            for b in range(BLOCKS):
                pool.iota(slot_no[b], pattern=[[1, P]], base=b * CAP, channel_multiplier=0,
                          allow_small_or_imprecise_dtypes=True).then_inc(S("slots_ready"), 1)
            pool.dma_start(mod[:, 0, :], g_final.rearrange("(o d) -> o d", o=1).broadcast_to([P, D])) \
                .then_inc(S("gfinal_landed"), 16)
        SMALLS = 21 * 16

        @block.tensor
        def _(pe):
            nj = [0]
            ns = [0]
            lows = [0]

            def begin(key):
                i = nj[0]
                assert order[i] == key, (order[i], key)
                if i >= NBANK:
                    pe.wait_ge(S(f"bank_free{i % NBANK}"), i // NBANK)
                return banks[i % NBANK]

            def end(ins):
                nj[0] += 1
                ins.then_inc(S("mm_done"), 1)

            def slab_at(i):
                pe.wait_ge(S(f"slab{i % RING}"), 16 * (i // RING + 1))
                return ring[:, i % RING]

            def take():
                ns[0] += 1
                return slab_at(ns[0] - 1)

            def mm(o, a, b, start, stop, **kw):
                return pe.matmul(o, a, b, start=start, stop=stop, skip_group_check=True, **kw)

            def T(o, a):
                n = a.shape[0]
                return pe.transpose(o, a, ident[0:n, 0:n])

            def project_cols(key, slabs, fts, release):
                o = begin(key)
                for i, ft in enumerate(fts):
                    for k in range(KD):
                        ins = mm(o[:, i * SEQ:(i + 1) * SEQ], slabs[k // 4][:, k % 4, ft * P:(ft + 1) * P], hT[:, k, :],
                                 k == 0, k == KD - 1)
                end(ins)

            def over_d(o, act_t, slabs, wd=W512):
                for k in range(KD):
                    ins = mm(o[:, 0:wd], act_t[:, k, :], slabs[k // 4][:, k % 4, 0:wd], k == 0, k == KD - 1)
                return ins

            def mods(l, pieces):
                for piece in pieces:
                    for hf in range(2):
                        s = [take(), take()]
                        o = begin(("mod", l, piece, hf))
                        for k in range(KD):
                            ins = mm(o[:], cact[:, k:k + 1].broadcast_to([P, P]), s[k // 4][:, k % 4, :],
                                     k == 0, k == KD - 1)
                        end(ins)
                        release(2)

            pending = []

            def release(n):
                pending.append((nj[0], n))
                if len(pending) > 1:
                    flush()

            def flush():
                if not pending:
                    return
                upto, n = pending.pop(0)
                pe.wait_ge(S("mm_done"), upto)
                pe.sem_inc(S("slab_used"), n)

            def transposes(key, src_of, n=4):
                o = begin(key)
                for i in range(n):
                    ins = T(o[:, i * P:(i + 1) * P], src_of(i))
                end(ins)

            pe.wait_ge(S("consts_ready"), 1)
            pe.wait_ge(S("c_landed"), 16)
            pe.transpose(banks[7][:, 0:8], crow[:], ident[0:8, 0:8]).then_inc(S("c_turned"), 1)
            pe.wait_ge(S("cact_ready"), 1)
            for l in range(DEPTH):
                pe.wait_ge(S("small_landed"), SMALLS * (l + 1))
                o = begin(("cols", l))
                for i in range(16):
                    T(o[:, 4 * i:4 * i + 4], convr[:, i * P:(i + 1) * P])
                end(T(o[:, 64:66], bglar[:]))
                mods(l, (0, 1))

                def make_hT(which):
                    pe.wait_ge(S("h_ready"), (2 * l + which + 1) * NT)
                    for t in range(NT):
                        for q in range(2):
                            transposes(("hT", l, which, t, q), lambda i: h[:, t, (4 * q + i) * P:(4 * q + i + 1) * P])
                    pe.wait_ge(S("hT_ready"), (2 * l + which + 1) * 4)

                make_hT(0)
                o = begin(("small", l))
                for t in range(NT):
                    for k in range(KD):
                        ins = mm(o[:, t * 16:(t + 1) * 16], hT[:, k, t * P:(t + 1) * P], wsm[:, k, 0:16],
                                 k == 0, k == KD - 1)
                end(ins)
                o = begin(("gT", l))
                for k in range(KD):
                    ins = mm(o[0:16, 0:SEQ], wsm[:, k, 16:32], hT[:, k, :], k == 0, k == KD - 1)
                end(ins)
                pe.wait_ge(S("decay_ready"), l + 1)
                o = begin(("cum", l))
                for t in range(NT):
                    for i, m in enumerate((tri[:], same[:], half[:, 0, :], half[:, 1, :])):
                        ins = mm(o[:, (4 * t + i) * 16:(4 * t + i + 1) * 16], m, scal[:, SP, t, :], True, True)
                end(ins)
                pe.wait_ge(S("gTs_ready"), l + 1)
                o = begin(("la", l))
                for f in range(2):
                    ins = mm(o[:, f * SEQ:(f + 1) * SEQ], wgla[:, f * P:(f + 1) * P], gTs[0:16, :], True, True)
                end(ins)
                for name, n in (("qkvA", 3), ("qkB", 1), ("qkC", 1)):
                    for i in range(n):
                        s = [take(), take()]
                        project_cols((name, l, 2 * i), s, (0, 1), 0)
                        project_cols((name, l, 2 * i + 1), s, (2, 3), 0)
                        release(2)
                for name in ("zA", "vB", "oB", "vC", "zC"):
                    s = [take(), take()]
                    for t in range(NT):
                        o = begin((name, l, t))
                        end(over_d(o, hT[:, :, t * P:(t + 1) * P], s))
                    release(2)
                pe.wait_ge(S("fA_ready"), (l + 1) * 12)
                for t in range(NT):
                    for i, name in enumerate(("TQ", "TK", "TV")):
                        transposes((name, l, t), lambda j: fA[:, 4 * i + j, t * P:(t + 1) * P])

                def row_matrix(key, where, mask, t):
                    o = begin(key)
                    if mask is not None:
                        for hh in range(H):
                            mm(o[:, hh * P:(hh + 1) * P], ident[:], mask[:], hh == 0, False)
                    for hh in range(H):
                        ins = mm(o[:, hh * P:(hh + 1) * P],
                                 scal[:, where[0], t, where[1] + hh:where[1] + hh + 1].broadcast_to([P, P]),
                                 ident[:], mask is None and hh == 0, hh == H - 1)
                    end(ins)

                def scores(key, kk, qq):
                    o = begin(key)
                    for hh in range(H):
                        ins = mm(o[:, hh * P:(hh + 1) * P], kk(hh), qq(hh), hh == 0, hh == H - 1)
                    end(ins)

                def by_halves(key, lhs, rhs, rw=slice(0, P)):
                    o = begin(key)
                    for i in range(2):
                        for hh in (i, i + 2):
                            ins = mm(o[rw, hh * P:(hh + 1) * P], lhs(hh), rhs(hh), True, True)
                        if i == 0:
                            ins.then_inc(S("low_half"), 1)
                            lows[0] += 1
                            pe.wait_ge(S("low_half"), lows[0])
                    end(ins)

                pe.wait_ge(S("zA_ready"), l + 1)
                for t in range(NT):
                    ts = slice(t * P, (t + 1) * P)
                    row_matrix(("R1", l, t), Z1, negS, t)
                    scores(("KK", l, t), lambda hh: fA[:, 4 + hh, ts], lambda hh: fA[:, 4 + hh, ts])
                    row_matrix(("R2", l, t), Z2, negI, t)
                    scores(("KQ", l, t), lambda hh: fA[:, 4 + hh, ts], lambda hh: fA[:, hh, ts])
                hd = lambda b, t, hh: b[:, t, hh * P:(hh + 1) * P]
                for t in range(NT):
                    pe.wait_ge(S("LB_ready"), l * 6 * NT + t + 1)
                    scores(("X", l, 0, t), lambda hh: hd(LB, t, hh), lambda hh: ident[:])
                for lev in range(1, 6):
                    for t in range(NT):
                        pe.wait_ge(S("LB_ready"), (l * 6 + lev) * NT + t + 1)
                        pe.wait_ge(S("D_ready"), (l * 5 + lev - 1) * NT + t + 1)
                        pe.wait_ge(S("DT_ready"), (l * 6 + lev - 1) * NT + t + 1)
                        scores(("X", l, lev, t), lambda hh: hd(LB, t, hh), lambda hh: hd(Dm, t, hh))
                    for t in range(NT):
                        pe.wait_ge(S("X_ready"), (l * 5 + lev - 1) * NT + t + 1)
                        if lev < 5:
                            scores(("Y", l, lev, t), lambda hh: hd(DT, t, hh), lambda hh: hd(XB, t, hh))
                        scores(("YT", l, lev, t), lambda hh: hd(XB, t, hh), lambda hh: hd(DT, t, hh))
                for t in range(NT):
                    pe.wait_ge(S("DT_ready"), (l * 6 + 5) * NT + t + 1)
                    pe.wait_ge(S("kbg_ready"), l * NT + t + 1)
                    scores(("U", l, t), lambda hh: hd(DT, t, hh), lambda hh: hd(vb, t, hh))
                    scores(("WT", l, t), lambda hh: hd(kbg, t, hh), lambda hh: hd(DT, t, hh))
                pe.wait_ge(S("aj_ready"), l + 1)
                for t in range(NT):
                    row_matrix(("RA", l, t), AJ, None, t)
                hp = lambda hh: slice(64 * (hh % 2), 64 * (hh % 2) + 64)
                pe.wait_ge(S("fB_ready"), (l + 1) * 4)
                pe.wait_ge(S("gla_ready"), l + 1)
                pe.wait_ge(S("stabB_ready"), l + 1)
                for t in range(NT):
                    ts = slice(t * P, (t + 1) * P)
                    transposes(("TKB", l, t), lambda i: fB[:, 2 + i, ts], n=2)
                    row_matrix(("RB", l, t), NZ, negI, t)
                    by_halves(("KQB", l, t), lambda hh: fB[hp(hh), 2 + hh // 2, ts], lambda hh: fB[hp(hh), hh // 2, ts])
                    by_halves(("KQC", l, t), lambda hh: fC[hp(hh), 2 + hh // 2, ts], lambda hh: fC[hp(hh), hh // 2, ts])
                    transposes(("TKC", l, t), lambda i: keT[:, i, ts], n=2)
                pe.wait_ge(S("scan_ready"), l + 1)
                for n in range(NCH):
                    t, r = n // 2, n % 2
                    rw = slice(64 * r, 64 * r + 64)
                    tk = slice(n * L, (n + 1) * L)
                    pe.wait_ge(S("SA_ready"), l * NCH + n + 1)
                    o = begin(("P1", l, n))
                    for hh in range(H):
                        ins = mm(o[rw, hh * P:(hh + 1) * P], wT[:, t, hh * P + 64 * r:hh * P + 64 * r + 64],
                                 SA[:, hh * P:(hh + 1) * P], True, True)
                    end(ins)
                    o = begin(("P2", l, n))
                    for hh in range(H):
                        ins = mm(o[rw, hh * P:(hh + 1) * P], fA[:, hh, tk], SA[:, hh * P:(hh + 1) * P], True, True)
                    end(ins)
                    pe.wait_ge(S("SB_ready"), l * NCH + n + 1)
                    for p in range(2):
                        o = begin((f"QB{p}", l, n))
                        for i in range(2):
                            ins = mm(o[rw, i * 129:(i + 1) * 129], fB[64 * p:64 * p + 64, i, tk],
                                     SB[64 * p:64 * p + 64, i, :], True, True)
                        end(ins)
                    o = begin(("KVB", l, n))
                    for hh in range(H):
                        ins = mm(o[hp(hh), (hh // 2) * 129:(hh // 2 + 1) * 129], kw[rw, t, hh * 64:(hh + 1) * 64],
                                 vB[rw, t, hh, :], True, True)
                    end(ins)
                    pe.wait_ge(S("SC_ready"), l * NCH + n + 1)
                    by_halves(("QC", l, n), lambda hh: qg[hp(hh), hh // 2, tk], lambda hh: SC[hp(hh), hh // 2, :], rw)
                    o = begin(("KVC", l, n))
                    for hh in range(H):
                        ins = mm(o[hp(hh), (hh // 2) * P:(hh // 2 + 1) * P], keC[rw, t, hh * 64:(hh + 1) * 64],
                                 vC[rw, t, hh * P:(hh + 1) * P], True, True)
                    end(ins)
                    pe.wait_ge(S("delta_ready"), l * NCH + n + 1)
                    o = begin(("P3", l, n))
                    for hh in range(H):
                        ins = mm(o[:, hh * P:(hh + 1) * P], kend[rw, t, hh * P:(hh + 1) * P],
                                 UU[rw, t, hh * P:(hh + 1) * P], True, True)
                    end(ins)
                for t in range(NT):
                    scores(("OA", l, t), lambda hh: hd(AT, t, hh), lambda hh: hd(UU, t, hh))
                    for p in range(2):
                        o = begin((f"OB{p}", l, t))
                        for i in range(2):
                            ins = mm(o[:, i * 129:(i + 1) * 129], hd(WB, t, p + 2 * i), vB[:, t, p + 2 * i, :], True, True)
                        end(ins)
                    scores(("OC", l, t), lambda hh: hd(AC, t, hh), lambda hh: hd(vC, t, hh))
                mods(l, (2, 3, 4, 5))
                ysrc = (oA, nB, oC)
                for g in range(3):
                    for t in range(NT):
                        pe.wait_ge(S("y_branch"), l * 6 + 2 * g + t + 1)
                        transposes(("yT", l, g, t), lambda i: ysrc[g][:, t, i * P:(i + 1) * P])
                pe.wait_ge(S("yT_ready"), (l + 1) * 6)
                pe.wait_ge(S("bmg_landed"), 48 * (l + 1))
                for g in range(3):
                    for hf in range(2):
                        s = [take(), take()]
                        sb_ = take()
                        for t in range(NT):
                            o = begin(("mg", l, g, hf, t))
                            over_d(o, hT[:, :, t * P:(t + 1) * P], s)
                            end(mm(o[:], ones[32 * g:32 * g + 1, :], bmg[32 * g:32 * g + 1, hf * W512:(hf + 1) * W512],
                                   False, True))
                            o = begin(("br", l, g, hf, t))
                            for k in range(4):
                                ins = mm(o[:], yTv[g][:, k, t * P:(t + 1) * P], sb_[:, k, :], k == 0, k == 3)
                            end(ins)
                        release(3)
                pe.wait_ge(S("merged_ready"), (l + 1) * 12)
                for t in range(NT):
                    for q in range(2):
                        transposes(("mT", l, t, q), lambda i: merged[:, t, (4 * q + i) * P:(4 * q + i + 1) * P])
                pe.wait_ge(S("mT_ready"), (l + 1) * 4)
                for hf in range(2):
                    s = [take(), take()]
                    for t in range(NT):
                        o = begin(("wo", l, hf, t))
                        end(over_d(o, mT[:, :, t * P:(t + 1) * P], s))
                    release(2)
                flush()
                make_hT(1)
                if l == 0:
                    widths = ffn_widths(D_FF)

                    def up(name, f):
                        u = [take(), take()]
                        for t in range(NT):
                            o = begin(("ffn", l, name, f, t))
                            end(over_d(o, hT[:, :, t * P:(t + 1) * P], u, widths[f]))
                        release(2)

                    def turn(f):
                        for t in range(NT):
                            pe.wait_ge(S("g_ready"), f * NT + t + 1)
                            o = begin(("ffn", l, "gT", f, t))
                            for i in range(widths[f] // P):
                                ins = T(o[:, i * P:(i + 1) * P], fg[t][:, i * P:(i + 1) * P])
                            end(ins)

                    def down(f):
                        s = [take(), take()]
                        kt = widths[f] // P
                        for t in range(NT):
                            pe.wait_ge(S("gT_ready"), f * NT + t + 1)
                            for hf in range(2):
                                for k in range(kt):
                                    ins = mm(facc_ps[2 * t + hf][:], fgT[t][:, k, :], s[hf][:, k, :],
                                             f == 0 and k == 0, f == len(widths) - 1 and k == kt - 1)
                            ins.then_inc(S("down_done"), 1)
                        flush()
                        pe.wait_ge(S("down_done"), NT * (f + 1))
                        pe.sem_inc(S("slab_used"), 2)

                    for f in range(len(widths) + 1):
                        if f < len(widths):
                            up("w1", f)
                        if f > 0:
                            turn(f - 1)
                        if f < len(widths):
                            up("w3", f)
                        if f > 0:
                            down(f - 1)
                else:
                    o = begin(("router", l))
                    for t in range(NT):
                        for k in range(KD):
                            ins = mm(o[:, 8 * t:8 * t + 8], hT[:, k, t * P:(t + 1) * P], wrt[:, k, :], k == 0, k == KD - 1)
                    end(ins)
                    pe.wait_ge(S("sel_ready"), 1)
                    o = begin(("rank", l))
                    mm(o[:, 0:8], before[:], sel[:, 0, :], True, True)
                    mm(o[:, 8:16], before[:], sel[:, 1, :], True, False)
                    mm(o[:, 8:16], ones[:], sel[:, 0, :], False, True)
                    mm(o[:, 16:24], ones[:], sel[:, 0, :], True, False)
                    end(mm(o[:, 16:24], ones[:], sel[:, 1, :], False, True))
            for i in range(PAD0):
                pe.wait_ge(S(f"bank_free{nj[0] % NBANK}"), nj[0] // NBANK)
                pe.wait_ge(S("mm_done"), nj[0])
                pe.sem_inc(S("mm_done"), 1)
                nj[0] += 1
            assert nj[0] == MOE_BASE
            flush()
            pe.sem_inc(S("mslab_used"), MRING)

            def expert_block(blk):
                jb = MOE_BASE + blk * JBLOCK

                def mbegin(e, i):
                    pe.wait_ge(S(f"bank_free{i % NBANK}"), e * (JPER // NBANK) + (jb + i) // NBANK)
                    return banks[i % NBANK]

                def scatter(e, i0):
                    pe.wait_ge(S("ey_ready"), e + (blk * (N_EXP + 1) + 1))
                    for t in range(NT):
                        for hf in range(2):
                            o = mbegin(e, i0 + 2 * t + hf)
                            mm(o[:], pwT[:, t * P:(t + 1) * P], y[:, hf * W512:(hf + 1) * W512], True, True) \
                                .then_inc(S("mm_done"), 1)

                with pe.Fori(0, N_EXP) as e:
                    got, rel = [0], []

                    def mtake():
                        i = got[0]
                        got[0] += 1
                        pe.wait_ge(S(f"mslab{i % MRING}"), e * (16 * SPER // MRING)
                                   + (blk * N_EXP * 16 * SPER // MRING + 16 * (i // MRING + 1)))
                        return mslot(i % MRING)

                    def mfree():
                        if rel:
                            pe.wait_ge(*rel.pop(0))
                            pe.sem_inc(S("mslab_used"), 2)

                    def mup(name, f):
                        u = [mtake(), mtake()]
                        i = MJOB[(name, f)]
                        o = mbegin(e, i)
                        over_d(o, xgT, u).then_inc(S("mm_done"), 1)
                        mfree()
                        rel.append((S("mm_done"), e * JPER + (jb + i + 1)))

                    def mturn(f):
                        pe.wait_ge(S("eg_ready"), e * NF + (blk * N_EXP * NF + f + 3))
                        o = mbegin(e, MJOB[("gT", f)])
                        for i in range(4):
                            ins = T(o[:, i * P:(i + 1) * P], fg[f % 2][:, i * P:(i + 1) * P])
                        ins.then_inc(S("mm_done"), 1)

                    def mdown(f):
                        s = [mtake(), mtake()]
                        pe.wait_ge(S("egT_ready"), e * NF + (blk * N_EXP * NF + f + 3))
                        if f == 0:
                            pe.wait_ge(S("ybank_free"), e + (blk * N_EXP + 1))
                        for hf in range(2):
                            for k in range(4):
                                ins = mm(facc_ps[hf][:], fgT[f % 2][:, k, :], s[hf][:, k, :], f == 0 and k == 0,
                                         f == NF - 1 and k == 3)
                        ins.then_inc(S("edown_done"), 1)
                        mfree()
                        rel.append((S("edown_done"), e * NF + (blk * N_EXP * NF + f + 3)))

                    pe.wait_ge(S("pick_ready"), e + (blk * N_EXP + 1))
                    for q in range(2):
                        o = mbegin(e, MJOB[("xg", q)])
                        for k in range(4):
                            for t in range(NT):
                                ins = mm(o[:, k * P:(k + 1) * P], h[:, t, (4 * q + k) * P:(4 * q + k + 1) * P],
                                         pick[:, t, :], t == 0, t == NT - 1)
                        ins.then_inc(S("mm_done"), 1)
                    scatter(e, MJOB[("sc", 0, 0)])
                    o = mbegin(e, MJOB[("pwt",)])
                    for t in range(NT):
                        ins = T(o[:, t * P:(t + 1) * P], pickw[:, t, :])
                    ins.then_inc(S("mm_done"), 1)
                    pe.wait_ge(S("xgT_ready"), e * 2 + (blk * N_EXP * 2 + 2))
                    for f in range(NF + 1):
                        if f < NF:
                            mup("w1", f)
                        if f > 0:
                            mturn(f - 1)
                        if f < NF:
                            mup("w3", f)
                        if f > 0:
                            mdown(f - 1)
                    mfree()
                pe.wait_ge(S("pwT_ready"), blk * (N_EXP + 1) + N_EXP + 1)
                scatter(N_EXP, 0)

            pe.sem_inc(S("edown_done"), 2)
            expert_block(0)
            pe.wait_ge(S("route_ready"), 1)
            with pe.If(pe.value_load(over[0:1, 0:1], min_val=0, max_val=1) > 0):
                expert_block(1)

        @block.scalar
        def _(act):
            k = [0]

            def chain(ins):
                k[0] += 1
                ins.then_inc(S("act_chain"), 1)
                act.wait_ge(S("act_chain"), k[0])

            def job(key):
                act.wait_ge(S("mm_done"), JOB[key] + 1)
                return banks[JOB[key] % NBANK]

            def free(key, ins):
                ins.then_inc(S(f"bank_free{JOB[key] % NBANK}"), 1)

            def done(name, ins, n=1):
                ins.then_inc(S(name), n)

            def rstd(dst, src, div):
                chain(act.activation(dst, src, ACT.Ln, bias=cst[:, 0:1], scale=1.0 / div))
                return act.activation(dst, dst, ACT.Exp, scale=-0.5)

            def rms(l, which):
                for t in range(NT):
                    for q in range(2):
                        chain(act.activation(facc_ps[q][:], xs[:, t, q * 512:(q + 1) * 512], ACT.Square,
                                             accum_out=st[:, 4 * t + q:4 * t + q + 1]))
                    chain(act.activation(st[:, 4 * t + 2:4 * t + 3], st[:, 4 * t:4 * t + 1], ACT.Identity,
                                         bias=st[:, 4 * t + 1:4 * t + 2]))
                    done("rstd_ready", rstd(st[:, 4 * t + 3:4 * t + 4], st[:, 4 * t + 2:4 * t + 3], D))

            act.wait_ge(S("consts_ready"), 1)
            act.wait_ge(S("c_turned"), 1)
            done("cact_ready", act.activation(cact[:], banks[7][:, 0:8], ACT.Silu))
            for l in range(DEPTH):
                if l == 0:
                    act.wait_ge(S("x_landed"), 16)
                    act.wait_ge(S("cact_ready"), 1)
                else:
                    act.wait_ge(S("x_ready"), 2 * NT * l)
                rms(l, 0)
                act.wait_ge(S("small_landed"), SMALLS * (l + 1))
                chain(act.activation(cf16[:, 0:4], cf16[:, 0:4], ACT.Exp))
                done("cf_exp", act.activation(cf16[:, 0:4], cf16[:, 0:4], ACT.Copy, scale=-1.0))

                def copy_hT(which):
                    for t in range(NT):
                        for q in range(2):
                            b = job(("hT", l, which, t, q))
                            chain(act.activation(hT[:, 4 * q:4 * q + 4, t * P:(t + 1) * P], h4(b[:]), ACT.Copy))
                            act.sem_inc(S(f"bank_free{JOB[('hT', l, which, t, q)] % NBANK}"), 1)
                            act.sem_inc(S("hT_ready"), 1)
                copy_hT(0)
                b = job(("gT", l))
                chain(act.activation(gTs[0:16, :], b[0:16, 0:SEQ], ACT.Copy))
                act.sem_inc(S(f"bank_free{JOB[('gT', l)] % NBANK}"), 1)
                act.sem_inc(S("gTs_ready"), 1)
                act.wait_ge(S("abs_ready"), 2 * l + 1)
                chain(act.activation(sc(EX), sc(AB_), ACT.Exp, scale=-1.0))
                done("softplus_ln", act.activation(sc(LG), sc(EX), ACT.Ln, bias=cst[:, 1:2]))
                act.wait_ge(S("decay_ready"), l + 1)
                done("beta_ready", act.activation(at(BETA), sc(SP, 4, 4), ACT.Exp))
                act.wait_ge(S("abs_ready"), 2 * l + 2)
                chain(act.activation(tc1, tc1, ACT.Exp, scale=-1.0))
                done("softplus_ln", act.activation(tc1, tc1, ACT.Ln, bias=cst[:, 1:2]))
                for i in range(6):
                    act.wait_ge(S("conv_ready"), l * 16 + 2 * i + 2)
                    done("fA_ready", act.activation(fA[:, 2 * i:2 * i + 2, :], fA[:, 2 * i:2 * i + 2, :], ACT.Silu), 2)
                for i in range(2):
                    act.wait_ge(S("conv_ready"), l * 16 + 12 + 2 * i + 2)
                    done("fB_ready", act.activation(fB[:, 2 * i:2 * i + 2, :], fB[:, 2 * i:2 * i + 2, :], ACT.Silu), 2)
                for i in range(2):
                    b = job(("qkC", l, i))
                    chain(act.activation(fC[:, 2 * i:2 * i + 2, :].rearrange("p a b -> p (a b)"), b[:], ACT.Copy,
                                         scale=0.125 if i == 0 else 1.0))
                    act.sem_inc(S(f"bank_free{JOB[('qkC', l, i)] % NBANK}"), 1)
                act.sem_inc(S("fC_ready"), 1)
                act.wait_ge(S("glaexp_in"), l + 1)
                chain(act.activation(tc2, uc, ACT.Exp, scale=-1.0))
                chain(act.activation(uc, uc, ACT.Exp))
                chain(act.activation(tc1, tc1, ACT.Exp))
                chain(act.activation(bc, bc, ACT.Exp))
                act.sem_inc(S("glaexp_ready"), 1)
                for name, dst, fn in (("zA", zA, ACT.Silu), ("vB", None, ACT.Copy), ("oB", oBg, ACT.Sigmoid),
                                      ("vC", vC, ACT.Copy), ("zC", zC, ACT.Silu)):
                    for t in range(NT):
                        b = job((name, l, t))
                        d = dst[:, t, :] if dst is not None else vB[:, t, :, 0:128]
                        chain(act.activation(d, b[:] if dst is not None else h4(b[:]), fn))
                        act.sem_inc(S(f"bank_free{JOB[(name, l, t)] % NBANK}"), 1)
                        act.sem_inc(S("tok_ready"), 1)
                for t in range(NT):
                    b = job(("TQ", l, t))
                    if t:
                        act.wait_ge(S("sq_used"), l * 4 + 2 * t - 1)
                    chain(act.activation(sq[0], b[:], ACT.Square))
                    act.sem_inc(S(f"bank_free{JOB[('TQ', l, t)] % NBANK}"), 1)
                    act.sem_inc(S("sq_ready"), 1)
                    b = job(("TK", l, t))
                    if t:
                        act.wait_ge(S("sq_used"), l * 4 + 2 * t)
                    chain(act.activation(ktok[:, t, :], b[:], ACT.Copy))
                    chain(act.activation(sq[1], b[:], ACT.Square))
                    act.sem_inc(S(f"bank_free{JOB[('TK', l, t)] % NBANK}"), 1)
                    act.sem_inc(S("sq_ready"), 1)
                act.wait_ge(S("ss_ready"), l + 1)
                done("lnss_ready", act.activation(ssA[:], ssA[:], ACT.Ln, bias=cst[:, 0:1]))
                act.wait_ge(S("zA_ready"), l + 1)
                chain(act.activation(sc(10, 0, 12)[:, :, 0:8], sc(7, 0, 8), ACT.Exp))
                chain(act.activation(at(EZE), at(ZE), ACT.Exp))
                chain(act.activation(geA[:], tot2[:, :, 0:4], ACT.Exp))
                act.sem_inc(S("expA_ready"), 1)
                for t in range(NT):
                    for name, dst in (("R1", LT), ("R2", AT)):
                        b = job((name, l, t))
                        for hh in range(H):
                            ins = act.activation(dst[:, t, hh * P:(hh + 1) * P], b[:, hh * P:(hh + 1) * P], ACT.Exp,
                                                 bias=scal[:, BJ[0], t, BJ[1] + hh:BJ[1] + hh + 1])
                            if hh < H - 1:
                                ins.then_inc(S("act_chain"), 1)
                                k[0] += 1
                            else:
                                chain(ins)
                        act.sem_inc(S(f"bank_free{JOB[(name, l, t)] % NBANK}"), 1)
                        act.sem_inc(S("decayA_ready"), 1)
                for t in range(NT):
                    b = job(("WT", l, t))
                    chain(act.activation(wT[:, t, :], b[:], ACT.Copy))
                    act.sem_inc(S(f"bank_free{JOB[('WT', l, t)] % NBANK}"), 1)
                    act.sem_inc(S("wT_ready"), 1)
                act.wait_ge(S("stabB_ready"), l + 1)
                chain(act.activation(at(SI), at(T0), ACT.Exp))
                chain(act.activation(at(THR), at(T1), ACT.Exp))
                chain(act.activation(at(KWS), at(MN), ACT.Exp, bias=cst[:, 2:3]))
                chain(act.activation(spB[:], spB[:], ACT.Exp))
                act.sem_inc(S("expB_ready"), 1)
                for t in range(NT):
                    b = job(("RB", l, t))
                    for hh in range(H):
                        chain(act.activation(WB[:, t, hh * P:(hh + 1) * P], b[:, hh * P:(hh + 1) * P], ACT.Exp,
                                             bias=scal[:, BJB[0], t, BJB[1] + hh:BJB[1] + hh + 1]))
                    act.sem_inc(S(f"bank_free{JOB[('RB', l, t)] % NBANK}"), 1)
                    act.sem_inc(S("decayB_ready"), 1)
                for g in range(3):
                    for t in range(NT):
                        act.wait_ge(S("o_ready"), l * 6 + 2 * g + t + 1)
                        src = (oA, nB, oC)[g][:, t, :]
                        src = h4(src)
                        done("osq_ready", act.activation(h4(UU[:, t, :]), src, ACT.Square))
                        act.wait_ge(S("oss_ready"), l * 6 + 2 * g + t + 1)
                        r = st[:, 16 + 8 * t:20 + 8 * t]
                        done("orstd_ready", rstd(r, r, P))
                for g in range(3):
                    for t in range(NT):
                        key = ("yT", l, g, t)
                        b = job(key)
                        chain(act.activation(yTv[g][:, :, t * P:(t + 1) * P], h4(b[:]), ACT.Copy))
                        act.sem_inc(S(f"bank_free{JOB[key] % NBANK}"), 1)
                        act.sem_inc(S("yT_ready"), 1)
                m = 0
                for g in range(3):
                    for hf in range(2):
                        for t in range(NT):
                            key = ("mg", l, g, hf, t)
                            b = job(key)
                            if m >= 2:
                                act.wait_ge(S("merged_ready"), l * 12 + m - 1)
                            chain(act.activation(mg_s[m % 2], b[:], ACT.Sigmoid))
                            act.sem_inc(S(f"bank_free{JOB[key] % NBANK}"), 1)
                            act.sem_inc(S("mgate_ready"), 1)
                            m += 1
                for t in range(NT):
                    for q in range(2):
                        key = ("mT", l, t, q)
                        b = job(key)
                        chain(act.activation(mT[:, 4 * q:4 * q + 4, t * P:(t + 1) * P], h4(b[:]), ACT.Copy))
                        act.sem_inc(S(f"bank_free{JOB[key] % NBANK}"), 1)
                        act.sem_inc(S("mT_ready"), 1)
                act.wait_ge(S("x_ready"), (2 * l + 1) * NT)
                rms(l, 1)
                copy_hT(1)
                if l == 0:
                    widths = ffn_widths(D_FF)

                    def gT_copy(f):
                        for t in range(NT):
                            key = ("ffn", l, "gT", f, t)
                            b = job(key)
                            if f > 0:
                                act.wait_ge(S("down_done"), (f - 1) * NT + t + 1)
                            kt = widths[f] // P
                            chain(act.activation(fgT[t][:, 0:kt, :],
                                                 b[:, 0:widths[f]].rearrange("p (a b) -> p a b", b=P), ACT.Copy))
                            act.sem_inc(S(f"bank_free{JOB[key] % NBANK}"), 1)
                            act.sem_inc(S("gT_ready"), 1)

                    for f in range(len(widths) + 1):
                        if f < len(widths):
                            for t in range(NT):
                                key = ("ffn", l, "w1", f, t)
                                b = job(key)
                                if f > 0:
                                    act.wait_ge(S("g_ready"), (f - 1) * NT + t + 1)
                                done("silu_ready", act.activation(fs[t][:, 0:widths[f]], b[:, 0:widths[f]], ACT.Silu))
                                act.wait_ge(S("silu_ready"), f * NT + t + 1)
                                act.sem_inc(S(f"bank_free{JOB[key] % NBANK}"), 1)
                        if f > 0:
                            gT_copy(f - 1)
            act.wait_ge(S("route_in"), 1)
            done("route_exp", act.activation(comb[:], comb[:], ACT.Exp))
            act.sem_inc(S("egT_ready"), 2)

            def expert_block(blk):
                jb = MOE_BASE + blk * JBLOCK
                fb = blk * N_EXP * NF
                with act.Fori(0, N_EXP) as e:
                    def mjob(i):
                        act.wait_ge(S("mm_done"), e * JPER + (jb + i + 1))
                        return banks[i % NBANK]

                    def mfree(i):
                        act.sem_inc(S(f"bank_free{i % NBANK}"), 1)

                    for q in range(2):
                        i = MJOB[("xg", q)]
                        b = mjob(i)
                        act.activation(xgT[:, 4 * q:4 * q + 4, :], h4(b[:]), ACT.Copy).then_inc(S("xgT_ready"), 1)
                        act.wait_ge(S("xgT_ready"), e * 2 + (blk * N_EXP * 2 + q + 1))
                        mfree(i)
                    i = MJOB[("pwt",)]
                    b = mjob(i)
                    act.activation(pwT, b[:, 0:SEQ], ACT.Copy).then_inc(S("pwT_ready"), 1)
                    act.wait_ge(S("pwT_ready"), e + (blk * (N_EXP + 1) + 2))
                    mfree(i)
                    for f in range(NF + 1):
                        if f < NF:
                            i = MJOB[("w1", f)]
                            b = mjob(i)
                            act.wait_ge(S("eg_ready"), e * NF + (fb + f + 1))
                            act.activation(fs[f % 2], b[:], ACT.Silu).then_inc(S("esilu_ready"), 1)
                            act.wait_ge(S("esilu_ready"), e * NF + (fb + f + 1))
                            mfree(i)
                        if f > 0:
                            i = MJOB[("gT", f - 1)]
                            b = mjob(i)
                            act.wait_ge(S("edown_done"), e * NF + (fb + f))
                            act.activation(fgT[(f - 1) % 2], h4(b[:]), ACT.Copy).then_inc(S("egT_ready"), 1)
                            act.wait_ge(S("egT_ready"), e * NF + (fb + f + 2))
                            mfree(i)
                    act.wait_ge(S("edown_done"), e * NF + (fb + NF + 2))
                    for hf in range(2):
                        act.activation(y[:, hf * W512:(hf + 1) * W512], facc_ps[hf][:], ACT.Copy) \
                            .then_inc(S("ey_half"), 1)
                    act.wait_ge(S("ey_half"), e * 2 + (blk * N_EXP * 2 + 2))
                    act.sem_inc(S("ybank_free"), 1)
                    act.sem_inc(S("ey_ready"), 1)

            act.sem_inc(S("ybank_free"), 1)
            act.wait_ge(S("route_ready"), 1)
            expert_block(0)
            with act.If(act.value_load(over[0:1, 0:1], min_val=0, max_val=1) > 0):
                act.wait_ge(S("y_zero"), 2)
                expert_block(1)
            act.wait_ge(S("x_ready"), 2 * NT * DEPTH)
            rms(DEPTH, 0)

        @block.vector
        def _(v):
            k = [0]

            def chain(ins):
                k[0] += 1
                ins.then_inc(S("dve_chain"), 1)
                v.wait_ge(S("dve_chain"), k[0])

            def job(key):
                v.wait_ge(S("mm_done"), JOB[key] + 1)
                return banks[JOB[key] % NBANK]

            def fr(key):
                v.sem_inc(S(f"bank_free{JOB[key] % NBANK}"), 1)

            def tt(o, a, b, op=ALU.mult):
                return v.tensor_tensor(o, a, b, op)

            def normalise(l, which):
                chain(v.scalar_tensor_tensor(mod[:, 1, :], mod[:, 1, :], 1.0, grow, ALU.add, ALU.mult))
                for t in range(NT):
                    v.wait_ge(S("rstd_ready"), (2 * l + which) * NT + t + 1)
                    chain(v.scalar_tensor_tensor(h[:, t, :], xs[:, t, :], st[:, 4 * t + 3:4 * t + 4], mod[:, 1, :],
                                                 ALU.mult, ALU.mult))
                    chain(tt(h[:, t, :], h[:, t, :], mod[:, 0, :], ALU.add))
                    v.sem_inc(S("h_ready"), 1)

            def add_mod(l, piece, slot):
                for hf in range(2):
                    b = job(("mod", l, piece, hf))
                    s = mod[:, slot, hf * 512:(hf + 1) * 512]
                    chain(tt(s, b[:], s, ALU.add))
                    fr(("mod", l, piece, hf))

            v.wait_ge(S("consts_ready"), 1)
            v.wait_ge(S("x_landed"), 16)
            for l in range(DEPTH):
                v.wait_ge(S("small_landed"), SMALLS * (l + 1))
                b = job(("cols", l))
                chain(v.tensor_copy(cols[:], b[:, 0:66]))
                fr(("cols", l))
                add_mod(l, 0, 0)
                add_mod(l, 1, 1)
                normalise(l, 0)
                b = job(("small", l))
                pv = b[:, 0:32].rearrange("p (t n) -> p t n", n=16)
                chain(tt(sc(RAW), pv, rep(bias16[:], NT), ALU.add))
                fr(("small", l))
                chain(tt(sc(RAW), sc(RAW), rep(sgn16[:], NT)))
                chain(v.scalar_tensor_tensor(sc(AB_), sc(RAW), -1.0, sc(RAW), ALU.mult, ALU.max))
                v.sem_inc(S("abs_ready"), 1)
                v.wait_ge(S("softplus_ln"), 2 * l + 1)
                chain(v.scalar_tensor_tensor(sc(SP), sc(RAW), 0.0, sc(LG), ALU.max, ALU.add))
                v.wait_ge(S("cf_exp"), l + 1)
                chain(tt(sc(SP), sc(SP), rep(cf16[:], NT)))
                v.sem_inc(S("decay_ready"), 1)
                b = job(("cum", l))
                pv = b[:, 0:128].rearrange("p (t i n) -> p t i n", t=NT, i=4)
                chain(v.tensor_copy(sc(CUM), pv[:, :, 0, :]))
                chain(v.tensor_copy(sc(TOT), pv[:, :, 1, :]))
                chain(v.tensor_copy(tot2[:].rearrange("p (t r) n -> p t r n", r=2), pv[:, :, 2:4, :]))
                fr(("cum", l))
                b = job(("la", l))
                for f in range(2):
                    chain(v.tensor_scalar(uc[:, f, :], b[:, f * SEQ:(f + 1) * SEQ], cols[:, 64 + f:65 + f], -1.0,
                                          ALU.add, ALU.mult))
                fr(("la", l))
                chain(v.scalar_tensor_tensor(tc1, uc, -1.0, uc, ALU.mult, ALU.max))
                v.sem_inc(S("abs_ready"), 1)
                v.wait_ge(S("softplus_ln"), 2 * l + 2)
                chain(v.scalar_tensor_tensor(tc2, uc, 0.0, tc1, ALU.max, ALU.add))
                chain(v.tensor_scalar(tc2, tc2, -1.0 / 16.0, None, ALU.mult))
                for f in range(2):
                    chain(v.tensor_tensor_scan(bc[:, f, :], rst[:], tc2[:, f, :], 0.0, ALU.mult, ALU.add))
                for i in range(8):
                    key = ("qkvA", l, i) if i < 6 else ("qkB", l, i - 6)
                    b = job(key)
                    for j in range(2):
                        f = 2 * i + j
                        dst = fA[:, f, :] if i < 6 else fB[:, f - 12, :]
                        src = b[:, j * SEQ:(j + 1) * SEQ]
                        tap = lambda q: cols[:, 4 * f + q:4 * f + q + 1]
                        chain(v.tensor_scalar(dst, src, tap(3), None, ALU.mult))
                        for s in range(1, 4):
                            chain(v.scalar_tensor_tensor(dst[:, s:SEQ], src[:, 0:SEQ - s], tap(3 - s),
                                                         dst[:, s:SEQ], ALU.mult, ALU.add))
                        v.sem_inc(S("conv_ready"), 1)
                    fr(key)
                v.wait_ge(S("fC_ready"), l + 1)
                bcv = bc.rearrange("p f (n i) -> p (f n) i", i=L)
                fc = lambda ap: ap.rearrange("p f (n i) -> p (f n) i", i=L)
                chain(tt(fc(uc), bcv, bcv[:, :, L // 2:L // 2 + 1].broadcast_to([P, 8, L]), ALU.subtract))
                chain(tt(fc(tc1), bcv[:, :, L - 1:L].broadcast_to([P, 8, L]), bcv, ALU.subtract))
                v.sem_inc(S("glaexp_in"), 1)
                v.wait_ge(S("glaexp_ready"), l + 1)
                chain(tt(keT, fC[:, 2:4, :], tc1))
                chain(tt(qg, fC[:, 0:2, :], bc))
                chain(v.tensor_copy(aeC[:], bc.rearrange("p f (n i) -> p f n i", i=L)[:, :, :, L - 1]))
                chain(tt(fC[:, 0:2, :], fC[:, 0:2, :], uc))
                chain(tt(fC[:, 2:4, :], fC[:, 2:4, :], tc2))
                v.sem_inc(S("gla_ready"), 1)
                for t in range(NT):
                    for i in range(2):
                        v.wait_ge(S("sq_ready"), l * 4 + 2 * t + i + 1)
                        chain(v.tensor_reduce(ssA[:, t, 4 * i:4 * i + 4], h4(sq[i]), X, ALU.add))
                        v.sem_inc(S("sq_used"), 1)
                    if t == 0:
                        v.wait_ge(S("beta_ready"), l + 1)
                    b = job(("TV", l, t))
                    chain(tt(h4(vb[:, t, :]), h4(b[:]), bc3(at(BETA, t), P)))
                    fr(("TV", l, t))
                v.sem_inc(S("ss_ready"), 1)
                v.wait_ge(S("lnss_ready"), l + 1)
                gc, lb = sc(CUM, 0, 4), sc(SP, 4, 4)
                lq, lk = ssA[:, :, 0:4], ssA[:, :, 4:8]
                stt = v.scalar_tensor_tensor
                chain(stt(at(BJ), lk, -0.5, gc, ALU.mult, ALU.subtract))
                chain(stt(at(Z1), lk, -0.5, gc, ALU.mult, ALU.add))
                chain(tt(at(Z1), at(Z1), lb, ALU.add))
                chain(stt(at(Z2), lq, -0.5, gc, ALU.mult, ALU.add))
                chain(v.tensor_scalar(at(Z2), at(Z2), LN_DKA, None, ALU.add))
                chain(tt(at(ZE), at(BJ), sc(TOT, 0, 4), ALU.add))
                chain(tt(at(AJ), sc(RAW, 8, 4), sc(CUM, 12, 4), ALU.subtract))
                v.sem_inc(S("zA_ready"), 1)
                v.sem_inc(S("aj_ready"), 1)
                for t in range(NT):
                    b = job(("KK", l, t))
                    v.wait_ge(S("decayA_ready"), l * 4 + 2 * t + 1)
                    chain(tt(LT[:, t, :], b[:], LT[:, t, :]))
                    fr(("KK", l, t))
                    b = job(("KQ", l, t))
                    v.wait_ge(S("decayA_ready"), l * 4 + 2 * t + 2)
                    chain(tt(AT[:, t, :], b[:], AT[:, t, :]))
                    fr(("KQ", l, t))
                for t in range(NT):
                    chain(tt(h4(LB[:, t, :]), h4(LT[:, t, :]), rep(lev_m[:, 0, :], H)))
                    v.sem_inc(S("LB_ready"), 1)
                    chain(tt(h4(DT[:, t, :]), rep(ident[:], H), h4(LB[:, t, :]), ALU.subtract))
                    v.sem_inc(S("DT_ready"), 1)
                for t in range(NT):
                    b = job(("X", l, 0, t))
                    chain(tt(h4(Dm[:, t, :]), rep(ident[:], H), h4(b[:]), ALU.subtract))
                    fr(("X", l, 0, t))
                    v.sem_inc(S("D_ready"), 1)
                    chain(tt(h4(LB[:, t, :]), h4(LT[:, t, :]), rep(lev_m[:, 1, :], H)))
                    v.sem_inc(S("LB_ready"), 1)
                for lev in range(1, 6):
                    for t in range(NT):
                        b = job(("X", l, lev, t))
                        chain(v.tensor_copy(XB[:, t, :], b[:]))
                        fr(("X", l, lev, t))
                        v.sem_inc(S("X_ready"), 1)
                        if lev < 5:
                            chain(tt(h4(LB[:, t, :]), h4(LT[:, t, :]), rep(lev_m[:, lev + 1, :], H)))
                            v.sem_inc(S("LB_ready"), 1)
                    for t in range(NT):
                        if lev < 5:
                            b = job(("Y", l, lev, t))
                            chain(tt(Dm[:, t, :], Dm[:, t, :], b[:], ALU.subtract))
                            fr(("Y", l, lev, t))
                            v.sem_inc(S("D_ready"), 1)
                        b = job(("YT", l, lev, t))
                        chain(tt(DT[:, t, :], DT[:, t, :], b[:], ALU.subtract))
                        fr(("YT", l, lev, t))
                        v.sem_inc(S("DT_ready"), 1)
                v.wait_ge(S("expA_ready"), l + 1)
                for t in range(NT):
                    chain(tt(h4(kbg[:, t, :]), h4(ktok[:, t, :]), bc3(at(EZ1, t), P)))
                    v.sem_inc(S("kbg_ready"), 1)
                    chain(tt(h4(kend[:, t, :]), h4(ktok[:, t, :]), bc3(at(EZE, t), P)))
                for t in range(NT):
                    b = job(("U", l, t))
                    chain(v.tensor_copy(UU[:, t, :], b[:]))
                    fr(("U", l, t))
                for t in range(NT):
                    b = job(("RA", l, t))
                    chain(v.tensor_reduce(cmaxB[:, 2 * t:2 * t + 2, :].rearrange("p r h -> p h r"),
                                          b[:].rearrange("p (h r i) -> p h r i", h=H, r=2), X, ALU.max))
                    chain(tt(h4(WB[:, t, :]), h4(b[:]), rep(negL[:], H), ALU.add))
                    fr(("RA", l, t))
                    chain(v.tensor_reduce(at(CM, t), h4(WB[:, t, :]), X, ALU.max))
                be = tot2[:, :, 12:16]
                chain(tt(cmaxB[:], cmaxB[:], be, ALU.add))
                for n in range(NCH):
                    chain(tt(spB[:, n, :], mB[:, n, :], be[:, n, :], ALU.add))
                    chain(tt(mB[:, n + 1, :], spB[:, n, :], cmaxB[:, n, :], ALU.max))
                chain(tt(spB[:], spB[:], mB[:, 1:NCH + 1, :], ALU.subtract))
                for r in range(2):
                    rw = slice(64 * r, 64 * r + 64)
                    mv = mB[rw, 0:NCH, :].rearrange("p (t r) h -> p t r h", r=2)
                    mw = mB[rw, 1:NCH + 1, :].rearrange("p (t r) h -> p t r h", r=2)
                    chain(v.tensor_copy(scal[rw, MP[0], :, MP[1]:MP[1] + 4], mv[:, :, r, :]))
                    chain(v.tensor_copy(scal[rw, MN[0], :, MN[1]:MN[1] + 4], mw[:, :, r, :]))
                chain(tt(at(MX), at(MP), at(CM), ALU.max))
                chain(v.tensor_scalar(at(NZ), at(MX), -1.0, None, ALU.mult))
                chain(tt(at(T0), at(MP), at(MX), ALU.subtract))
                chain(stt(at(T1), at(MX), -1.0, sc(CUM, 12, 4), ALU.mult, ALU.subtract))
                chain(tt(at(MN), sc(TOT, 12, 4), at(MN), ALU.subtract))
                chain(tt(at(MN), at(MN), at(AJ), ALU.add))
                chain(v.tensor_scalar(at(BJB), at(AJ), LN_DKB, None, ALU.add))
                v.sem_inc(S("stabB_ready"), 1)
                v.wait_ge(S("expB_ready"), l + 1)
                for i in range(2):
                    rw = slice(64 * i, 64 * i + 64)
                    chain(v.tensor_copy(spc[rw], spB[rw].rearrange("p n (a b) -> p n a b", b=2)[:, :, :, i]))
                chain(v.memset(vB[:, :, :, 128:129], 1.0))
                chain(v.memset(AC[:], 0.0))
                for t in range(NT):
                    b = job(("TKB", l, t))
                    chain(tt(h4(kw[:, t, :], 64), h4(b[:, 0:256], 64), bc3(at(KWS, t), 64)))
                    fr(("TKB", l, t))
                    b = job(("KQB", l, t))
                    v.wait_ge(S("decayB_ready"), l * NT + t + 1)
                    chain(tt(WB[:, t, :], b[:], WB[:, t, :]))
                    fr(("KQB", l, t))
                    b = job(("KQC", l, t))
                    chain(v.copy_predicated(h4(AC[:, t, :]), rep(tri[:].bitcast(U32), H), h4(b[:])))
                    fr(("KQC", l, t))
                    b = job(("TKC", l, t))
                    chain(v.tensor_copy(keC[:, t, :], b[:, 0:256]))
                    fr(("TKC", l, t))
                chain(v.memset(SA[:], 0.0))
                chain(v.memset(SB[:], 0.0))
                chain(v.memset(SC[:], 0.0))
                v.wait_ge(S("wT_ready"), (l + 1) * NT)
                v.wait_ge(S("tok_ready"), (l + 1) * 5 * NT)
                v.sem_inc(S("scan_ready"), 1)
                for name in ("SA_ready", "SB_ready", "SC_ready"):
                    v.sem_inc(S(name), 1)
                for n in range(NCH):
                    t, r = n // 2, n % 2
                    rw = slice(64 * r, 64 * r + 64)
                    b = job(("P1", l, n))
                    chain(tt(UU[rw, t, :], UU[rw, t, :], b[rw, :], ALU.subtract))
                    fr(("P1", l, n))
                    v.sem_inc(S("delta_ready"), 1)
                    b = job(("P2", l, n))
                    chain(tt(h4(oA[rw, t, :]), h4(b[rw, :]), bc3(scal[rw, EZ2[0], t, EZ2[1]:EZ2[1] + 4], P)))
                    fr(("P2", l, n))
                    for p in range(2):
                        b = job((f"QB{p}", l, n))
                        bv = b[rw, 0:258].rearrange("p (a d) -> p a d", d=129)
                        sv = scal[rw, SI[0], t, SI[1] + p:SI[1] + 4:2]
                        chain(tt(h4(nB[rw, t, :])[:, p:4:2, :], bv[:, :, 0:128], bc3(sv, P)))
                        chain(tt(dB[rw, t, p:4:2], bv[:, :, 128], sv))
                        fr((f"QB{p}", l, n))
                    b = job(("KVB", l, n))
                    for p in range(2):
                        chain(stt(SB[:, p, :], SB[:, p, :], spc[:, n, p:p + 1], b[:, p * 129:(p + 1) * 129],
                                  ALU.mult, ALU.add))
                    fr(("KVB", l, n))
                    b = job(("QC", l, n))
                    chain(v.tensor_copy(oC[rw, t, :], b[rw, :]))
                    fr(("QC", l, n))
                    b = job(("KVC", l, n))
                    for p in range(2):
                        chain(stt(SC[:, p, :], SC[:, p, :], aeC[:, p, n:n + 1], b[:, p * P:(p + 1) * P],
                                  ALU.mult, ALU.add))
                    fr(("KVC", l, n))
                    b = job(("P3", l, n))
                    for hh in range(H):
                        hs = slice(hh * P, (hh + 1) * P)
                        chain(stt(SA[:, hs], SA[:, hs], geA[:, n, hh:hh + 1], b[:, hs], ALU.mult, ALU.add))
                    fr(("P3", l, n))
                    if n < NCH - 1:
                        for name in ("SA_ready", "SB_ready", "SC_ready"):
                            v.sem_inc(S(name), 1)
                for t in range(NT):
                    b = job(("OA", l, t))
                    chain(tt(oA[:, t, :], oA[:, t, :], b[:], ALU.add))
                    fr(("OA", l, t))
                    for p in range(2):
                        b = job((f"OB{p}", l, t))
                        bv = b[:, 0:258].rearrange("p (a d) -> p a d", d=129)
                        nv = h4(nB[:, t, :])[:, p:4:2, :]
                        chain(tt(nv, nv, bv[:, :, 0:128], ALU.add))
                        dv = dB[:, t, p:4:2]
                        chain(tt(dv, dv, bv[:, :, 128], ALU.add))
                        fr((f"OB{p}", l, t))
                    b = job(("OC", l, t))
                    chain(tt(oC[:, t, :], oC[:, t, :], b[:], ALU.add))
                    fr(("OC", l, t))
                chain(stt(at(T0), dB[:], -1.0, dB[:], ALU.mult, ALU.max))
                chain(tt(at(T0), at(T0), at(THR), ALU.max))
                chain(v.reciprocal(at(T0), at(T0)))
                for t in range(NT):
                    chain(tt(h4(nB[:, t, :]), h4(nB[:, t, :]), bc3(at(T0, t), P)))
                add_mod(l, 2, 2)
                v.wait_ge(S("ffn_rows_landed"), 32 * (l + 1))
                add_mod(l, 3, 0)
                add_mod(l, 4, 1)
                add_mod(l, 5, 3)
                for g, (o, z) in enumerate(((oA, zA), (nB, oBg), (oC, zC))):
                    for t in range(NT):
                        chain(tt(h4(z[:, t, :]), h4(z[:, t, :]), rep(normr[:, g, :], H)))
                        v.sem_inc(S("o_ready"), 1)
                        v.wait_ge(S("osq_ready"), l * 6 + 2 * g + t + 1)
                        r = st[:, 16 + 8 * t:20 + 8 * t]
                        chain(v.tensor_reduce(r, h4(UU[:, t, :]), X, ALU.add))
                        v.sem_inc(S("oss_ready"), 1)
                        v.wait_ge(S("orstd_ready"), l * 6 + 2 * g + t + 1)
                        chain(tt(h4(o[:, t, :]), h4(o[:, t, :]), bc3(r, P)))
                        chain(tt(o[:, t, :], o[:, t, :], z[:, t, :]))
                        v.sem_inc(S("y_branch"), 1)
                m = 0
                for g in range(3):
                    for hf in range(2):
                        for t in range(NT):
                            v.wait_ge(S("mgate_ready"), l * 12 + m + 1)
                            b = job(("br", l, g, hf, t))
                            dst = merged[:, t, hf * 512:(hf + 1) * 512]
                            if g == 0:
                                chain(tt(dst, b[:], mg_s[m % 2]))
                            else:
                                chain(tt(mg_s[m % 2], b[:], mg_s[m % 2]))
                                chain(tt(dst, dst, mg_s[m % 2], ALU.add))
                            fr(("br", l, g, hf, t))
                            v.sem_inc(S("merged_ready"), 1)
                            m += 1

                def residual(bank_ap, gate, t, hf, tmp):
                    cs = slice(hf * 512, (hf + 1) * 512)
                    chain(tt(tmp, bank_ap, mod[:, gate, cs]))
                    chain(tt(xs[:, t, cs], xs[:, t, cs], tmp, ALU.add))

                for hf in range(2):
                    for t in range(NT):
                        b = job(("wo", l, hf, t))
                        residual(b[:], 2, t, hf, ktok[:, 0, :])
                        fr(("wo", l, hf, t))
                        if hf == 1:
                            v.sem_inc(S("x_ready"), 1)
                v.wait_ge(S("gffn_landed"), 16 * (l + 1))
                normalise(l, 1)
                if l == 0:
                    widths = ffn_widths(D_FF)
                    for f, wd in enumerate(widths):
                        for t in range(NT):
                            key = ("ffn", l, "w3", f, t)
                            b = job(key)
                            v.wait_ge(S("silu_ready"), f * NT + t + 1)
                            if f > 0:
                                v.wait_ge(S("gT_ready"), (f - 1) * NT + t + 1)
                            chain(tt(fg[t][:, 0:wd], fs[t][:, 0:wd], b[:, 0:wd]))
                            fr(key)
                            v.sem_inc(S("g_ready"), 1)
                    v.wait_ge(S("down_done"), NT * len(widths))
                    for t in range(NT):
                        for hf in range(2):
                            residual(facc_ps[2 * t + hf][:], 3, t, hf, Dm[:, 0, :])
                        v.sem_inc(S("x_ready"), 1)
                else:
                    b = job(("router", l))
                    lg = route[:, 0:16].rearrange("p (t n) -> p t n", n=8)
                    chain(tt(lg, b[:, 0:16].rearrange("p (t n) -> p t n", n=8), rep(brt[:], NT), ALU.add))
                    fr(("router", l))
                    cmp = route[:, 64:128].rearrange("p (a b) -> p a b", b=8)
                    eq = route[:, 128:192].rearrange("p (a b) -> p a b", b=8)
                    lower = route[:, 192:256].rearrange("p (a b) -> p a b", b=8)
                    chain(v.memset(lower, 0.0))
                    for i in range(1, 8):
                        chain(v.memset(lower[:, i, 0:i], 1.0))
                    top = st[:, 32:34]
                    for t in range(NT):
                        mine = bc3(lg[:, t, :], 8)
                        other = rep(lg[:, t, :], 8)
                        chain(tt(cmp, other, mine, ALU.is_gt))
                        chain(tt(eq, other, mine, ALU.is_equal))
                        chain(tt(eq, eq, lower))
                        chain(tt(cmp, cmp, eq, ALU.add))
                        chain(v.tensor_reduce(sel[:, t, :], cmp, X, ALU.add))
                        chain(v.tensor_scalar(sel[:, t, :], sel[:, t, :], 2.0, None, ALU.is_lt))
                        chain(v.tensor_reduce(top[:, t:t + 1], lg[:, t, :], X, ALU.max))
                        chain(v.tensor_scalar(comb[:, t, :], lg[:, t, :], top[:, t:t + 1], None, ALU.subtract))
                    v.sem_inc(S("sel_ready"), 1)
                    v.sem_inc(S("route_in"), 1)
                    v.wait_ge(S("route_exp"), 1)
                    for t in range(NT):
                        chain(tt(comb[:, t, :], comb[:, t, :], sel[:, t, :]))
                        chain(v.tensor_reduce(top[:, t:t + 1], comb[:, t, :], X, ALU.add))
                        chain(v.reciprocal(top[:, t:t + 1], top[:, t:t + 1]))
                        chain(v.tensor_scalar(comb[:, t, :], comb[:, t, :], top[:, t:t + 1], None, ALU.mult))
                    chain(v.memset(facc, 0.0))
                    b = job(("rank", l))
                    chain(v.tensor_copy(rank[:], b[:, 0:16].rearrange("p (t n) -> p t n", n=8)))
                    chain(v.tensor_reduce(top[:, 0:1], b[:, 16:24], X, ALU.max))
                    fr(("rank", l))
                    chain(v.tensor_scalar(over[:], top[:, 0:1], float(CAP), None, ALU.is_gt))
            for i in range(len(order), MOE_BASE):
                v.wait_ge(S("mm_done"), i + 1)
                v.sem_inc(S(f"bank_free{i % NBANK}"), 1)
            v.wait_ge(S("slots_ready"), BLOCKS)

            def expert_block(blk):
                jb = MOE_BASE + blk * JBLOCK
                fb = blk * N_EXP * NF

                def add_scattered(e, i0):
                    for t in range(NT):
                        for hf in range(2):
                            i = i0 + 2 * t + hf
                            v.wait_ge(S("mm_done"), e * JPER + (jb + i + 1))
                            dst = facc[:, t, hf * W512:(hf + 1) * W512]
                            v.tensor_tensor(dst, dst, banks[i % NBANK][:], ALU.add).then_inc(S("facc_done"), 1)
                            v.wait_ge(S("facc_done"), e * (2 * NT) + (blk * 2 * NT * (N_EXP + 1) + 2 * t + hf + 1))
                            v.sem_inc(S(f"bank_free{i % NBANK}"), 1)

                if blk == 0:
                    chain(v.memset(pwT, 0.0))
                v.memset(y, 0.0).then_inc(S("y_zero"), 1)
                v.wait_ge(S("y_zero"), blk + 1)
                v.sem_inc(S("ey_ready"), 1)
                v.sem_inc(S("pwT_ready"), 1)
                if blk == 0:
                    v.sem_inc(S("route_ready"), 1)
                with v.Fori(0, N_EXP) as e:
                    for t in range(NT):
                        v.tensor_scalar(pick[:, t, :], slot_no[blk], rank[:, t, bass.ds(e, 1)],
                                        sel[:, t, bass.ds(e, 1)], ALU.is_equal, ALU.mult)
                        ins = v.tensor_scalar(pickw[:, t, :], slot_no[blk], rank[:, t, bass.ds(e, 1)],
                                              comb[:, t, bass.ds(e, 1)], ALU.is_equal, ALU.mult)
                    ins.then_inc(S("pick_ready"), 1)
                    add_scattered(e, MJOB[("sc", 0, 0)])
                    for f in range(NF):
                        i = MJOB[("w3", f)]
                        v.wait_ge(S("mm_done"), e * JPER + (jb + i + 1))
                        v.wait_ge(S("esilu_ready"), e * NF + (fb + f + 1))
                        v.wait_ge(S("egT_ready"), e * NF + (fb + f + 1))
                        v.tensor_tensor(fg[f % 2], fs[f % 2], banks[i % NBANK][:], ALU.mult) \
                            .then_inc(S("eg_ready"), 1)
                        v.wait_ge(S("eg_ready"), e * NF + (fb + f + 3))
                        v.sem_inc(S(f"bank_free{i % NBANK}"), 1)
                add_scattered(N_EXP, 0)

            v.sem_inc(S("eg_ready"), 2)
            expert_block(0)
            with v.If(v.value_load(over[0:1, 0:1], min_val=0, max_val=1) > 0):
                expert_block(1)
            for t in range(NT):
                chain(tt(facc[:, t, :], facc[:, t, :], mod[:, 3, :]))
                chain(tt(xs[:, t, :], xs[:, t, :], facc[:, t, :], ALU.add))
                v.sem_inc(S("x_ready"), 1)
            v.wait_ge(S("gfinal_landed"), 16)
            for t in range(NT):
                v.wait_ge(S("rstd_ready"), 2 * DEPTH * NT + t + 1)
                chain(stt(xs[:, t, :], xs[:, t, :], st[:, 4 * t + 3:4 * t + 4], mod[:, 0, :], ALU.mult, ALU.mult))
                v.sem_inc(S("y_ready"), 1)


_INS = ["x", "c", "w_ada", "b_ada", "g_mix", "g_ffn", "g_final", "w_in", "conv_a", "a_log", "dt_bias", "norm_a",
        "conv_b", "b_i", "b_f", "norm_b", "w_gla2", "b_gla", "norm_c", "w_br", "w_mg", "b_mg", "w_o",
        "w1_d", "w3_d", "w2_d", "w_router", "b_router", "w1_e", "w3_e", "w2_e"]


def kernel(**inputs):
    import numpy as _np
    import concourse.bacc as _bacc
    from concourse import mybir as _mybir
    from concourse.bass_utils import run_bass_kernel_spmd as _run

    nc = _bacc.Bacc("TRN2", target_bir_lowering=False, num_devices=1)
    arrays, args = {}, []
    for name in _INS:
        a = _np.ascontiguousarray(inputs[name])
        arrays[f"in_{name}_dram"] = a
        args.append(nc.dram_tensor(f"in_{name}_dram", a.shape, _mybir.dt.from_np(a.dtype), kind="ExternalInput").ap())
    args.append(nc.dram_tensor("out_0_dram", (1, SEQ, D), F32, kind="ExternalOutput").ap())
    hybrid_kernel(nc, *args)
    r = _run(nc, [arrays], core_ids=[0])
    return r.results[0]["out_0_dram"]
```

```python
from contextlib import ExitStack

import numpy as np

import concourse.bass as bass
from concourse import mybir

F32 = mybir.dt.float32
F32R = mybir.dt.float32r
I32 = mybir.dt.int32
U32 = mybir.dt.uint32
ACT = mybir.ActivationFunctionType
ALU = mybir.AluOpType
X = mybir.AxisListType.X

P = 128
D = 1024
KD = D // P
SEQ = 256
NT = SEQ // P
L = 64
NCH = SEQ // L
H = 4
DEPTH = 2
W512 = 512
NEG = -1.0e30
EPS = 1e-6
D_FF = 2816
N_EXP = 8
D_FFE = 3584
RING = 4
SPLITS = 3
NBANK = 4
ALL_BANKS = 8

QA, ZA = 0, 1536
AB = 2048
QB, VB, OB = 2056, 2568, 3080
IF = 3592
QC, VC, ZC = 3600, 4112, 4624
GC = 5136
LN_DKA = float(-0.5 * np.log(128.0))
LN_DKB = float(-0.5 * np.log(64.0))


def ffn_widths(dff):
    return [W512] * (dff // W512) + ([dff % W512] if dff % W512 else [])


class Schedule:

    def __init__(self):
        self.slabs, self.jobs, self.mids, self.downs = [], [], 0, 0
        self.need = {}

    def add(self, *jobs):
        self.jobs += jobs
        for j in jobs:
            self.need[j] = len(self.slabs)

    def group(self, slabs, jobs, shape=(4, W512)):
        for key in slabs[:-1]:
            self.mids += 1
            self.slabs.append((key, shape, ("slab_mid", self.mids)))
        self.jobs += jobs
        self.slabs.append((slabs[-1], shape, ("mm_done", len(self.jobs))))
        for j in jobs:
            self.need[j] = len(self.slabs)

    def down(self, slabs, shape):
        for key in slabs:
            self.downs += 1
            self.slabs.append((key, shape, ("down_done", self.downs)))


def mod_group(s, l, piece, hf):
    s.group([("ada", l, k, piece * D + hf * W512) for k in range(2)], [("mod", l, piece, hf)])


def schedule():
    s = Schedule()
    for l in range(DEPTH):
        for piece in (0, 1):
            for hf in range(2):
                mod_group(s, l, piece, hf)
        s.add(("cols", l))
        s.add(*[("hT", l, 0, t, q) for t in range(NT) for q in range(2)])
        s.add(("small", l), ("turned", l))
        for name, col, i in (("qkvA", QA, 0), ("qkvA", QA + 512, 2), ("qkvA", QA + 1024, 4), ("qkB", QB, 0),
                             ("qkC", QC, 0)):
            if name == "qkC":
                s.add(*[(n, l, t) for t in range(NT) for n in ("TQ", "TK")])
            s.group([("in", l, k, col) for k in range(2)], [(name, l, i), (name, l, i + 1)])
            if col == QA:
                s.add(("cum", l), ("la", l))
        for name, col in (("vB", VB), ("vC", VC)):
            s.group([("in", l, k, col) for k in range(2)], [(name, l, t) for t in range(NT)])
        for t in range(NT):
            s.add(("R1", l, t), ("KK", l, t), ("R2", l, t), ("KQ", l, t))
        s.add(*[("X", l, 0, t) for t in range(NT)])
        for lev in range(1, LEVELS):
            s.add(*[("X", l, lev, t) for t in range(NT)])
            if lev < 5:
                mod_group(s, l, *LEVEL_MODS[lev - 1])
            if lev == 1:
                s.add(*[("RA", l, t) for t in range(NT)])
            for t in range(NT):
                s.add(*([("Y", l, lev, t)] if lev < LEVELS - 1 else []), ("YT", l, lev, t))
        for t in range(NT):
            s.add(("TK2", l, t), ("TV", l, t))
        for t in range(NT):
            s.add(("U", l, t), ("WT", l, t))
        for t in range(NT):
            s.add(("TKB", l, t), ("RB", l, t), ("KQB", l, t), ("KQC", l, t), ("TKC", l, t))
        for n in range(NCH):
            s.add(("P1", l, n), ("P2", l, n), ("QB0", l, n), ("QB1", l, n), ("KVB", l, n), ("P3", l, n),
                  ("QC", l, n), ("KVC", l, n))
            if n == 0:
                s.group([("in", l, k, OB) for k in range(2)], [("oB", l, t) for t in range(NT)])
        for t in range(NT):
            s.add(("OA", l, t), ("OB0", l, t), ("OB1", l, t), ("OC", l, t))
        for name, col in (("zA", ZA), ("zC", ZC)):
            s.group([("in", l, k, col) for k in range(2)], [(name, l, t) for t in range(NT)])
        for piece in (2, 5):
            for hf in range(2):
                mod_group(s, l, piece, hf)
        s.add(*[("yT", l, g, t) for g in range(2) for t in range(NT)])
        for g in range(3):
            for hf in range(2):
                s.group([("mg", l, g, k, hf) for k in range(2)], [("mg", l, g, hf, t) for t in range(NT)])
                s.group([("br", l, g, hf)], [("br", l, g, hf, t) for t in range(NT)])
            if g == 0:
                s.add(*[("yT", l, 2, t) for t in range(NT)])
        s.add(*[("mT", l, t, q) for t in range(NT) for q in range(2)])
        for hf in range(2):
            s.group([("wo", l, k, hf) for k in range(2)], [("wo", l, hf, t) for t in range(NT)])
        s.add(*[("hT", l, 1, t, q) for t in range(NT) for q in range(2)])
        if l % 2 == 1:
            s.add(("logitsT", l), ("router", l), ("rank", l))
        else:
            widths = ffn_widths(D_FF)
            for f in range(len(widths) + 1):
                if f < len(widths):
                    s.group([("w1", k, f) for k in range(2)], [("ffn", l, "w1", f, t) for t in range(NT)],
                            (4, widths[f]))
                if f > 0:
                    s.add(*[("ffn", l, "gT", f - 1, t) for t in range(NT)])
                if f < len(widths):
                    s.group([("w3", k, f) for k in range(2)], [("ffn", l, "w3", f, t) for t in range(NT)],
                            (4, widths[f]))
                if f > 0:
                    s.down([("w2", f - 1, hf) for hf in range(2)], (widths[f - 1] // P, W512))
    return s


def place_jobs(jobs):
    uses, where, sums_at = [0] * ALL_BANKS, {}, None
    for i, key in enumerate(jobs):
        ffn = key[0] == "ffn"
        if ffn and sums_at is None:
            sums_at = list(uses)
        if i > 0 and jobs[i - 1][0] == "ffn" and not ffn:
            for b in range(NBANK, ALL_BANKS):
                uses[b] += 1
        b = i % (NBANK if ffn else ALL_BANKS)
        where[key] = (b, uses[b])
        uses[b] += 1
    return where, sums_at, uses


def low_makers(slabs):
    made, out = {"low_pool": 0, "low_dve": 0}, []
    for (kind, *where), _, _ in slabs:
        who = "low_pool"
        if kind == "ada":
            l, k, col = where
            piece = col // D
            if piece in (0, 1, 2, 5) and (k == 1 or l == 0 and piece < 2):
                who = "low_dve"
        made[who] += 1
        out.append((who, made[who]))
    return out, made


SMALLS = 19 * 16
LEVELS = 6
LEVEL_MODS = [(3, 0), (3, 1), (4, 0), (4, 1)]
NF = D_FFE // W512
CAP = P
BLOCKS = SEQ // CAP
EXPERT_JOBS = []
for _f in range(NF + 1):
    if _f < NF:
        EXPERT_JOBS.append(("w1", _f))
    if _f == 0:
        EXPERT_JOBS += [("sc", t, hf) for t in range(NT) for hf in range(2)] + [("pwt",)]
    if _f > 0:
        EXPERT_JOBS.append(("gT", _f - 1))
    if _f < NF:
        EXPERT_JOBS.append(("w3", _f))
    if _f == NF - 1:
        EXPERT_JOBS += [("xg", 0), ("xg", 1)]
MJOB = {k: i for i, k in enumerate(EXPERT_JOBS)}
JPER = len(EXPERT_JOBS)
FIRST = 4
JBLOCK = FIRST + N_EXP * JPER + 2 * NT
SPER = 6 * NF
MRING = 7


def low_part(i):
    if i % 6 == 4:
        return "mlow_pool", i // 6 + 1, SPER // 6
    return "mlow_dve", i + 1 - (i + 1) // 6, SPER - SPER // 6


def moe_slab(name, f):
    if name == "w2":
        return moe_slab("w3", f + 1) + 2 if f + 1 < NF else SPER - 2
    return (6 * f - 2 if f else 0) + (2 if name == "w3" else 0)


def moe_free(i):
    back, i = (1, i + SPER) if i < 0 else (0, i)
    for f in range(NF):
        for j, name in enumerate(("w1", "w3")):
            if i == moe_slab(name, f):
                return "mslab_mid", 2 * f + j + 1 - back * 2 * NF
            if i == moe_slab(name, f) + 1:
                return "mm_done", MJOB[(name, f)] + 1 - back * JPER
        if moe_slab("w2", f) <= i < moe_slab("w2", f) + 2:
            return "edown_done", 2 * f + i - moe_slab("w2", f) + 1 - back * 2 * NF


def hybrid_kernel(nc, x, c, w_ada, b_ada, g_mix, g_ffn, g_final, w_in, conv_a, a_log, dt_bias, norm_a,
                  conv_b, b_i, b_f, norm_b, w_gla2, b_gla, norm_c, w_br, w_mg, b_mg, w_o,
                  w1_d, w3_d, w2_d, w_router, b_router, w1_e, w3_e, w2_e, out):
    with ExitStack() as ctx:
        sems = {}

        def S(name):
            if name not in sems:
                sems[name] = ctx.enter_context(nc.semaphore(name))
            return sems[name]

        def sb(name, shape, dt=F32):
            return ctx.enter_context(nc.sbuf_tensor(name, shape, dt))

        ring = sb("ring", [P, RING, 4, W512])
        wsplit = sb("wsplit", [P, SPLITS, 2, 4, W512], F32R)
        hT = sb("hT", [P, 2, KD, SEQ], F32R)
        xs = sb("xs", [P, NT, D])
        mod = sb("mod", [P, 2, D])
        ident = sb("ident", [P, P])
        tri = sb("tri", [P, P])
        same = sb("same", [P, P])
        half = sb("half", [P, 2, P])
        negI = sb("negI", [P, P])
        negS = sb("negS", [P, P])
        negL = sb("negL", [P, P])
        lev_m = sb("lev_m", [P, 6, P])
        ones = sb("ones", [P, P])
        rst = sb("rst", [P, SEQ])
        cst = sb("cst", [P, 8])
        crow = sb("crow", [8, P])
        cactf = sb("cactf", [P, KD])
        cact = sb("cact", [P, 2, KD], F32R)
        bglar = sb("bglar", [2, P])
        cols = sb("cols", [P, 66])
        wsm = sb("wsm", [P, KD, 40])
        wsm2 = sb("wsm2", [P, 2, KD, 40], F32R)
        wgla = sb("wgla", [16, 256])
        bias16 = sb("bias16", [P, 16])
        sgn16 = sb("sgn16", [P, 16])
        cf16 = sb("cf16", [P, 16])
        normr = sb("normr", [P, 3, P])
        brt = sb("brt", [P, 8])
        st = sb("st", [P, 64])
        comb = sb("comb", [P, NT, N_EXP + 1])
        lower = sb("lower", [P, 8, 8])
        scal = sb("scal", [P, 12, NT, 16])
        WORK = 18442
        work = sb("work", [P, WORK])
        WORK_AT = nc.sbuf_base - 4 * WORK
        used = [0]

        def wk(n, *shape):
            a = used[0]
            used[0] += n
            assert used[0] <= WORK, used
            v = work[:, a:a + n]
            if len(shape) == 2:
                return v.rearrange("p (a b) -> p a b", b=shape[1])
            if len(shape) == 3:
                return v.rearrange("p (a b c) -> p a b c", b=shape[1], c=shape[2])
            return v

        fA = wk(12 * SEQ, 12, SEQ)
        fB = wk(4 * SEQ, 4, SEQ)
        fC = wk(4 * SEQ, 4, SEQ)
        vb_at = used[0]
        vB = wk(NT * 516, NT, 4, 129)
        vC = wk(NT * 512, NT, 512)
        lt_at = used[0]
        LT = wk(NT * 512, NT, 512)
        a2_at = used[0]
        AT = wk(NT * 512, NT, 512)
        WB = wk(NT * 512, NT, 512)
        AC = wk(NT * 512, NT, 512)
        kw = wk(NT * 256, NT, 256)
        keC = wk(NT * 256, NT, 256)
        dm_at = used[0]
        Dm = wk(NT * 512, NT, 512)
        DT = wk(NT * 512, NT, 512)
        LB = wk(NT * 512, NT, 512)
        XB = wk(NT * 512, NT, 512)
        sa_at = used[0]
        SA = wk(512)
        SB = wk(2 * 129, 2, 129)
        SC = wk(2 * 128, 2, 128)
        qg_at = used[0]
        qg = wk(2 * SEQ, 2, SEQ)
        keT = wk(2 * SEQ, 2, SEQ)
        flat = lambda a, n: work[:, a:a + n]
        UU = flat(4 * SEQ, NT * 512).rearrange("p (t n) -> p t n", t=NT)
        wT = flat(8 * SEQ, NT * 512).rearrange("p (t n) -> p t n", t=NT)
        convr = work[0:4, lt_at:lt_at + 2048]
        kbg, kend = XB, LB
        vb = Dm
        oA, nB, oC = Dm, DT, LT
        zA, oBg, zC = LB, XB, fC.rearrange("p a b -> p (a b)").rearrange("p (t n) -> p t n", t=NT)
        half_t = lambda b, t: b[:, t, :].rearrange("p (f i) -> p f i", f=2)
        bc, uc, tc1, tc2 = half_t(Dm, 0), half_t(Dm, 1), half_t(DT, 0), half_t(DT, 1)
        small_T = LB[0:32, 0, 0:SEQ]
        gTs = small_T[0:16, :]
        grow = LB.rearrange("p t n -> p (t n)")
        bmg = XB.rearrange("p t n -> p (t n)")
        oss = st[:, 16:40]
        osq = [UU.rearrange("p t n -> p (t n)"), wT.rearrange("p t n -> p (t n)"), AT.rearrange("p t n -> p (t n)")]
        sq = [XB[:, 0, :], XB[:, 1, :]]
        h = work[:, 0:NT * D].rearrange("p (t d) -> p t d", t=NT)
        mg_s = [wT[:, 0, :], wT[:, 1, :]]
        gates = {2: flat(vb_at, D), 5: flat(qg_at, D)}
        merged = work[:, 12 * SEQ:12 * SEQ + NT * D].rearrange("p (t d) -> p t d", t=NT)
        act2 = nc.alloc_sbuf_tensor_at("act2", [P, 2, KD, SEQ], F32R, offset=WORK_AT + 4 * a2_at)
        mT = act2
        yT = [act2[:, :, 4 * (g % 2):4 * (g % 2) + 4, :] for g in range(3)]
        fgT = [act2[:, :, 2 * i:2 * i + 2, :].rearrange("p s a b -> p s (a b)").rearrange("p s (f i) -> p s f i", f=4)
               for i in range(2)]
        fs = [LB[:, i, :] for i in range(2)]
        fg = [flat(sa_at + i * 512, 512) for i in range(2)]
        h_words = NT * D
        extra = work[:, h_words:h_words + (MRING - RING) * 2048].rearrange("p (s k n) -> p s k n", s=MRING - RING, k=4)
        assert h_words + (MRING - RING) * 2048 <= a2_at
        facc = flat(dm_at, NT * D).rearrange("p (t d) -> p t d", t=NT)
        y = XB.rearrange("p t n -> p (t n)")
        xgT = hT[:].rearrange("p s k i -> p s (k i)")[:, :, 0:D].rearrange("p s (k i) -> p s k i", i=P)
        m1 = mod[:, 1, :]
        pick = m1[:, 0:256].rearrange("p (t c) -> p t c", t=NT)
        pickw = m1[:, 256:512].rearrange("p (t c) -> p t c", t=NT)
        pwT = m1[:, 512:768]
        slot_no = [m1[:, 768:896], m1[:, 896:1024]]
        logits_T = LB[0:8, 0, 0:SEQ]
        route = XB.rearrange("p t n -> p (t n)")

        RAW, AB_, EX, LG, SP, CUM, TOT = 0, 1, 2, 3, 4, 5, 6
        Z1, Z2, BJ, ZE, AJ = (7, 0), (7, 4), (7, 8), (7, 12), (8, 0)

        def sc(kind, a=0, n=16):
            return scal[:, kind, :, a:a + n]

        def at(where, t=None, n=4):
            k, a = where
            return scal[:, k, :, a:a + n] if t is None else scal[:, k, t, a:a + n]

        CM, MX, MP, MN = (8, 4), (8, 8), (9, 0), (9, 4)
        EZ1, EZ2, EZE, BETA = (10, 0), (10, 4), (10, 8), (9, 8)
        SI, THR, KWS, NZ = (11, 0), (11, 4), (11, 8), (11, 12)
        BJB, T0, T1 = (10, 12), (9, 12), (8, 12)
        tot2 = sb("tot2", [P, NCH, 16])
        geA = sb("geA", [P, NCH, 4])
        cmaxB = sb("cmaxB", [P, NCH, 4])
        mB = sb("mB", [P, NCH + 1, 4])
        spB = sb("spB", [P, NCH, 4])
        spc = sb("spc", [P, NCH, 2])
        aeC = sb("aeC", [P, 2, NCH])
        dB = sb("dB", [P, NT, 4])
        sel = sb("sel", [P, NT, N_EXP + 1])
        rank = sb("rank", [P, NT, N_EXP + 1])
        before = sb("before", [P, P])
        over = sb("over", [P, 1], I32)
        ssA = sb("ssA", [P, NT, 8])

        banks = [ctx.enter_context(nc.psum_tensor(f"bank{i}", [P, 512], F32)) for i in range(8)]
        facc_ps = banks[4:8]

        plan = schedule()
        order = plan.jobs
        lows_by, lows_made = low_makers(plan.slabs)
        JOB = {k: i for i, k in enumerate(order)}
        WHERE, sums_at, bank_uses = place_jobs(order)
        MOE_BASE = len(order)
        assert JPER % NBANK == 0 and JBLOCK % NBANK == 0 and SPER % MRING == 0

        def bc3(ap, n):
            return ap.rearrange("p (a o) -> p a o", o=1).broadcast_to([ap.shape[0], ap.shape[1], n])

        def rep(ap, n):
            return ap.rearrange("p (o w) -> p o w", o=1).broadcast_to([ap.shape[0], n, ap.shape[1]])

        def h4(ap, w=128):
            return ap.rearrange("p (h d) -> p h d", d=w)

        def mslot(i):
            return ring[:, i] if i < RING else extra[:, i - RING]

        block = ctx.enter_context(nc.Block())

        @block.sync
        def _(sp):
            def source(key):
                kind = key[0]
                if kind in ("ada", "in"):
                    _, l, k, col = key
                    w = (w_ada if kind == "ada" else w_in)[l]
                    return w[k * 512:(k + 1) * 512, col:col + W512]
                if kind == "mg":
                    _, l, g, k, hf = key
                    return w_mg[l, g][k * 512:(k + 1) * 512, hf * W512:(hf + 1) * W512]
                if kind == "br":
                    _, l, g, hf = key
                    return w_br[l, g][:, hf * W512:(hf + 1) * W512]
                if kind == "wo":
                    _, l, k, hf = key
                    return w_o[l][k * 512:(k + 1) * 512, hf * W512:(hf + 1) * W512]
                if kind == "w2":
                    _, f, hf = key
                    return w2_d[0, f * W512:min((f + 1) * W512, D_FF), hf * W512:(hf + 1) * W512]
                _, k, f = key
                return (w1_d if kind == "w1" else w3_d)[0, k * 512:(k + 1) * 512, f * W512:min((f + 1) * W512, D_FF)]

            for n, (key, (kt, width), _) in enumerate(plan.slabs):
                if n == RING:
                    sp.dma_start(xs[:], x[0].rearrange("(t p) d -> p t d", p=P)).then_inc(S("x_landed"), 16)
                if n >= RING:
                    sp.wait_ge(S(lows_by[n - RING][0]), lows_by[n - RING][1])
                sp.dma_start(ring[:, n % RING, 0:kt, 0:width],
                             source(key).rearrange("(k p) n -> p k n", p=P)).then_inc(S(f"slab{n % RING}"), 16)
            def experts(blk):
                with sp.Fori(0, N_EXP) as e:
                    m = [0]

                    def mslab(w, r0, c0):
                        i = m[0]
                        m[0] += 1
                        who, n, per = low_part((i - MRING) % SPER)
                        back = per if i < MRING else 0
                        sp.wait_ge(S(who), e * per + (blk * N_EXP * per + per + n - back))
                        if i == RING:
                            sp.wait_ge(S("h_ready"), 2 * DEPTH * NT)
                        src = w[0, bass.ds(e, 1), r0:r0 + 512, c0:c0 + W512].rearrange("o (k p) n -> p (o k) n", p=P)
                        sp.dma_start(mslot(i % MRING), src).then_inc(S(f"mslab{i % MRING}"), 16)

                    for f in range(NF + 1):
                        if f < NF:
                            for w in (w1_e, w3_e):
                                for k in range(2):
                                    mslab(w, k * 512, f * W512)
                        if f > 0:
                            for hf in range(2):
                                mslab(w2_e, (f - 1) * W512, hf * W512)

            for who in lows_made:
                sp.wait_ge(S(who), lows_made[who])
            experts(0)
            sp.wait_ge(S("route_ready"), 1)
            with sp.If(sp.value_load(over[0:1, 0:1], min_val=0, max_val=1) > 0):
                experts(1)
            for t in range(NT):
                sp.wait_ge(S("y_ready"), t + 1)
                sp.dma_start(out[0, t * P:(t + 1) * P, :], xs[:, t, :]).then_inc(S("out_stored"), 16)
            sp.wait_ge(S("out_stored"), 16 * NT)

        @block.gpsimd
        def _(pool):
            k = [0]

            def chain(ins):
                k[0] += 1
                ins.then_inc(S("pool_chain"), 1)
                pool.wait_ge(S("pool_chain"), k[0])

            chain(pool.memset(ident[:], 0.0))
            chain(pool.affine_select(out=ident[:], in_=ident[:], compare_op=ALU.not_equal, fill=1.0, base=0,
                                     pattern=[[-1, P]], channel_multiplier=1))
            pool.sem_inc(S("ident_ready"), 1)
            chain(pool.memset(ones[:], 1.0))
            for i, v in enumerate((EPS, 1.0, LN_DKB, 0.0)):
                chain(pool.memset(cst[:, i:i + 1], v))
            chain(pool.memset(sgn16[:], 1.0))
            chain(pool.memset(sgn16[:, 4:8], -1.0))
            chain(pool.memset(sgn16[:, 12:16], -1.0))
            chain(pool.memset(cf16[:], -1.0))
            chain(pool.memset(bias16[:], 0.0))
            chain(pool.memset(mB[:], 0.0))
            chain(pool.memset(st[:], 0.0))
            pool.memset(cst[:, 4:8], 0.0).then_inc(S("consts_ready"), 1)
            pool.sem_inc(S("mlow_pool"), low_part(4)[2])
            chain(pool.memset(same[:], 1.0))
            sv = same[:].rearrange("p (q w) -> p q w", w=L)
            chain(pool.affine_select(out=sv, in_=sv, compare_op=ALU.is_ge, fill=0.0, base=0,
                                     pattern=[[-L, 2], [0, L]], channel_multiplier=1))
            chain(pool.affine_select(out=sv, in_=sv, compare_op=ALU.is_ge, fill=0.0, base=L - 1,
                                     pattern=[[L, 2], [0, L]], channel_multiplier=-1))
            chain(pool.affine_select(out=tri[:], in_=same[:], compare_op=ALU.is_ge, fill=0.0, base=0,
                                     pattern=[[1, P]], channel_multiplier=-1))
            chain(pool.affine_select(out=negL[:], in_=same[:], compare_op=ALU.is_ge, fill=0.0, base=0,
                                     pattern=[[-1, P]], channel_multiplier=1))
            chain(pool.affine_select(out=negS[:], in_=same[:], compare_op=ALU.is_ge, fill=0.0, base=-1,
                                     pattern=[[1, P]], channel_multiplier=-1))
            chain(pool.tensor_scalar(negI[:], tri[:], -1.0, -NEG, ALU.add, ALU.mult))
            chain(pool.tensor_scalar(negS[:], negS[:], -1.0, -NEG, ALU.add, ALU.mult))
            chain(pool.tensor_scalar(negL[:], negL[:], -1.0, -NEG, ALU.add, ALU.mult))
            chain(pool.memset(half[:], 1.0))
            chain(pool.affine_select(out=half[:], in_=half[:], compare_op=ALU.is_ge, fill=0.0, base=0,
                                     pattern=[[-L, 2], [0, P]], channel_multiplier=1))
            chain(pool.affine_select(out=half[:], in_=half[:], compare_op=ALU.is_ge, fill=0.0, base=L - 1,
                                     pattern=[[L, 2], [0, P]], channel_multiplier=-1))
            chain(pool.memset(lev_m[:], 0.0))
            for lev in range(6):
                b = 1 << lev
                q = P // (2 * b)
                v = lev_m[:, lev, :].rearrange("p (q w) -> p q w", w=2 * b)[:, :, b:2 * b]
                chain(pool.memset(v, 1.0))
                chain(pool.affine_select(out=v, in_=v, compare_op=ALU.is_ge, fill=0.0, base=0,
                                         pattern=[[-2 * b, q], [0, b]], channel_multiplier=1))
                chain(pool.affine_select(out=v, in_=v, compare_op=ALU.is_ge, fill=0.0, base=b - 1,
                                         pattern=[[2 * b, q], [0, b]], channel_multiplier=-1))
            chain(pool.memset(rst[:], 1.0))
            chain(pool.memset(rst[:].rearrange("p (q w) -> p q w", w=L)[:, :, 0:1], 0.0))
            chain(pool.memset(before[:], 1.0))
            chain(pool.affine_select(out=before[:], in_=before[:], compare_op=ALU.is_ge, fill=0.0, base=-1,
                                     pattern=[[1, P]], channel_multiplier=-1))
            chain(pool.memset(lower[:], 0.0))
            for i in range(1, 8):
                chain(pool.memset(lower[:, i, 0:i], 1.0))
            chain(pool.memset(comb[:], 0.0))
            chain(pool.memset(sel[:], 0.0))
            pool.memset(rank[:], 0.0).then_inc(S("masks_ready"), 1)

            for n, (key, (kt, width), _) in enumerate(plan.slabs):
                if lows_by[n][0] != "low_pool":
                    continue
                pool.wait_ge(S("high_ready"), n + 1)
                w = wsplit[:, n % SPLITS, :, 0:kt, 0:width]
                pool.tensor_tensor(w[:, 1], ring[:, n % RING, 0:kt, 0:width], w[:, 0].bitcast(F32), ALU.subtract) \
                    .then_inc(S("low_pool"), 1)
            pool.wait_ge(S("h_ready"), 2 * DEPTH * NT)
            for b in range(BLOCKS):
                pool.iota(slot_no[b], pattern=[[1, P]], base=b * CAP, channel_multiplier=0,
                          allow_small_or_imprecise_dtypes=True).then_inc(S("slots_ready"), 1)
            pool.memset(facc, 0.0).then_inc(S("slots_ready"), 1)

            def expert_block(blk):
                with pool.Fori(0, N_EXP) as e:
                    for i in range(SPER):
                        if low_part(i)[0] == "mlow_pool":
                            w = wsplit[:, (len(plan.slabs) + i) % SPLITS]
                            pool.wait_ge(S("mhigh_ready"), e * SPER + (blk * N_EXP * SPER + i + 1))
                            pool.tensor_tensor(w[:, 1], mslot(i % MRING), w[:, 0].bitcast(F32), ALU.subtract) \
                                .then_inc(S("mlow_pool"), 1)

            expert_block(0)
            pool.wait_ge(S("route_ready"), 1)
            with pool.If(pool.value_load(over[0:1, 0:1], min_val=0, max_val=1) > 0):
                expert_block(1)

        @block.tensor
        def _(pe):
            nj = [0]
            ns = [0]
            lows = [0]

            def open_bank(key):
                b, uses = WHERE[key]
                if uses > 0:
                    pe.wait_ge(S(f"bank_free{b}"), uses)
                return banks[b]

            def begin(key):
                i = nj[0]
                assert order[i] == key, (order[i], key)
                return open_bank(key)

            def end(ins):
                nj[0] += 1
                ins.then_inc(S("mm_done"), 1)

            def mm(o, a, b, start, stop, **kw):
                return pe.matmul(o, a, b, start=start, stop=stop, skip_group_check=True, **kw)

            def T(o, a):
                n = a.shape[0]
                return pe.transpose(o, a, ident[0:n, 0:n])

            def products(o, w, kt, operands, first, low, last):
                for kk in range(kt):
                    for xp in ((0,) if low else (0, 1)):
                        a, b = operands(w, kk, xp, 1 if low else 0)
                        ins = mm(o, a, b, first and kk == 0 and xp == 0, last and kk == kt - 1)
                return ins

            def group(keys, nslab, targets, pre=None):
                opened = []
                for i in range(len(keys)):
                    j = nj[0] + i
                    assert order[j] == keys[i], (order[j], keys[i])
                    opened.append(open_bank(keys[i]))
                if pre is not None:
                    pre(opened)
                for si in range(nslab):
                    n = ns[0]
                    ns[0] += 1
                    kt = plan.slabs[n][1][0]
                    w = wsplit[:, n % SPLITS]
                    pe.wait_ge(S("high_ready"), n + 1)
                    for job, cs, operands, starts in targets:
                        products(opened[job][:, cs], w, kt, lambda *a: operands(4 * si, *a), si == 0 and starts,
                                 False, False)
                    pe.wait_ge(S(lows_by[n][0]), lows_by[n][1])
                    for i, (job, cs, operands, starts) in enumerate(targets):
                        ins = products(opened[job][:, cs], w, kt, lambda *a: operands(4 * si, *a), False, True,
                                       si == nslab - 1)
                        if si == nslab - 1 and (i + 1 == len(targets) or targets[i + 1][0] != job):
                            end(ins)
                    if si < nslab - 1:
                        ins.then_inc(S("slab_mid"), 1)

            def by_tokens(x, t, wd=W512):
                return lambda k0, w, kk, xp, wp: (x[:, xp, k0 + kk, t * P:(t + 1) * P], w[:, wp, kk, 0:wd])

            def token_group(keys, x, nslab=2, wd=W512, pre=None):
                group(keys, nslab, [(t, slice(0, wd), by_tokens(x, t, wd), pre is None) for t in range(NT)], pre)

            def feature_group(keys):
                def operands(ft):
                    return lambda k0, w, kk, xp, wp: (w[:, wp, kk, ft * P:(ft + 1) * P], hT[:, xp, k0 + kk, :])
                group(keys, 2, [(ft // 2, slice((ft % 2) * SEQ, (ft % 2 + 1) * SEQ), operands(ft), ft % 2 == 0)
                                for ft in range(4)])

            def mod_products(l, piece, hf):
                def operands(k0, w, kk, xp, wp):
                    return cact[:, xp, k0 + kk:k0 + kk + 1].broadcast_to([P, P]), w[:, wp, kk, :]
                group([("mod", l, piece, hf)], 2, [(0, slice(0, W512), operands, True)])

            def transposes(key, src_of, n=4):
                o = begin(key)
                for i in range(n):
                    ins = T(o[:, i * P:(i + 1) * P], src_of(i))
                end(ins)

            pe.wait_ge(S("ident_ready"), 1)
            pe.wait_ge(S("c_landed"), 16)
            pe.transpose(banks[7][:, 0:8], crow[:], ident[0:8, 0:8]).then_inc(S("c_turned"), 1)
            pe.wait_ge(S("cact_low"), 1)
            for l in range(DEPTH):
                for piece in (0, 1):
                    for hf in range(2):
                        mod_products(l, piece, hf)
                pe.wait_ge(S("consts_ready"), 1)
                pe.wait_ge(S("small_landed"), SMALLS * (l + 1))
                o = begin(("cols", l))
                for i in range(16):
                    T(o[:, 4 * i:4 * i + 4], convr[:, i * P:(i + 1) * P])
                end(T(o[:, 64:66], bglar[:]))

                def make_hT(which):
                    for t in range(NT):
                        pe.wait_ge(S("h_ready"), (2 * l + which) * NT + t + 1)
                        for q in range(2):
                            transposes(("hT", l, which, t, q), lambda i: h[:, t, (4 * q + i) * P:(4 * q + i + 1) * P])
                    pe.wait_ge(S("hT_ready"), (2 * l + which + 1) * 4)

                make_hT(0)
                def narrow(o, a, b):
                    for k in range(KD):
                        for i, (xp, wp) in enumerate(((0, 0), (1, 0), (0, 1))):
                            ins = mm(o[0:b - a, 0:SEQ], wsm2[:, wp, k, a:b], hT[:, xp, k, :], k == 0 and i == 0,
                                     k == KD - 1 and i == 2)
                    return ins

                def to_tokens(key, src, n):
                    o = begin(key)
                    for t in range(NT):
                        ins = T(o[:, t * n:(t + 1) * n], src[:, t * P:(t + 1) * P])
                    end(ins)

                pe.wait_ge(S("wsm_ready"), l + 1)
                o = begin(("small", l))
                end(narrow(o, 0, 32))
                pe.wait_ge(S("small_T_ready"), l + 1)
                to_tokens(("turned", l), small_T, 32)
                def small_products():
                    pe.wait_ge(S("decay_ready"), l + 1)
                    pe.wait_ge(S("masks_ready"), 1)
                    o = begin(("cum", l))
                    for t in range(NT):
                        for i, m in enumerate((tri[:], same[:], half[:, 0, :], half[:, 1, :])):
                            ins = mm(o[:, (4 * t + i) * 16:(4 * t + i + 1) * 16], m, scal[:, SP, t, :], True, True)
                    end(ins)
                    o = begin(("la", l))
                    for f in range(2):
                        ins = mm(o[:, f * SEQ:(f + 1) * SEQ], wgla[:, f * P:(f + 1) * P], gTs[0:16, :], True, True)
                    end(ins)

                for i in range(3):
                    feature_group([("qkvA", l, 2 * i), ("qkvA", l, 2 * i + 1)])
                    if i == 0:
                        small_products()
                feature_group([("qkB", l, 0), ("qkB", l, 1)])
                pe.wait_ge(S("fA_ready"), (l + 1) * 12)
                for t in range(NT):
                    for i, name in enumerate(("TQ", "TK")):
                        transposes((name, l, t), lambda j: fA[:, 4 * i + j, t * P:(t + 1) * P])
                feature_group([("qkC", l, 0), ("qkC", l, 1)])
                for name in ("vB", "vC"):
                    token_group([(name, l, t) for t in range(NT)], hT)
                def row_matrix(key, where, mask, t):
                    o = begin(key)
                    if mask is not None:
                        for hh in range(H):
                            mm(o[:, hh * P:(hh + 1) * P], ident[:], mask[:], hh == 0, False)
                    for hh in range(H):
                        ins = mm(o[:, hh * P:(hh + 1) * P],
                                 scal[:, where[0], t, where[1] + hh:where[1] + hh + 1].broadcast_to([P, P]),
                                 ident[:], mask is None and hh == 0, hh == H - 1)
                    end(ins)

                def scores(key, kk, qq):
                    o = begin(key)
                    for hh in range(H):
                        ins = mm(o[:, hh * P:(hh + 1) * P], kk(hh), qq(hh), hh == 0, hh == H - 1)
                    end(ins)

                def by_halves(key, lhs, rhs, rw=slice(0, P)):
                    o = begin(key)
                    for i in range(2):
                        for hh in (i, i + 2):
                            ins = mm(o[rw, hh * P:(hh + 1) * P], lhs(hh), rhs(hh), True, True)
                        if i == 0:
                            ins.then_inc(S("low_half"), 1)
                            lows[0] += 1
                            pe.wait_ge(S("low_half"), lows[0])
                    end(ins)

                pe.wait_ge(S("zA_ready"), l + 1)
                for t in range(NT):
                    ts = slice(t * P, (t + 1) * P)
                    row_matrix(("R1", l, t), Z1, negS, t)
                    scores(("KK", l, t), lambda hh: fA[:, 4 + hh, ts], lambda hh: fA[:, 4 + hh, ts])
                    row_matrix(("R2", l, t), Z2, negI, t)
                    scores(("KQ", l, t), lambda hh: fA[:, 4 + hh, ts], lambda hh: fA[:, hh, ts])
                hd = lambda b, t, hh: b[:, t, hh * P:(hh + 1) * P]
                for t in range(NT):
                    pe.wait_ge(S("LB_ready"), l * 6 * NT + t + 1)
                    scores(("X", l, 0, t), lambda hh: hd(LB, t, hh), lambda hh: ident[:])
                for lev in range(1, 6):
                    for t in range(NT):
                        pe.wait_ge(S("LB_ready"), (l * 6 + lev) * NT + t + 1)
                        pe.wait_ge(S("D_ready"), (l * 5 + lev - 1) * NT + t + 1)
                        pe.wait_ge(S("DT_ready"), (l * 6 + lev - 1) * NT + t + 1)
                        scores(("X", l, lev, t), lambda hh: hd(LB, t, hh), lambda hh: hd(Dm, t, hh))
                    if lev < 5:
                        mod_products(l, *LEVEL_MODS[lev - 1])
                    if lev == 1:
                        pe.wait_ge(S("aj_ready"), l + 1)
                        for t in range(NT):
                            row_matrix(("RA", l, t), AJ, None, t)
                    for t in range(NT):
                        pe.wait_ge(S("X_ready"), (l * 5 + lev - 1) * NT + t + 1)
                        if lev < 5:
                            scores(("Y", l, lev, t), lambda hh: hd(DT, t, hh), lambda hh: hd(XB, t, hh))
                        scores(("YT", l, lev, t), lambda hh: hd(XB, t, hh), lambda hh: hd(DT, t, hh))
                for t in range(NT):
                    for i, name in ((4, "TK2"), (8, "TV")):
                        transposes((name, l, t), lambda j: fA[:, i + j, t * P:(t + 1) * P])
                for t in range(NT):
                    pe.wait_ge(S("DT_ready"), (l * 6 + 5) * NT + t + 1)
                    pe.wait_ge(S("kbg_ready"), l * NT + t + 1)
                    scores(("U", l, t), lambda hh: hd(DT, t, hh), lambda hh: hd(vb, t, hh))
                    scores(("WT", l, t), lambda hh: hd(kbg, t, hh), lambda hh: hd(DT, t, hh))
                hp = lambda hh: slice(64 * (hh % 2), 64 * (hh % 2) + 64)
                pe.wait_ge(S("fB_ready"), (l + 1) * 4)
                pe.wait_ge(S("gla_ready"), l + 1)
                pe.wait_ge(S("stabB_ready"), l + 1)
                for t in range(NT):
                    ts = slice(t * P, (t + 1) * P)
                    transposes(("TKB", l, t), lambda i: fB[:, 2 + i, ts], n=2)
                    row_matrix(("RB", l, t), NZ, negI, t)
                    by_halves(("KQB", l, t), lambda hh: fB[hp(hh), 2 + hh // 2, ts], lambda hh: fB[hp(hh), hh // 2, ts])
                    by_halves(("KQC", l, t), lambda hh: fC[hp(hh), 2 + hh // 2, ts], lambda hh: fC[hp(hh), hh // 2, ts])
                    transposes(("TKC", l, t), lambda i: keT[:, i, ts], n=2)
                pe.wait_ge(S("scan_ready"), l + 1)
                for n in range(NCH):
                    t, r = n // 2, n % 2
                    rw = slice(64 * r, 64 * r + 64)
                    tk = slice(n * L, (n + 1) * L)
                    pe.wait_ge(S("SA_ready"), l * NCH + n + 1)
                    o = begin(("P1", l, n))
                    for hh in range(H):
                        ins = mm(o[rw, hh * P:(hh + 1) * P], wT[:, t, hh * P + 64 * r:hh * P + 64 * r + 64],
                                 SA[:, hh * P:(hh + 1) * P], True, True)
                    end(ins)
                    o = begin(("P2", l, n))
                    for hh in range(H):
                        ins = mm(o[rw, hh * P:(hh + 1) * P], fA[:, hh, tk], SA[:, hh * P:(hh + 1) * P], True, True)
                    end(ins)
                    pe.wait_ge(S("SB_ready"), l * NCH + n + 1)
                    for p in range(2):
                        o = begin((f"QB{p}", l, n))
                        for i in range(2):
                            ins = mm(o[rw, i * 129:(i + 1) * 129], fB[64 * p:64 * p + 64, i, tk],
                                     SB[64 * p:64 * p + 64, i, :], True, True)
                        end(ins)
                    o = begin(("KVB", l, n))
                    for hh in range(H):
                        ins = mm(o[hp(hh), (hh // 2) * 129:(hh // 2 + 1) * 129], kw[rw, t, hh * 64:(hh + 1) * 64],
                                 vB[rw, t, hh, :], True, True)
                    end(ins)
                    pe.wait_ge(S("delta_ready"), l * NCH + n + 1)
                    o = begin(("P3", l, n))
                    for hh in range(H):
                        ins = mm(o[:, hh * P:(hh + 1) * P], kend[rw, t, hh * P:(hh + 1) * P],
                                 UU[rw, t, hh * P:(hh + 1) * P], True, True)
                    end(ins)
                    pe.wait_ge(S("SC_ready"), l * NCH + n + 1)
                    by_halves(("QC", l, n), lambda hh: qg[hp(hh), hh // 2, tk], lambda hh: SC[hp(hh), hh // 2, :], rw)
                    o = begin(("KVC", l, n))
                    for hh in range(H):
                        ins = mm(o[hp(hh), (hh // 2) * P:(hh // 2 + 1) * P], keC[rw, t, hh * 64:(hh + 1) * 64],
                                 vC[rw, t, hh * P:(hh + 1) * P], True, True)
                    end(ins)
                    if n == 0:
                        token_group([("oB", l, i) for i in range(NT)], hT)
                for t in range(NT):
                    scores(("OA", l, t), lambda hh: hd(AT, t, hh), lambda hh: hd(UU, t, hh))
                    for p in range(2):
                        o = begin((f"OB{p}", l, t))
                        for i in range(2):
                            ins = mm(o[:, i * 129:(i + 1) * 129], hd(WB, t, p + 2 * i), vB[:, t, p + 2 * i, :],
                                     True, True)
                        end(ins)
                    scores(("OC", l, t), lambda hh: hd(AC, t, hh), lambda hh: hd(vC, t, hh))
                for name in ("zA", "zC"):
                    token_group([(name, l, t) for t in range(NT)], hT)
                for piece in (2, 5):
                    for hf in range(2):
                        mod_products(l, piece, hf)
                ysrc = (oA, nB, oC)

                def turn_y(g):
                    for t in range(NT):
                        pe.wait_ge(S("y_branch"), l * 6 + 2 * g + t + 1)
                        transposes(("yT", l, g, t), lambda i: ysrc[g][:, t, i * P:(i + 1) * P])

                turn_y(0)
                turn_y(1)
                pe.wait_ge(S("bmg_landed"), 48 * (l + 1))
                for g in range(3):
                    for hf in range(2):
                        def bias(opened):
                            for t in range(NT):
                                mm(opened[t][:], ones[32 * g:32 * g + 1, :],
                                   bmg[32 * g:32 * g + 1, hf * W512:(hf + 1) * W512], True, False)

                        token_group([("mg", l, g, hf, t) for t in range(NT)], hT, pre=bias)
                        pe.wait_ge(S("yT_ready"), l * 6 + 2 * g + 2)
                        token_group([("br", l, g, hf, t) for t in range(NT)], yT[g], nslab=1)
                    if g == 0:
                        turn_y(2)
                pe.wait_ge(S("merged_ready"), (l + 1) * 12)
                for t in range(NT):
                    for q in range(2):
                        transposes(("mT", l, t, q), lambda i: merged[:, t, (4 * q + i) * P:(4 * q + i + 1) * P])
                pe.wait_ge(S("mT_ready"), (l + 1) * 4)
                for hf in range(2):
                    token_group([("wo", l, hf, t) for t in range(NT)], mT)
                make_hT(1)
                if l == 0:
                    widths = ffn_widths(D_FF)

                    def up(name, f):
                        token_group([("ffn", l, name, f, t) for t in range(NT)], hT, wd=widths[f])

                    def turn(f):
                        for t in range(NT):
                            pe.wait_ge(S("g_ready"), f * NT + t + 1)
                            o = begin(("ffn", l, "gT", f, t))
                            for i in range(widths[f] // P):
                                ins = T(o[:, i * P:(i + 1) * P], fg[t][:, i * P:(i + 1) * P])
                            end(ins)

                    def down(f):
                        kt = widths[f] // P
                        pe.wait_ge(S("gT_ready"), f * NT + 2)
                        if f == 0:
                            for b in range(NBANK, ALL_BANKS):
                                pe.wait_ge(S(f"bank_free{b}"), sums_at[b])
                        for hf in range(2):
                            n = ns[0]
                            ns[0] += 1
                            w = wsplit[:, n % SPLITS]
                            for low in (False, True):
                                who, count = lows_by[n] if low else ("high_ready", n + 1)
                                pe.wait_ge(S(who), count)
                                for t in range(NT):
                                    ins = products(facc_ps[2 * t + hf][:], w, kt,
                                                   lambda w, kk, xp, wp: (fgT[t][:, xp, kk, :], w[:, wp, kk, :]),
                                                   f == 0 and not low, low, f == len(widths) - 1 and low)
                            ins.then_inc(S("down_done"), 1)

                    for f in range(len(widths) + 1):
                        if f < len(widths):
                            up("w1", f)
                        if f > 0:
                            turn(f - 1)
                        if f < len(widths):
                            up("w3", f)
                        if f > 0:
                            down(f - 1)
                else:
                    o = begin(("logitsT", l))
                    end(narrow(o, 32, 40))
                    pe.wait_ge(S("logits_T_ready"), 1)
                    to_tokens(("router", l), logits_T, 8)
                    pe.wait_ge(S("sel_ready"), 1)
                    o = begin(("rank", l))
                    mm(o[:, 0:8], before[:], sel[:, 0, 0:8], True, True)
                    mm(o[:, 8:16], before[:], sel[:, 1, 0:8], True, False)
                    mm(o[:, 8:16], ones[:], sel[:, 0, 0:8], False, True)
                    mm(o[:, 16:24], ones[:], sel[:, 0, 0:8], True, False)
                    end(mm(o[:, 16:24], ones[:], sel[:, 1, 0:8], False, True))
            assert nj[0] == MOE_BASE
            assert ns[0] == len(plan.slabs)

            def expert_block(blk):
                jb = MOE_BASE + blk * JBLOCK + FIRST

                def mbegin(e, i):
                    b = i % NBANK
                    pe.wait_ge(S(f"bank_free{b}"),
                               e * (JPER // NBANK) + (bank_uses[b] + (blk * JBLOCK + FIRST + i) // NBANK))
                    return banks[i % NBANK]

                def scatter(e, i0):
                    pe.wait_ge(S("ey_ready"), e + (blk * (N_EXP + 1) + 1))
                    for t in range(NT):
                        for hf in range(2):
                            o = mbegin(e, i0 + 2 * t + hf)
                            mm(o[:], pwT[:, t * P:(t + 1) * P], y[:, hf * W512:(hf + 1) * W512], True, True) \
                                .then_inc(S("mm_done"), 1)

                def gather(o, ks):
                    for j, k in enumerate(ks):
                        for t in range(NT):
                            ins = mm(o[:, j * P:(j + 1) * P], h[:, t, k * P:(k + 1) * P], pick[:, t, :],
                                     t == 0, t == NT - 1)
                    ins.then_inc(S("mm_done"), 1)

                pe.wait_ge(S("pick_ready"), blk * (N_EXP + 1) + 1)
                for q in range(FIRST):
                    gather(mbegin(0, q - FIRST), (2 * q, 2 * q + 1))
                with pe.Fori(0, N_EXP) as e:
                    got = [0]

                    def mpasses(o, operands, first, last):
                        i = got[0]
                        got[0] += 1
                        w = wsplit[:, (len(plan.slabs) + i) % SPLITS]
                        pe.wait_ge(S("mhigh_ready"), e * SPER + (blk * N_EXP * SPER + i + 1))
                        products(o, w, 4, operands, first, False, False)
                        who, n, per = low_part(i)
                        pe.wait_ge(S(who), e * per + (blk * N_EXP * per + per + n))
                        return products(o, w, 4, operands, False, True, last)

                    def mup(name, f):
                        o = mbegin(e, MJOB[(name, f)])
                        for k0 in (0, 4):
                            ins = mpasses(o[:], lambda w, kk, xp, wp: (xgT[:, xp, k0 + kk, :], w[:, wp, kk, :]),
                                          k0 == 0, k0 == 4)
                            ins.then_inc(S("mslab_mid" if k0 == 0 else "mm_done"), 1)

                    def mturn(f):
                        pe.wait_ge(S("eg_ready"), e * NF + (blk * N_EXP * NF + f + 3))
                        o = mbegin(e, MJOB[("gT", f)])
                        for i in range(4):
                            ins = T(o[:, i * P:(i + 1) * P], fg[f % 2][:, i * P:(i + 1) * P])
                        ins.then_inc(S("mm_done"), 1)

                    def mdown(f):
                        pe.wait_ge(S("egT_ready"), e * NF + (blk * N_EXP * NF + f + 3))
                        if f == 0:
                            pe.wait_ge(S("ybank_free"), e + (blk * (N_EXP + 1) + 1))
                        for hf in range(2):
                            mpasses(facc_ps[hf][:], lambda w, kk, xp, wp: (fgT[f % 2][:, xp, kk, :], w[:, wp, kk, :]),
                                    f == 0, f == NF - 1).then_inc(S("edown_done"), 1)

                    pe.wait_ge(S("xgT_ready"), e * 2 + (blk * (N_EXP * 2 + FIRST) + FIRST))
                    for f in range(NF + 1):
                        if f < NF:
                            mup("w1", f)
                        if f == 0:
                            scatter(e, MJOB[("sc", 0, 0)])
                            o = mbegin(e, MJOB[("pwt",)])
                            for t in range(NT):
                                ins = T(o[:, t * P:(t + 1) * P], pickw[:, t, :])
                            ins.then_inc(S("mm_done"), 1)
                        if f > 0:
                            mturn(f - 1)
                        if f < NF:
                            mup("w3", f)
                        if f == NF - 1:
                            pe.wait_ge(S("pick_ready"), e + (blk * (N_EXP + 1) + 2))
                            for q in range(2):
                                gather(mbegin(e, MJOB[("xg", q)]), range(4 * q, 4 * q + 4))
                        if f > 0:
                            mdown(f - 1)
                pe.wait_ge(S("pwT_ready"), blk * (N_EXP + 1) + N_EXP + 1)
                scatter(N_EXP, 0)

            pe.sem_inc(S("edown_done"), 2 * NF)
            pe.sem_inc(S("mslab_mid"), 2 * NF)
            expert_block(0)
            pe.wait_ge(S("route_ready"), 1)
            with pe.If(pe.value_load(over[0:1, 0:1], min_val=0, max_val=1) > 0):
                expert_block(1)

        @block.scalar
        def _(act):
            k = [0]

            def chain(ins):
                k[0] += 1
                ins.then_inc(S("act_chain"), 1)
                act.wait_ge(S("act_chain"), k[0])

            hi = [0]

            def slabs_ahead(count):
                while hi[0] < min(count, len(plan.slabs)):
                    n = hi[0]
                    hi[0] += 1
                    kt, width = plan.slabs[n][1]
                    act.wait_ge(S(f"slab{n % RING}"), 16 * (n // RING + 1))
                    if n >= SPLITS:
                        act.wait_ge(S(plan.slabs[n - SPLITS][2][0]), plan.slabs[n - SPLITS][2][1])
                    act.activation(wsplit[:, n % SPLITS, 0, 0:kt, 0:width], ring[:, n % RING, 0:kt, 0:width],
                                   ACT.Copy).then_inc(S("high_ready"), 1)

            def ahead(key):
                slabs_ahead(plan.need[key] + 2)

            def job(key):
                ahead(key)
                act.wait_ge(S("mm_done"), JOB[key] + 1)
                return banks[WHERE[key][0]]

            def free(key, ins):
                ins.then_inc(S(f"bank_free{WHERE[key][0]}"), 1)

            def done(name, ins, n=1):
                ins.then_inc(S(name), n)

            def rstd(dst, src, div):
                chain(act.activation(dst, src, ACT.Ln, bias=cst[:, 0:1], scale=1.0 / div))
                return act.activation(dst, dst, ACT.Exp, scale=-0.5)

            def rms(parts):
                for t, q, ready in parts:
                    if ready is not None:
                        act.wait_ge(S(ready[0]), ready[1])
                    chain(act.activation(h[:, t, q * 512:(q + 1) * 512], xs[:, t, q * 512:(q + 1) * 512], ACT.Square,
                                         accum_out=st[:, 4 * t + q:4 * t + q + 1]))
                for t in range(NT):
                    chain(act.activation(st[:, 4 * t + 2:4 * t + 3], st[:, 4 * t:4 * t + 1], ACT.Identity,
                                         bias=st[:, 4 * t + 1:4 * t + 2]))
                both = st[:, 0:4 * NT].rearrange("p (t a) -> p t a", a=4)
                done("rstd_ready", rstd(both[:, :, 3], both[:, :, 2], D))

            def load(name, dst, src):
                act.dma_start(dst, src).then_inc(S(name), 16)

            load("c_landed", crow[:], c[0].rearrange("(k p) -> k p", p=P))
            slabs_ahead(2)
            def small_loads(l):
                def small(dst, src):
                    load("small_landed", dst, src)
                small(grow, g_mix[l:l + 1, :].broadcast_to([P, D]))
                for s in range(2):
                    small(mod[:, s, :], b_ada[l:l + 1, s * D:(s + 1) * D].broadcast_to([P, D]))
                small(convr[:, 0:1536], conv_a[l])
                small(convr[:, 1536:2048], conv_b[l])
                small(bglar[:], b_gla[l].rearrange("(k p) -> k p", p=P))
                win = w_in[l].rearrange("(k p) n -> p k n", p=P)
                small(wsm[:, :, 16:24], win[:, :, AB:AB + 8])
                small(wsm[:, :, 24:32], win[:, :, IF:IF + 8])
                small(wsm[:, :, 0:16], win[:, :, GC:GC + 16])
                small(wsm[:, :, 32:40], w_router[0].rearrange("(k p) n -> p k n", p=P))
                small(wgla[:], w_gla2[l])
                small(bias16[:, 0:4], dt_bias[l:l + 1, :].broadcast_to([P, 4]))
                small(bias16[:, 8:12], b_i[l:l + 1, :].broadcast_to([P, 4]))
                small(bias16[:, 12:16], b_f[l:l + 1, :].broadcast_to([P, 4]))
                small(cf16[:, 0:4], a_log[l:l + 1, :].broadcast_to([P, 4]))
                small(normr[:, 0, :], norm_a[l:l + 1, :].broadcast_to([P, P]))
                small(normr[:, 1, :], norm_b[l:l + 1, :].broadcast_to([P, P]))
                small(normr[:, 2, :], norm_c[l:l + 1, :].broadcast_to([P, P]))
                small(brt[:], b_router[0:1, :].broadcast_to([P, 8]))

            act.wait_ge(S("c_turned"), 1)
            chain(act.activation(cactf[:], banks[7][:, 0:8], ACT.Silu))
            done("cact_ready", act.activation(cact[:, 0, :], cactf[:], ACT.Copy))
            act.wait_ge(S("consts_ready"), 1)
            small_loads(0)
            for l in range(DEPTH):
                if l == 0:
                    act.wait_ge(S("x_landed"), 16)
                    act.wait_ge(S("cact_ready"), 1)
                else:
                    slabs_ahead(plan.need[("ffn", l - 1, "gT", len(ffn_widths(D_FF)) - 1, NT - 1)] + 4)
                    act.wait_ge(S("x_ready"), NT * l)
                    small_loads(l)
                ahead(("mod", l, 0, 1))
                rms([(t, q, None) for t in range(NT) for q in range(2)])
                act.wait_ge(S("small_landed"), SMALLS * (l + 1))
                chain(act.activation(cf16[:, 0:4], cf16[:, 0:4], ACT.Exp))
                done("cf_exp", act.activation(cf16[:, 0:4], cf16[:, 0:4], ACT.Copy, scale=-1.0))
                done("wsm_high", act.activation(wsm2[:, 0], wsm[:], ACT.Copy))

                def copy_hT(which):
                    for t in range(NT):
                        for q in range(2):
                            b = job(("hT", l, which, t, q))
                            done("hT_high", act.activation(hT[:, 0, 4 * q:4 * q + 4, t * P:(t + 1) * P], h4(b[:]),
                                                           ACT.Copy))
                copy_hT(0)
                act.wait_ge(S("h_ready"), (2 * l + 1) * NT)
                for s in range(2):
                    load("ffn_rows_landed", mod[:, s, :],
                         b_ada[l:l + 1, (3 + s) * D:(4 + s) * D].broadcast_to([P, D]))
                ahead(("small", l))
                act.wait_ge(S("abs_ready"), 2 * l + 1)
                chain(act.activation(sc(EX), sc(AB_), ACT.Exp, scale=-1.0))
                done("softplus_ln", act.activation(sc(LG), sc(EX), ACT.Ln, bias=cst[:, 1:2]))
                act.wait_ge(S("decay_ready"), l + 1)
                done("beta_ready", act.activation(at(BETA), sc(SP, 4, 4), ACT.Exp))
                ahead(("la", l))
                act.wait_ge(S("abs_ready"), 2 * l + 2)
                chain(act.activation(tc1, tc1, ACT.Exp, scale=-1.0))
                done("softplus_ln", act.activation(tc1, tc1, ACT.Ln, bias=cst[:, 1:2]))
                for i in range(6):
                    ahead(("qkvA", l, i))
                    act.wait_ge(S("conv_ready"), l * 16 + 2 * i + 2)
                    done("fA_ready", act.activation(fA[:, 2 * i:2 * i + 2, :], fA[:, 2 * i:2 * i + 2, :], ACT.Silu), 2)
                for i in range(2):
                    ahead(("qkB", l, i))
                    act.wait_ge(S("conv_ready"), l * 16 + 12 + 2 * i + 2)
                    done("fB_ready", act.activation(fB[:, 2 * i:2 * i + 2, :], fB[:, 2 * i:2 * i + 2, :], ACT.Silu), 2)
                for t in range(NT):
                    b = job(("TQ", l, t))
                    if t:
                        act.wait_ge(S("sq_used"), l * 4 + 2 * t - 1)
                    chain(act.activation(sq[0], b[:], ACT.Square))
                    act.sem_inc(S(f"bank_free{WHERE[('TQ', l, t)][0]}"), 1)
                    act.sem_inc(S("sq_ready"), 1)
                    b = job(("TK", l, t))
                    if t:
                        act.wait_ge(S("sq_used"), l * 4 + 2 * t)
                    chain(act.activation(sq[1], b[:], ACT.Square))
                    act.sem_inc(S(f"bank_free{WHERE[('TK', l, t)][0]}"), 1)
                    act.sem_inc(S("sq_ready"), 1)
                ahead(("qkC", l, 0))
                act.wait_ge(S("ss_ready"), l + 1)
                done("lnss_ready", act.activation(ssA[:], ssA[:], ACT.Ln, bias=cst[:, 0:1]))
                for i in range(2):
                    b = job(("qkC", l, i))
                    chain(act.activation(fC[:, 2 * i:2 * i + 2, :].rearrange("p a b -> p (a b)"), b[:], ACT.Copy,
                                         scale=0.125 if i == 0 else 1.0))
                    act.sem_inc(S(f"bank_free{WHERE[('qkC', l, i)][0]}"), 1)
                act.sem_inc(S("fC_ready"), 1)
                ahead(("vB", l, 0))
                act.wait_ge(S("glaexp_in"), l + 1)
                chain(act.activation(tc2, uc, ACT.Exp, scale=-1.0))
                chain(act.activation(uc, uc, ACT.Exp))
                chain(act.activation(tc1, tc1, ACT.Exp))
                chain(act.activation(bc, bc, ACT.Exp))
                act.sem_inc(S("glaexp_ready"), 1)
                for name in ("vB", "vC"):
                    for t in range(NT):
                        b = job((name, l, t))
                        dst = vB[:, t, :, 0:128] if name == "vB" else h4(vC[:, t, :])
                        chain(act.activation(dst, h4(b[:]), ACT.Copy))
                        act.sem_inc(S(f"bank_free{WHERE[(name, l, t)][0]}"), 1)
                        act.sem_inc(S("tok_ready"), 1)
                act.wait_ge(S("zA_ready"), l + 1)
                chain(act.activation(sc(10, 0, 12)[:, :, 0:8], sc(7, 0, 8), ACT.Exp))
                chain(act.activation(at(EZE), at(ZE), ACT.Exp))
                chain(act.activation(geA[:], tot2[:, :, 0:4], ACT.Exp))
                act.sem_inc(S("expA_ready"), 1)
                for t in range(NT):
                    for name, dst in (("R1", LT), ("R2", AT)):
                        b = job((name, l, t))
                        for hh in range(H):
                            ins = act.activation(dst[:, t, hh * P:(hh + 1) * P], b[:, hh * P:(hh + 1) * P], ACT.Exp,
                                                 bias=scal[:, BJ[0], t, BJ[1] + hh:BJ[1] + hh + 1])
                            if hh < H - 1:
                                ins.then_inc(S("act_chain"), 1)
                                k[0] += 1
                            else:
                                chain(ins)
                        act.sem_inc(S(f"bank_free{WHERE[(name, l, t)][0]}"), 1)
                        act.sem_inc(S("decayA_ready"), 1)
                ahead(("mod", l, *LEVEL_MODS[2]))
                act.wait_ge(S("stabB_ready"), l + 1)
                chain(act.activation(at(SI), at(T0), ACT.Exp))
                chain(act.activation(at(THR), at(T1), ACT.Exp))
                chain(act.activation(at(KWS), at(MN), ACT.Exp, bias=cst[:, 2:3]))
                chain(act.activation(spB[:], spB[:], ACT.Exp))
                act.sem_inc(S("expB_ready"), 1)
                ahead(("X", l, LEVELS - 1, 0))
                for t in range(NT):
                    b = job(("WT", l, t))
                    chain(act.activation(wT[:, t, :], b[:], ACT.Copy))
                    act.sem_inc(S(f"bank_free{WHERE[('WT', l, t)][0]}"), 1)
                    act.sem_inc(S("wT_ready"), 1)
                for t in range(NT):
                    b = job(("RB", l, t))
                    for hh in range(H):
                        chain(act.activation(WB[:, t, hh * P:(hh + 1) * P], b[:, hh * P:(hh + 1) * P], ACT.Exp,
                                             bias=scal[:, BJB[0], t, BJB[1] + hh:BJB[1] + hh + 1]))
                    act.sem_inc(S(f"bank_free{WHERE[('RB', l, t)][0]}"), 1)
                    act.sem_inc(S("decayB_ready"), 1)
                def gate(name, dst, fn):
                    for t in range(NT):
                        b = job((name, l, t))
                        chain(act.activation(dst[:, t, :], b[:], fn))
                        act.sem_inc(S(f"bank_free{WHERE[(name, l, t)][0]}"), 1)
                        act.sem_inc(S("gate_ready"), 1)

                gate("oB", oBg, ACT.Sigmoid)
                job(("OC", l, NT - 1))
                for piece in (2, 5):
                    load("gate_rows_landed", gates[piece],
                         b_ada[l:l + 1, piece * D:(piece + 1) * D].broadcast_to([P, D]))
                for i, (g, o) in enumerate(((0, oA), (2, oC), (1, nB))):
                    act.wait_ge(S("o_ready"), l * 3 + i + 1)
                    done("osq_ready", act.activation(osq[g], o.rearrange("p t n -> p (t n)"), ACT.Square))
                act.wait_ge(S("oss_ready"), l + 1)
                done("orstd_ready", rstd(oss, oss, P))
                gate("zA", zA, ACT.Silu)
                gate("zC", zC, ACT.Silu)
                ahead(("mod", l, 5, 1))
                act.wait_ge(S("y_branch"), l * 6 + 4)
                load("gffn_landed", grow, g_ffn[l:l + 1, :].broadcast_to([P, D]))
                for g in range(3):
                    load("bmg_landed", bmg[32 * g:32 * g + 1, :], b_mg[l, g:g + 1, :])

                def y_high(g):
                    for t in range(NT):
                        b = job(("yT", l, g, t))
                        done("yT_high", act.activation(yT[g][:, 0, :, t * P:(t + 1) * P], h4(b[:]), ACT.Copy))

                y_high(0)
                y_high(1)
                m = 0
                for g in range(3):
                    for hf in range(2):
                        for t in range(NT):
                            key = ("mg", l, g, hf, t)
                            b = job(key)
                            if m >= 2:
                                act.wait_ge(S("merged_ready"), l * 12 + m - 1)
                            chain(act.activation(mg_s[m % 2], b[:], ACT.Sigmoid))
                            act.sem_inc(S(f"bank_free{WHERE[key][0]}"), 1)
                            act.sem_inc(S("mgate_ready"), 1)
                            m += 1
                    if g == 0:
                        y_high(2)
                for t in range(NT):
                    for q in range(2):
                        key = ("mT", l, t, q)
                        b = job(key)
                        done("mT_high", act.activation(mT[:, 0, 4 * q:4 * q + 4, t * P:(t + 1) * P], h4(b[:]),
                                                       ACT.Copy))
                ahead(("wo", l, 1, 1))
                rms([(t, hf, ("x_half", (2 * l + hf) * NT + t + 1)) for hf in range(2) for t in range(NT)])
                copy_hT(1)
                if l == 0:
                    widths = ffn_widths(D_FF)

                    def gT_copy(f):
                        for t in range(NT):
                            key = ("ffn", l, "gT", f, t)
                            b = job(key)
                            if f > 0:
                                act.wait_ge(S("down_done"), 2 * f)
                            kt = widths[f] // P
                            done("gT_high", act.activation(fgT[t][:, 0, 0:kt, :],
                                                           b[:, 0:widths[f]].rearrange("p (a b) -> p a b", b=P),
                                                           ACT.Copy))

                    for f in range(len(widths) + 1):
                        if f < len(widths):
                            for t in range(NT):
                                key = ("ffn", l, "w1", f, t)
                                b = job(key)
                                if f > 0:
                                    act.wait_ge(S("g_ready"), (f - 1) * NT + t + 1)
                                done("silu_ready", act.activation(fs[t][:, 0:widths[f]], b[:, 0:widths[f]], ACT.Silu))
                                act.wait_ge(S("silu_ready"), f * NT + t + 1)
                                act.sem_inc(S(f"bank_free{WHERE[key][0]}"), 1)
                        if f > 0:
                            gT_copy(f - 1)
            act.wait_ge(S("route_in"), 1)
            done("route_exp", act.activation(comb[:, :, 0:8], comb[:, :, 0:8], ACT.Exp))
            act.wait_ge(S("h_ready"), 2 * DEPTH * NT)
            load("gfinal_landed", mod[:, 0, :], g_final.rearrange("(o d) -> o d", o=1).broadcast_to([P, D]))
            assert hi[0] == len(plan.slabs)

            def expert_block(blk):
                jb = MOE_BASE + blk * JBLOCK + FIRST
                fb = blk * N_EXP * NF

                def take_y(e):
                    act.wait_ge(S("edown_done"), e * (2 * NF) + (2 * fb + 2 * NF))
                    for hf in range(2):
                        act.activation(y[:, hf * W512:(hf + 1) * W512], facc_ps[hf][:], ACT.Copy) \
                            .then_inc(S("ey_half"), 1)
                    act.wait_ge(S("ey_half"), e * 2 + (blk * (N_EXP + 1) * 2 + 2))
                    act.sem_inc(S("ybank_free"), 1)
                    act.sem_inc(S("ey_ready"), 1)

                act.wait_ge(S("y_zero"), 2 * blk + 2)
                for q in range(FIRST):
                    act.wait_ge(S("mm_done"), jb - FIRST + q + 1)
                    act.activation(xgT[:, 0, 2 * q:2 * q + 2, :], h4(banks[q][:, 0:2 * P]), ACT.Copy) \
                        .then_inc(S("xg_high"), 1)
                with act.Fori(0, N_EXP) as e:
                    def mjob(i):
                        act.wait_ge(S("mm_done"), e * JPER + (jb + i + 1))
                        return banks[i % NBANK]

                    def mfree(i):
                        act.sem_inc(S(f"bank_free{i % NBANK}"), 1)

                    cur = [0]

                    def mhigh(upto):
                        while cur[0] <= min(upto, SPER - 1):
                            i = cur[0]
                            cur[0] += 1
                            act.wait_ge(S(f"mslab{i % MRING}"), e * (16 * SPER // MRING)
                                        + (blk * N_EXP * 16 * SPER // MRING + 16 * (i // MRING + 1)))
                            kind, n = moe_free(i - SPLITS)
                            if kind == "mm_done":
                                act.wait_ge(S(kind), e * JPER + (jb + n))
                            else:
                                act.wait_ge(S(kind), e * (2 * NF) + (blk * N_EXP * 2 * NF + 2 * NF + n))
                            act.activation(wsplit[:, (len(plan.slabs) + i) % SPLITS, 0], mslot(i % MRING), ACT.Copy) \
                                .then_inc(S("mhigh_ready"), 1)

                    mhigh(1)
                    take_y(e)
                    for f in range(NF + 1):
                        if f < NF:
                            mhigh(moe_slab("w1", f) + 3)
                            i = MJOB[("w1", f)]
                            b = mjob(i)
                            act.wait_ge(S("eg_ready"), e * NF + (fb + f + 1))
                            act.activation(fs[f % 2], b[:], ACT.Silu).then_inc(S("esilu_ready"), 1)
                            act.wait_ge(S("esilu_ready"), e * NF + (fb + f + 1))
                            mfree(i)
                        if f == 0:
                            i = MJOB[("pwt",)]
                            b = mjob(i)
                            act.activation(pwT, b[:, 0:SEQ], ACT.Copy).then_inc(S("pwT_ready"), 1)
                            act.wait_ge(S("pwT_ready"), e + (blk * (N_EXP + 1) + 2))
                            mfree(i)
                        if f > 0:
                            i = MJOB[("gT", f - 1)]
                            b = mjob(i)
                            act.wait_ge(S("edown_done"), e * (2 * NF) + (2 * fb + 2 * NF + 2 * (f - 3) + 2))
                            act.activation(fgT[(f - 1) % 2][:, 0], h4(b[:]), ACT.Copy).then_inc(S("egT_high"), 1)
                        if f < NF - 1:
                            mhigh(moe_slab("w1", f) + (5 if f else 3) + 2)
                        if f == NF - 1:
                            mhigh(SPER - 3)
                            for q in range(2):
                                b = mjob(MJOB[("xg", q)])
                                act.activation(xgT[:, 0, 4 * q:4 * q + 4, :], h4(b[:]), ACT.Copy) \
                                    .then_inc(S("xg_high"), 1)
                            mhigh(SPER - 1)
                take_y(N_EXP)

            expert_block(0)
            act.wait_ge(S("route_ready"), 1)
            with act.If(act.value_load(over[0:1, 0:1], min_val=0, max_val=1) > 0):
                expert_block(1)
            rms([(t, q, ("x_ready", NT * (DEPTH - 1) + t + 1)) for t in range(NT) for q in range(2)])

        @block.vector
        def _(v):
            k = [0]

            def chain(ins):
                k[0] += 1
                ins.then_inc(S("dve_chain"), 1)
                v.wait_ge(S("dve_chain"), k[0])

            def apart(*instructions):
                for ins in instructions:
                    k[0] += 1
                    ins.then_inc(S("dve_chain"), 1)
                v.wait_ge(S("dve_chain"), k[0])

            def job(key):
                v.wait_ge(S("mm_done"), JOB[key] + 1)
                return banks[WHERE[key][0]]

            def fr(key):
                v.sem_inc(S(f"bank_free{WHERE[key][0]}"), 1)

            def tt(o, a, b, op=ALU.mult):
                return v.tensor_tensor(o, a, b, op)

            def gain():
                chain(v.scalar_tensor_tensor(mod[:, 1, :], mod[:, 1, :], 1.0, grow, ALU.add, ALU.mult))

            def normalise(l, which):
                v.wait_ge(S("rstd_ready"), 2 * l + which + 1)
                for t in range(NT):
                    chain(v.scalar_tensor_tensor(h[:, t, :], xs[:, t, :], st[:, 4 * t + 3:4 * t + 4], mod[:, 1, :],
                                                 ALU.mult, ALU.mult))
                    chain(tt(h[:, t, :], h[:, t, :], mod[:, 0, :], ALU.add))
                    v.sem_inc(S("h_ready"), 1)

            def mod_low(l, piece, hf):
                for n, (key, _, _) in enumerate(plan.slabs):
                    ours = lows_by[n][0] == "low_dve" and key[0] == "ada"
                    if ours and (key[1], key[3]) == (l, piece * D + hf * W512):
                        w = wsplit[:, n % SPLITS]
                        v.wait_ge(S("high_ready"), n + 1)
                        tt(w[:, 1], ring[:, n % RING], w[:, 0].bitcast(F32), ALU.subtract).then_inc(S("low_dve"), 1)

            def add_mods(l, where):
                groups = [(piece, hf) for piece, _ in where for hf in range(2)]
                mod_low(l, *groups[0])
                for i, (piece, hf) in enumerate(groups):
                    if i + 1 < len(groups):
                        mod_low(l, *groups[i + 1])
                    if i == 0:
                        v.wait_ge(S("small_landed"), SMALLS * (l + 1))
                    add_mod(l, piece, dict(where)[piece], (hf,))

            def add_mod(l, piece, row, halves=(0, 1)):
                for hf in halves:
                    b = job(("mod", l, piece, hf))
                    s = row[:, hf * 512:(hf + 1) * 512]
                    chain(tt(s, b[:], s, ALU.add))
                    fr(("mod", l, piece, hf))

            def low(key, high, n, src, hi_ap, lo_ap, ready):
                v.wait_ge(S(high), n)
                chain(tt(lo_ap, src, hi_ap.bitcast(F32), ALU.subtract))
                fr(key)
                v.sem_inc(S(ready), 1)

            def hT_low(l, which):
                for t in range(NT):
                    for q in range(2):
                        key = ("hT", l, which, t, q)
                        d = hT[:, :, 4 * q:4 * q + 4, t * P:(t + 1) * P]
                        low(key, "hT_high", (2 * l + which) * 4 + 2 * t + q + 1, h4(job(key)[:]), d[:, 0], d[:, 1],
                            "hT_ready")

            v.sem_inc(S("mlow_dve"), low_part(0)[2])
            v.wait_ge(S("cact_ready"), 1)
            tt(cact[:, 1, :], cactf[:], cact[:, 0, :].bitcast(F32), ALU.subtract).then_inc(S("cact_low"), 1)
            v.wait_ge(S("x_landed"), 16)
            for l in range(DEPTH):
                v.wait_ge(S("consts_ready"), 1)
                add_mods(l, ((0, mod[:, 0, :]), (1, mod[:, 1, :])))
                gain()
                normalise(l, 0)
                b = job(("cols", l))
                chain(v.tensor_copy(cols[:], b[:, 0:66]))
                fr(("cols", l))
                v.wait_ge(S("wsm_high"), l + 1)
                tt(wsm2[:, 1], wsm[:], wsm2[:, 0].bitcast(F32), ALU.subtract).then_inc(S("wsm_ready"), 1)
                hT_low(l, 0)
                v.wait_ge(S("masks_ready"), 1)
                b = job(("small", l))
                chain(v.tensor_copy(small_T, b[0:32, 0:SEQ]))
                fr(("small", l))
                v.sem_inc(S("small_T_ready"), 1)
                b = job(("turned", l))
                pv = b[:, 0:64].rearrange("p (t n) -> p t n", n=32)
                chain(tt(sc(RAW), pv[:, :, 16:32], rep(bias16[:], NT), ALU.add))
                fr(("turned", l))
                chain(tt(sc(RAW), sc(RAW), rep(sgn16[:], NT)))
                chain(v.scalar_tensor_tensor(sc(AB_), sc(RAW), -1.0, sc(RAW), ALU.mult, ALU.max))
                v.sem_inc(S("abs_ready"), 1)
                v.wait_ge(S("softplus_ln"), 2 * l + 1)
                chain(v.scalar_tensor_tensor(sc(SP), sc(RAW), 0.0, sc(LG), ALU.max, ALU.add))
                v.wait_ge(S("cf_exp"), l + 1)
                chain(tt(sc(SP), sc(SP), rep(cf16[:], NT)))
                v.sem_inc(S("decay_ready"), 1)
                def conv(i):
                    key = ("qkvA", l, i) if i < 6 else ("qkB", l, i - 6)
                    b = job(key)
                    dst = [fA[:, 2 * i + j, :] if i < 6 else fB[:, 2 * i + j - 12, :] for j in range(2)]
                    src = [b[:, j * SEQ:(j + 1) * SEQ] for j in range(2)]
                    tap = lambda j, q: cols[:, 4 * (2 * i + j) + q:4 * (2 * i + j) + q + 1]
                    apart(*[v.tensor_scalar(dst[j], src[j], tap(j, 3), None, ALU.mult) for j in range(2)])
                    for s in range(1, 4):
                        apart(*[v.scalar_tensor_tensor(dst[j][:, s:SEQ], src[j][:, 0:SEQ - s], tap(j, 3 - s),
                                                       dst[j][:, s:SEQ], ALU.mult, ALU.add) for j in range(2)])
                    v.sem_inc(S("conv_ready"), 2)
                    fr(key)

                conv(0)
                conv(1)
                b = job(("cum", l))
                pv = b[:, 0:128].rearrange("p (t i n) -> p t i n", t=NT, i=4)
                chain(v.tensor_copy(sc(CUM), pv[:, :, 0, :]))
                chain(v.tensor_copy(sc(TOT), pv[:, :, 1, :]))
                chain(v.tensor_copy(tot2[:].rearrange("p (t r) n -> p t r n", r=2), pv[:, :, 2:4, :]))
                fr(("cum", l))
                b = job(("la", l))
                for f in range(2):
                    chain(v.tensor_scalar(uc[:, f, :], b[:, f * SEQ:(f + 1) * SEQ], cols[:, 64 + f:65 + f], -1.0,
                                          ALU.add, ALU.mult))
                fr(("la", l))
                chain(v.scalar_tensor_tensor(tc1, uc, -1.0, uc, ALU.mult, ALU.max))
                v.sem_inc(S("abs_ready"), 1)
                v.wait_ge(S("softplus_ln"), 2 * l + 2)
                chain(v.scalar_tensor_tensor(tc2, uc, 0.0, tc1, ALU.max, ALU.add))
                chain(v.tensor_scalar(tc2, tc2, -1.0 / 16.0, None, ALU.mult))
                for f in range(2):
                    chain(v.tensor_tensor_scan(bc[:, f, :], rst[:], tc2[:, f, :], 0.0, ALU.mult, ALU.add))
                for i in range(2, 8):
                    conv(i)
                for t in range(NT):
                    for i in range(2):
                        v.wait_ge(S("sq_ready"), l * 4 + 2 * t + i + 1)
                        chain(v.tensor_reduce(ssA[:, t, 4 * i:4 * i + 4], h4(sq[i]), X, ALU.add))
                        v.sem_inc(S("sq_used"), 1)
                v.sem_inc(S("ss_ready"), 1)
                v.wait_ge(S("lnss_ready"), l + 1)
                gc, lb = sc(CUM, 0, 4), sc(SP, 4, 4)
                lq, lk = ssA[:, :, 0:4], ssA[:, :, 4:8]
                stt = v.scalar_tensor_tensor
                chain(stt(at(BJ), lk, -0.5, gc, ALU.mult, ALU.subtract))
                chain(stt(at(Z1), lk, -0.5, gc, ALU.mult, ALU.add))
                chain(tt(at(Z1), at(Z1), lb, ALU.add))
                chain(stt(at(Z2), lq, -0.5, gc, ALU.mult, ALU.add))
                chain(v.tensor_scalar(at(Z2), at(Z2), LN_DKA, None, ALU.add))
                chain(tt(at(ZE), at(BJ), sc(TOT, 0, 4), ALU.add))
                chain(tt(at(AJ), sc(RAW, 8, 4), sc(CUM, 12, 4), ALU.subtract))
                v.sem_inc(S("zA_ready"), 1)
                v.sem_inc(S("aj_ready"), 1)
                v.wait_ge(S("fC_ready"), l + 1)
                bcv = bc.rearrange("p f (n i) -> p (f n) i", i=L)
                fc = lambda ap: ap.rearrange("p f (n i) -> p (f n) i", i=L)
                chain(tt(fc(uc), bcv, bcv[:, :, L // 2:L // 2 + 1].broadcast_to([P, 8, L]), ALU.subtract))
                chain(tt(fc(tc1), bcv[:, :, L - 1:L].broadcast_to([P, 8, L]), bcv, ALU.subtract))
                v.sem_inc(S("glaexp_in"), 1)
                v.wait_ge(S("glaexp_ready"), l + 1)
                chain(tt(keT, fC[:, 2:4, :], tc1))
                chain(tt(qg, fC[:, 0:2, :], bc))
                chain(v.tensor_copy(aeC[:], bc.rearrange("p f (n i) -> p f n i", i=L)[:, :, :, L - 1]))
                chain(tt(fC[:, 0:2, :], fC[:, 0:2, :], uc))
                chain(tt(fC[:, 2:4, :], fC[:, 2:4, :], tc2))
                v.sem_inc(S("gla_ready"), 1)
                for t in range(NT):
                    b = job(("KK", l, t))
                    v.wait_ge(S("decayA_ready"), l * 4 + 2 * t + 1)
                    chain(tt(LT[:, t, :], b[:], LT[:, t, :]))
                    fr(("KK", l, t))
                    b = job(("KQ", l, t))
                    v.wait_ge(S("decayA_ready"), l * 4 + 2 * t + 2)
                    chain(tt(AT[:, t, :], b[:], AT[:, t, :]))
                    fr(("KQ", l, t))
                be = tot2[:, :, 12:16]

                def stabilise_1():
                    for t in range(NT):
                        b = job(("RA", l, t))
                        chain(v.tensor_reduce(cmaxB[:, 2 * t:2 * t + 2, :].rearrange("p r h -> p h r"),
                                              b[:].rearrange("p (h r i) -> p h r i", h=H, r=2), X, ALU.max))
                        chain(tt(h4(WB[:, t, :]), h4(b[:]), rep(negL[:], H), ALU.add))
                        fr(("RA", l, t))
                        chain(v.tensor_reduce(at(CM, t), h4(WB[:, t, :]), X, ALU.max))

                def stabilise_2():
                    chain(tt(cmaxB[:], cmaxB[:], be, ALU.add))
                    for n in range(NCH):
                        chain(tt(spB[:, n, :], mB[:, n, :], be[:, n, :], ALU.add))
                        chain(tt(mB[:, n + 1, :], spB[:, n, :], cmaxB[:, n, :], ALU.max))
                    chain(tt(spB[:], spB[:], mB[:, 1:NCH + 1, :], ALU.subtract))

                def stabilise_3():
                    for r in range(2):
                        rw = slice(64 * r, 64 * r + 64)
                        mv = mB[rw, 0:NCH, :].rearrange("p (t r) h -> p t r h", r=2)
                        mw = mB[rw, 1:NCH + 1, :].rearrange("p (t r) h -> p t r h", r=2)
                        chain(v.tensor_copy(scal[rw, MP[0], :, MP[1]:MP[1] + 4], mv[:, :, r, :]))
                        chain(v.tensor_copy(scal[rw, MN[0], :, MN[1]:MN[1] + 4], mw[:, :, r, :]))
                    chain(tt(at(MX), at(MP), at(CM), ALU.max))
                    chain(v.tensor_scalar(at(NZ), at(MX), -1.0, None, ALU.mult))
                    chain(tt(at(T0), at(MP), at(MX), ALU.subtract))
                    chain(stt(at(T1), at(MX), -1.0, sc(CUM, 12, 4), ALU.mult, ALU.subtract))
                    chain(tt(at(MN), sc(TOT, 12, 4), at(MN), ALU.subtract))
                    chain(tt(at(MN), at(MN), at(AJ), ALU.add))
                    chain(v.tensor_scalar(at(BJB), at(AJ), LN_DKB, None, ALU.add))
                    v.sem_inc(S("stabB_ready"), 1)

                for t in range(NT):
                    chain(tt(h4(LB[:, t, :]), h4(LT[:, t, :]), rep(lev_m[:, 0, :], H)))
                    v.sem_inc(S("LB_ready"), 1)
                    chain(tt(h4(DT[:, t, :]), rep(ident[:], H), h4(LB[:, t, :]), ALU.subtract))
                    v.sem_inc(S("DT_ready"), 1)
                for t in range(NT):
                    b = job(("X", l, 0, t))
                    chain(tt(h4(Dm[:, t, :]), rep(ident[:], H), h4(b[:]), ALU.subtract))
                    fr(("X", l, 0, t))
                    v.sem_inc(S("D_ready"), 1)
                    chain(tt(h4(LB[:, t, :]), h4(LT[:, t, :]), rep(lev_m[:, 1, :], H)))
                    v.sem_inc(S("LB_ready"), 1)
                for lev in range(1, 6):
                    for t in range(NT):
                        b = job(("X", l, lev, t))
                        chain(v.tensor_copy(XB[:, t, :], b[:]))
                        fr(("X", l, lev, t))
                        v.sem_inc(S("X_ready"), 1)
                        if lev < 5:
                            chain(tt(h4(LB[:, t, :]), h4(LT[:, t, :]), rep(lev_m[:, lev + 1, :], H)))
                            v.sem_inc(S("LB_ready"), 1)
                    if lev < 5:
                        if lev == 1:
                            v.wait_ge(S("ffn_rows_landed"), 32 * (l + 1))
                        piece, hf = LEVEL_MODS[lev - 1]
                        add_mod(l, piece, mod[:, piece - 3, :], (hf,))
                        if lev < 4:
                            (stabilise_1, stabilise_2, stabilise_3)[lev - 1]()
                    for t in range(NT):
                        if lev < 5:
                            b = job(("Y", l, lev, t))
                            chain(tt(Dm[:, t, :], Dm[:, t, :], b[:], ALU.subtract))
                            fr(("Y", l, lev, t))
                            v.sem_inc(S("D_ready"), 1)
                        b = job(("YT", l, lev, t))
                        chain(tt(DT[:, t, :], DT[:, t, :], b[:], ALU.subtract))
                        fr(("YT", l, lev, t))
                        v.sem_inc(S("DT_ready"), 1)
                v.wait_ge(S("expA_ready"), l + 1)
                v.wait_ge(S("beta_ready"), l + 1)
                for t in range(NT):
                    b = job(("TK2", l, t))
                    apart(tt(h4(kbg[:, t, :]), h4(b[:]), bc3(at(EZ1, t), P)),
                          tt(h4(kend[:, t, :]), h4(b[:]), bc3(at(EZE, t), P)))
                    fr(("TK2", l, t))
                    b = job(("TV", l, t))
                    chain(tt(h4(vb[:, t, :]), h4(b[:]), bc3(at(BETA, t), P)))
                    fr(("TV", l, t))
                    v.sem_inc(S("kbg_ready"), 1)
                for t in range(NT):
                    b = job(("U", l, t))
                    chain(v.tensor_copy(UU[:, t, :], b[:]))
                    fr(("U", l, t))
                v.wait_ge(S("expB_ready"), l + 1)
                for i in range(2):
                    rw = slice(64 * i, 64 * i + 64)
                    chain(v.tensor_copy(spc[rw], spB[rw].rearrange("p n (a b) -> p n a b", b=2)[:, :, :, i]))
                chain(v.memset(vB[:, :, :, 128:129], 1.0))
                chain(v.memset(AC[:], 0.0))
                for t in range(NT):
                    b = job(("TKB", l, t))
                    chain(tt(h4(kw[:, t, :], 64), h4(b[:, 0:256], 64), bc3(at(KWS, t), 64)))
                    fr(("TKB", l, t))
                    b = job(("KQB", l, t))
                    v.wait_ge(S("decayB_ready"), l * NT + t + 1)
                    chain(tt(WB[:, t, :], b[:], WB[:, t, :]))
                    fr(("KQB", l, t))
                    b = job(("KQC", l, t))
                    chain(v.copy_predicated(h4(AC[:, t, :]), rep(tri[:].bitcast(U32), H), h4(b[:])))
                    fr(("KQC", l, t))
                    b = job(("TKC", l, t))
                    chain(v.tensor_copy(keC[:, t, :], b[:, 0:256]))
                    fr(("TKC", l, t))
                chain(v.memset(SA[:], 0.0))
                chain(v.memset(SB[:], 0.0))
                chain(v.memset(SC[:], 0.0))
                v.wait_ge(S("wT_ready"), (l + 1) * NT)
                v.wait_ge(S("tok_ready"), (l + 1) * 2 * NT)
                v.sem_inc(S("scan_ready"), 1)
                for name in ("SA_ready", "SB_ready", "SC_ready"):
                    v.sem_inc(S(name), 1)
                for n in range(NCH):
                    t, r = n // 2, n % 2
                    rw = slice(64 * r, 64 * r + 64)
                    b = job(("P1", l, n))
                    chain(tt(UU[rw, t, :], UU[rw, t, :], b[rw, :], ALU.subtract))
                    fr(("P1", l, n))
                    v.sem_inc(S("delta_ready"), 1)
                    b = job(("P2", l, n))
                    chain(tt(h4(oA[rw, t, :]), h4(b[rw, :]), bc3(scal[rw, EZ2[0], t, EZ2[1]:EZ2[1] + 4], P)))
                    fr(("P2", l, n))
                    for p in range(2):
                        b = job((f"QB{p}", l, n))
                        bv = b[rw, 0:258].rearrange("p (a d) -> p a d", d=129)
                        sv = scal[rw, SI[0], t, SI[1] + p:SI[1] + 4:2]
                        apart(tt(h4(nB[rw, t, :])[:, p:4:2, :], bv[:, :, 0:128], bc3(sv, P)),
                              tt(dB[rw, t, p:4:2], bv[:, :, 128], sv))
                        fr((f"QB{p}", l, n))
                    b = job(("KVB", l, n))
                    apart(*[stt(SB[:, p, :], SB[:, p, :], spc[:, n, p:p + 1], b[:, p * 129:(p + 1) * 129],
                                ALU.mult, ALU.add) for p in range(2)])
                    fr(("KVB", l, n))
                    if n < NCH - 1:
                        v.sem_inc(S("SB_ready"), 1)
                    b = job(("P3", l, n))
                    heads_at = [slice(hh * P, (hh + 1) * P) for hh in range(H)]
                    apart(*[stt(SA[:, hs], SA[:, hs], geA[:, n, hh:hh + 1], b[:, hs], ALU.mult, ALU.add)
                            for hh, hs in enumerate(heads_at)])
                    fr(("P3", l, n))
                    if n < NCH - 1:
                        v.sem_inc(S("SA_ready"), 1)
                    b = job(("QC", l, n))
                    chain(v.tensor_copy(oC[rw, t, :], b[rw, :]))
                    fr(("QC", l, n))
                    b = job(("KVC", l, n))
                    apart(*[stt(SC[:, p, :], SC[:, p, :], aeC[:, p, n:n + 1], b[:, p * P:(p + 1) * P],
                                ALU.mult, ALU.add) for p in range(2)])
                    fr(("KVC", l, n))
                    if n < NCH - 1:
                        v.sem_inc(S("SC_ready"), 1)
                for t in range(NT):
                    b = job(("OA", l, t))
                    chain(tt(oA[:, t, :], oA[:, t, :], b[:], ALU.add))
                    fr(("OA", l, t))
                    if t == NT - 1:
                        v.sem_inc(S("o_ready"), 1)
                    for p in range(2):
                        b = job((f"OB{p}", l, t))
                        bv = b[:, 0:258].rearrange("p (a d) -> p a d", d=129)
                        nv = h4(nB[:, t, :])[:, p:4:2, :]
                        dv = dB[:, t, p:4:2]
                        apart(tt(nv, nv, bv[:, :, 0:128], ALU.add), tt(dv, dv, bv[:, :, 128], ALU.add))
                        fr((f"OB{p}", l, t))
                    b = job(("OC", l, t))
                    chain(tt(oC[:, t, :], oC[:, t, :], b[:], ALU.add))
                    fr(("OC", l, t))
                v.sem_inc(S("o_ready"), 1)
                chain(stt(at(T0), dB[:], -1.0, dB[:], ALU.mult, ALU.max))
                chain(tt(at(T0), at(T0), at(THR), ALU.max))
                chain(v.reciprocal(at(T0), at(T0)))
                for t in range(NT):
                    chain(tt(h4(nB[:, t, :]), h4(nB[:, t, :]), bc3(at(T0, t), P)))
                v.sem_inc(S("o_ready"), 1)
                heads = lambda b: b.rearrange("p t (h d) -> p (t h) d", d=P)
                for i, g in enumerate((0, 2, 1)):
                    v.wait_ge(S("osq_ready"), l * 3 + i + 1)
                    chain(v.tensor_reduce(oss[:, 8 * g:8 * g + 8], h4(osq[g]), X, ALU.add))
                v.sem_inc(S("oss_ready"), 1)
                v.wait_ge(S("gate_ready"), l * 3 * NT + NT)
                chain(tt(heads(oBg), heads(oBg), rep(normr[:, 1, :], NT * H)))
                v.wait_ge(S("orstd_ready"), l + 1)
                for g, o in enumerate((oA, nB, oC)):
                    chain(tt(heads(o), heads(o), bc3(oss[:, 8 * g:8 * g + 8], P)))
                for g, (o, z) in enumerate(((oA, zA), (nB, oBg), (oC, zC))):
                    if g != 1:
                        v.wait_ge(S("gate_ready"), l * 3 * NT + (2 if g == 0 else 3) * NT)
                        chain(tt(heads(z), heads(z), rep(normr[:, g, :], NT * H)))
                    for t in range(NT):
                        chain(tt(o[:, t, :], o[:, t, :], z[:, t, :]))
                        v.sem_inc(S("y_branch"), 1)
                v.wait_ge(S("gate_rows_landed"), 32 * (l + 1))
                add_mods(l, ((2, gates[2]), (5, gates[5])))

                def y_low(g):
                    for t in range(NT):
                        key = ("yT", l, g, t)
                        d = yT[g][:, :, :, t * P:(t + 1) * P]
                        low(key, "yT_high", l * 6 + 2 * g + t + 1, h4(job(key)[:]), d[:, 0], d[:, 1], "yT_ready")

                y_low(0)
                y_low(1)
                m = 0
                for g in range(3):
                    for hf in range(2):
                        for t in range(NT):
                            v.wait_ge(S("mgate_ready"), l * 12 + m + 1)
                            b = job(("br", l, g, hf, t))
                            dst = merged[:, t, hf * 512:(hf + 1) * 512]
                            if g == 0:
                                chain(tt(dst, b[:], mg_s[m % 2]))
                            else:
                                chain(tt(mg_s[m % 2], b[:], mg_s[m % 2]))
                                chain(tt(dst, dst, mg_s[m % 2], ALU.add))
                            fr(("br", l, g, hf, t))
                            v.sem_inc(S("merged_ready"), 1)
                            m += 1
                    if g == 0:
                        y_low(2)
                for t in range(NT):
                    for q in range(2):
                        key = ("mT", l, t, q)
                        d = mT[:, :, 4 * q:4 * q + 4, t * P:(t + 1) * P]
                        low(key, "mT_high", l * 4 + 2 * t + q + 1, h4(job(key)[:]), d[:, 0], d[:, 1], "mT_ready")

                def residual(bank_ap, gate, t, hf, tmp):
                    cs = slice(hf * 512, (hf + 1) * 512)
                    chain(tt(tmp, bank_ap, gates[gate][:, cs]))
                    chain(tt(xs[:, t, cs], xs[:, t, cs], tmp, ALU.add))

                v.wait_ge(S("gffn_landed"), 16 * (l + 1))
                gain()
                for hf in range(2):
                    for t in range(NT):
                        b = job(("wo", l, hf, t))
                        residual(b[:], 2, t, hf, Dm[:, 0, :])
                        fr(("wo", l, hf, t))
                        v.sem_inc(S("x_half"), 1)
                normalise(l, 1)
                hT_low(l, 1)
                if l == 0:
                    widths = ffn_widths(D_FF)
                    def g_low(f):
                        for t in range(NT):
                            key = ("ffn", l, "gT", f, t)
                            kt = widths[f] // P
                            low(key, "gT_high", f * NT + t + 1,
                                job(key)[:, 0:widths[f]].rearrange("p (a b) -> p a b", b=P), fgT[t][:, 0, 0:kt, :],
                                fgT[t][:, 1, 0:kt, :], "gT_ready")

                    for f, wd in enumerate(widths):
                        if f > 0:
                            g_low(f - 1)
                        for t in range(NT):
                            key = ("ffn", l, "w3", f, t)
                            b = job(key)
                            v.wait_ge(S("silu_ready"), f * NT + t + 1)
                            if f > 0:
                                v.wait_ge(S("gT_ready"), (f - 1) * NT + t + 1)
                            chain(tt(fg[t][:, 0:wd], fs[t][:, 0:wd], b[:, 0:wd]))
                            fr(key)
                            v.sem_inc(S("g_ready"), 1)
                    g_low(len(widths) - 1)
                    v.wait_ge(S("down_done"), 2 * len(widths))
                    for t in range(NT):
                        for hf in range(2):
                            residual(facc_ps[2 * t + hf][:], 5, t, hf, Dm[:, 0, :])
                            v.sem_inc(S(f"bank_free{NBANK + 2 * t + hf}"), 1)
                        v.sem_inc(S("x_ready"), 1)
                else:
                    b = job(("logitsT", l))
                    chain(v.tensor_copy(logits_T, b[0:8, 0:SEQ]))
                    fr(("logitsT", l))
                    v.sem_inc(S("logits_T_ready"), 1)
                    b = job(("router", l))
                    lg = route[:, 0:16].rearrange("p (t n) -> p t n", n=8)
                    lg2 = route[:, 0:16]
                    chain(tt(lg, b[:, 0:16].rearrange("p (t n) -> p t n", n=8), rep(brt[:], NT), ALU.add))
                    fr(("router", l))
                    four = lambda ap: ap.rearrange("p (t a b) -> p t a b", t=NT, b=8)
                    cmp, eq = four(route[:, 64:192]), four(route[:, 192:320])
                    mine = lg2.rearrange("p (t a o) -> p t a o", t=NT, o=1).broadcast_to([P, NT, 8, 8])
                    other = lg2.rearrange("p (t o a) -> p t o a", t=NT, o=1).broadcast_to([P, NT, 8, 8])
                    chain(tt(cmp, other, mine, ALU.is_gt))
                    chain(tt(eq, other, mine, ALU.is_equal))
                    chain(tt(eq, eq, lower[:].rearrange("p (o a) b -> p o a b", o=1).broadcast_to([P, NT, 8, 8])))
                    chain(tt(cmp, cmp, eq, ALU.add))
                    sl, cb = sel[:, :, 0:8], comb[:, :, 0:8]
                    chain(v.tensor_reduce(sl, cmp, X, ALU.add))
                    chain(v.tensor_scalar(sl, sl, 2.0, None, ALU.is_lt))
                    v.sem_inc(S("sel_ready"), 1)
                    top = st[:, 32:34]
                    chain(v.tensor_reduce(top, lg, X, ALU.max))
                    chain(tt(cb, lg, bc3(top, 8), ALU.subtract))
                    v.sem_inc(S("route_in"), 1)
                    v.wait_ge(S("route_exp"), 1)
                    chain(tt(cb, cb, sl))
                    chain(v.tensor_reduce(top, cb, X, ALU.add))
                    chain(v.reciprocal(top, top))
                    chain(tt(cb, cb, bc3(top, 8)))
                    b = job(("rank", l))
                    chain(v.tensor_copy(rank[:, :, 0:8], b[:, 0:16].rearrange("p (t n) -> p t n", n=8)))
                    chain(v.tensor_reduce(top[:, 0:1], b[:, 16:24], X, ALU.max))
                    fr(("rank", l))
                    chain(v.tensor_scalar(over[:], top[:, 0:1], float(CAP), None, ALU.is_gt))
            v.wait_ge(S("slots_ready"), BLOCKS + 1)

            def expert_block(blk):
                jb = MOE_BASE + blk * JBLOCK + FIRST
                fb = blk * N_EXP * NF

                def add_scattered(e, i0):
                    for t in range(NT):
                        for hf in range(2):
                            i = i0 + 2 * t + hf
                            v.wait_ge(S("mm_done"), e * JPER + (jb + i + 1))
                            dst = facc[:, t, hf * W512:(hf + 1) * W512]
                            v.tensor_tensor(dst, dst, banks[i % NBANK][:], ALU.add).then_inc(S("facc_done"), 1)
                            v.wait_ge(S("facc_done"), e * (2 * NT) + (blk * 2 * NT * (N_EXP + 1) + 2 * t + hf + 1))
                            v.sem_inc(S(f"bank_free{i % NBANK}"), 1)

                def make_picks(e):
                    for t in range(NT):
                        v.tensor_scalar(pick[:, t, :], slot_no[blk], rank[:, t, e], sel[:, t, e],
                                        ALU.is_equal, ALU.mult)
                        ins = v.tensor_scalar(pickw[:, t, :], slot_no[blk], rank[:, t, e], comb[:, t, e],
                                              ALU.is_equal, ALU.mult)
                    ins.then_inc(S("pick_ready"), 1)

                def xg_low(src, d, n, i):
                    v.wait_ge(S("xg_high"), n)
                    v.tensor_tensor(d[:, 1], src, d[:, 0].bitcast(F32), ALU.subtract).then_inc(S("xgT_ready"), 1)
                    v.wait_ge(S("xgT_ready"), n)
                    v.sem_inc(S(f"bank_free{i % NBANK}"), 1)

                make_picks(bass.ds(0, 1))
                if blk == 0:
                    chain(v.memset(pwT, 0.0))
                    for b in (NBANK, NBANK + 1):
                        v.wait_ge(S(f"bank_free{b}"), bank_uses[b])
                else:
                    v.wait_ge(S("ey_ready"), N_EXP + 1)
                for q in range(2):
                    v.memset(facc_ps[q][:], 0.0).then_inc(S("y_zero"), 1)
                v.wait_ge(S("y_zero"), 2 * blk + 2)
                v.sem_inc(S("pwT_ready"), 1)
                if blk == 0:
                    v.sem_inc(S("route_ready"), 1)
                for q in range(FIRST):
                    xg_low(h4(banks[q][:, 0:2 * P]), xgT[:, :, 2 * q:2 * q + 2, :],
                           blk * (N_EXP * 2 + FIRST) + q + 1, q)
                with v.Fori(0, N_EXP) as e:
                    cur = [0]

                    def mlow(upto):
                        while cur[0] <= min(upto, SPER - 1):
                            i = cur[0]
                            cur[0] += 1
                            if low_part(i)[0] != "mlow_dve":
                                continue
                            w = wsplit[:, (len(plan.slabs) + i) % SPLITS]
                            v.wait_ge(S("mhigh_ready"), e * SPER + (blk * N_EXP * SPER + i + 1))
                            v.tensor_tensor(w[:, 1], mslot(i % MRING), w[:, 0].bitcast(F32), ALU.subtract) \
                                .then_inc(S("mlow_dve"), 1)

                    def g_low(f):
                        i = MJOB[("gT", f)]
                        d = fgT[f % 2]
                        v.wait_ge(S("egT_high"), e * NF + (fb + f + 1))
                        v.tensor_tensor(d[:, 1], h4(banks[i % NBANK][:]), d[:, 0].bitcast(F32), ALU.subtract) \
                            .then_inc(S("egT_ready"), 1)
                        v.wait_ge(S("egT_ready"), e * NF + (fb + f + 3))
                        v.sem_inc(S(f"bank_free{i % NBANK}"), 1)

                    for f in range(NF):
                        mlow(moe_slab("w1", f) + 3)
                        if f == 0:
                            add_scattered(e, MJOB[("sc", 0, 0)])
                        else:
                            g_low(f - 1)
                        mlow(moe_slab("w1", f) + 5)
                        i = MJOB[("w3", f)]
                        v.wait_ge(S("mm_done"), e * JPER + (jb + i + 1))
                        v.wait_ge(S("esilu_ready"), e * NF + (fb + f + 1))
                        v.wait_ge(S("egT_ready"), e * NF + (fb + f + 1))
                        v.tensor_tensor(fg[f % 2], fs[f % 2], banks[i % NBANK][:], ALU.mult) \
                            .then_inc(S("eg_ready"), 1)
                        v.wait_ge(S("eg_ready"), e * NF + (fb + f + 3))
                        v.sem_inc(S(f"bank_free{i % NBANK}"), 1)
                        if f == 2:
                            make_picks(bass.ds(e + 1, 1))
                        if f == NF - 1:
                            for q in range(2):
                                v.wait_ge(S("mm_done"), e * JPER + (jb + MJOB[("xg", q)] + 1))
                                xg_low(h4(banks[MJOB[("xg", q)] % NBANK][:]), xgT[:, :, 4 * q:4 * q + 4, :],
                                       e * 2 + (blk * (N_EXP * 2 + FIRST) + FIRST + q + 1), MJOB[("xg", q)])
                        mlow(moe_slab("w1", f) + (5 if f else 3) + 2)
                    g_low(NF - 1)
                    mlow(SPER - 1)
                add_scattered(N_EXP, 0)

            v.sem_inc(S("eg_ready"), 2)
            v.sem_inc(S("egT_ready"), 2)
            expert_block(0)
            with v.If(v.value_load(over[0:1, 0:1], min_val=0, max_val=1) > 0):
                expert_block(1)
            for t in range(NT):
                chain(tt(facc[:, t, :], facc[:, t, :], gates[5]))
                chain(tt(xs[:, t, :], xs[:, t, :], facc[:, t, :], ALU.add))
                v.sem_inc(S("x_ready"), 1)
            v.wait_ge(S("gfinal_landed"), 16)
            for t in range(NT):
                v.wait_ge(S("rstd_ready"), 2 * DEPTH + 1)
                chain(stt(xs[:, t, :], xs[:, t, :], st[:, 4 * t + 3:4 * t + 4], mod[:, 0, :], ALU.mult, ALU.mult))
                v.sem_inc(S("y_ready"), 1)


_INS = ["x", "c", "w_ada", "b_ada", "g_mix", "g_ffn", "g_final", "w_in", "conv_a", "a_log", "dt_bias", "norm_a",
        "conv_b", "b_i", "b_f", "norm_b", "w_gla2", "b_gla", "norm_c", "w_br", "w_mg", "b_mg", "w_o",
        "w1_d", "w3_d", "w2_d", "w_router", "b_router", "w1_e", "w3_e", "w2_e"]


def kernel(**inputs):
    import numpy as _np
    import concourse.bacc as _bacc
    from concourse import mybir as _mybir
    from concourse.bass_utils import run_bass_kernel_spmd as _run

    nc = _bacc.Bacc("TRN2", target_bir_lowering=False, num_devices=1)
    arrays, args = {}, []
    for name in _INS:
        a = _np.ascontiguousarray(inputs[name])
        arrays[f"in_{name}_dram"] = a
        args.append(nc.dram_tensor(f"in_{name}_dram", a.shape, _mybir.dt.from_np(a.dtype), kind="ExternalInput").ap())
    args.append(nc.dram_tensor("out_0_dram", (1, SEQ, D), F32, kind="ExternalOutput").ap())
    hybrid_kernel(nc, *args)
    r = _run(nc, [arrays], core_ids=[0])
    return r.results[0]["out_0_dram"]
```
